# Optimizing a Trainium2 kernel written in Bass

```python
import math
import jax
import jax.numpy as jnp
from jax import lax
import numpy as np
import jax, jax.numpy as jnp

D_MODEL = 1024
BATCH = 1
SEQ = 256
DEPTH = 1

N_MEM = 256
D_FF = 2816
NORM_EPS = 1e-6
NEG_INF = -1e30
FORCE_SCORE = 1e4

NSA_HEADS = 8
NSA_GROUPS = 2
NSA_HPG = NSA_HEADS // NSA_GROUPS
NSA_HEAD_DIM = 64
CMP_BLOCK = 32
CMP_STRIDE = 16
CMP_HIDDEN = 256
SEL_BLOCK = 64
SEL_TOPK = 16
WINDOW = 512
WIN_QBLOCK = 128
SEL_QCHUNK = 16

REL_BUCKETS = 32
REL_MAX_DIST = 128

DN_HEADS = 4
DN_HEAD_DIM = 128
DN_CONV = 4
DN_CHUNK = 64

X_HEADS = 4
X_HEAD_DIM = 128

N_BRANCH = 3
NSA_Q = NSA_HEADS * NSA_HEAD_DIM
NSA_KV = NSA_GROUPS * NSA_HEAD_DIM
DN_W = DN_HEADS * DN_HEAD_DIM
X_W = X_HEADS * X_HEAD_DIM
IN_SPLITS = (NSA_Q, 6 * NSA_KV, 3 * NSA_HEADS, 3 * DN_W, DN_HEADS, DN_HEADS, DN_W, X_W)
IN_WIDTH = NSA_Q + 6 * NSA_KV + 3 * NSA_HEADS + 3 * DN_W + 2 * DN_HEADS + DN_W + X_W


def rms_norm(x, gain):
    xf = x.astype(jnp.float32)
    y = xf * lax.rsqrt(jnp.mean(xf * xf, axis=-1, keepdims=True) + NORM_EPS)
    return (y * gain.astype(jnp.float32)).astype(x.dtype)

def l2_norm(x):
    xf = x.astype(jnp.float32)
    return xf * lax.rsqrt(jnp.sum(xf * xf, axis=-1, keepdims=True) + NORM_EPS)

def swiglu(x, w_gate, w_up, w_down):
    return (jax.nn.silu(x @ w_gate) * (x @ w_up)) @ w_down

def split_cols(a, sizes):
    out, start = [], 0
    for n in sizes:
        out.append(a[..., start:start + n])
        start += n
    return out

def rel_bucket(dist):
    exact = REL_BUCKETS // 2
    d = jnp.maximum(dist, 1).astype(jnp.float32)
    log_bucket = exact + (jnp.log(d / exact) / math.log(REL_MAX_DIST / exact)
                          * (REL_BUCKETS - exact)).astype(jnp.int32)
    return jnp.where(dist < exact, dist, jnp.minimum(log_bucket, REL_BUCKETS - 1))

def masked_softmax(logits, mask):
    return jax.nn.softmax(jnp.where(mask, logits.astype(jnp.float32), NEG_INF), axis=-1)

def compress_blocks(kv, pos_emb, w1, w2):
    b, s, g, dh = kv.shape
    r = CMP_BLOCK // CMP_STRIDE
    n_chunk = s // CMP_STRIDE
    n_cmp = n_chunk - r + 1
    ch = kv.reshape(b, n_chunk, CMP_STRIDE, g, dh)
    blocks = jnp.concatenate([ch[:, j:j + n_cmp] for j in range(r)], axis=2)
    blocks = blocks + pos_emb[:, None, :]
    flat = blocks.transpose(0, 1, 3, 2, 4).reshape(b, n_cmp, g, CMP_BLOCK * dh)
    return jax.nn.silu(flat @ w1) @ w2

def nsa_compressed(q, k_c, v_c, rel_bias):
    seq, n_cmp = q.shape[1], k_c.shape[1]
    t = jnp.arange(seq)
    block_end = jnp.arange(n_cmp) * CMP_STRIDE + CMP_BLOCK - 1
    dist = t[:, None] - block_end[None, :]
    bias = rel_bias[rel_bucket(jnp.maximum(dist, 0))]
    bias = bias.reshape(seq, n_cmp, NSA_GROUPS, NSA_HPG).transpose(2, 3, 0, 1)
    logits = jnp.einsum('bsgjd,bcgd->bgjsc', q, k_c) * NSA_HEAD_DIM ** -0.5 + bias
    has_block = (t >= CMP_BLOCK - 1).astype(jnp.float32)[:, None]
    p = masked_softmax(logits, dist >= 0) * has_block
    out = jnp.einsum('bgjsc,bcgd->bsgjd', p.astype(v_c.dtype), v_c)
    return out, p

def select_blocks(p_cmp, seq):
    n_cmp = p_cmp.shape[-1]
    n_blk = seq // SEL_BLOCK
    n_sel = min(SEL_TOPK, n_blk)
    c0 = jnp.arange(n_cmp) * CMP_STRIDE
    s0 = jnp.arange(n_blk) * SEL_BLOCK
    overlap = jnp.maximum(jnp.minimum(c0[:, None] + CMP_BLOCK, s0[None, :] + SEL_BLOCK)
                          - jnp.maximum(c0[:, None], s0[None, :]), 0)
    to_sel = overlap.astype(jnp.float32) / CMP_BLOCK
    importance = jnp.einsum('bgjsc,cn->bgsn', p_cmp, to_sel)
    cur = jnp.arange(seq) // SEL_BLOCK
    blk = jnp.arange(n_blk)
    forced = (blk[None] == 0) | (blk[None] == cur[:, None]) | (blk[None] == cur[:, None] - 1)
    causal = blk[None] <= cur[:, None]
    score = jnp.where(forced, FORCE_SCORE, jnp.where(causal, importance, -FORCE_SCORE))
    vals, idx = lax.top_k(score, n_sel)
    return idx, vals > -1.0

def nsa_selected(q, k_s, v_s, idx, ok, rel_bias):
    b, s, g, j, dh = q.shape
    n_blk = s // SEL_BLOCK
    n_sel = idx.shape[-1]
    kb = k_s.reshape(b, n_blk, SEL_BLOCK, g, dh).transpose(0, 3, 1, 2, 4)
    vb = v_s.reshape(b, n_blk, SEL_BLOCK, g, dh).transpose(0, 3, 1, 2, 4)
    table_g = rel_bias.reshape(REL_BUCKETS, NSA_GROUPS, NSA_HPG)
    offs = jnp.arange(SEL_BLOCK)

    def one(qg, kg, vg, ix, okg, t, tab):
        ks = kg[ix]
        vs = vg[ix]
        dist = t[:, None, None] - (ix[..., None] * SEL_BLOCK + offs)
        mask = okg[..., None] & (dist >= 0)
        bias = tab[rel_bucket(jnp.maximum(dist, 0))].transpose(0, 3, 1, 2)
        logits = jnp.einsum('qjd,qknd->qjkn', qg, ks) * NSA_HEAD_DIM ** -0.5 + bias
        nq = logits.shape[0]
        p = masked_softmax(logits.reshape(nq, j, n_sel * SEL_BLOCK),
                           mask.reshape(nq, 1, n_sel * SEL_BLOCK)).reshape(nq, j, n_sel, SEL_BLOCK)
        return jnp.einsum('qjkn,qknd->qjd', p.astype(vs.dtype), vs)

    per_g = jax.vmap(one, in_axes=(1, 0, 0, 0, 0, None, 1), out_axes=1)
    per_bg = jax.vmap(per_g, in_axes=(0, 0, 0, 0, 0, None, None), out_axes=0)
    n_chunk = s // SEL_QCHUNK
    qs = q.reshape(b, n_chunk, SEL_QCHUNK, g, j, dh).transpose(1, 0, 2, 3, 4, 5)
    ixs = idx.reshape(b, g, n_chunk, SEL_QCHUNK, n_sel).transpose(2, 0, 1, 3, 4)
    oks = ok.reshape(b, g, n_chunk, SEL_QCHUNK, n_sel).transpose(2, 0, 1, 3, 4)
    ts = jnp.arange(s).reshape(n_chunk, SEL_QCHUNK)

    def chunk(args):
        qc, ixc, okc, tc = args
        return per_bg(qc, kb, vb, ixc, okc, tc, table_g)

    out = lax.map(chunk, (qs, ixs, oks, ts))
    return out.transpose(1, 0, 2, 3, 4, 5).reshape(b, s, g, j, dh)

def nsa_window(q, k_w, v_w, rel_bias):
    b, s, g, j, dh = q.shape
    n_qb = s // WIN_QBLOCK
    span = WINDOW + WIN_QBLOCK
    pad = ((0, 0), (WINDOW, 0), (0, 0), (0, 0))
    kp = jnp.pad(k_w, pad)
    vp = jnp.pad(v_w, pad)
    qi = jnp.arange(WIN_QBLOCK)
    kj = jnp.arange(span)
    rel = qi[:, None] + WINDOW - kj[None, :]
    bias = rel_bias[rel_bucket(jnp.maximum(rel, 0))]
    bias = bias.reshape(WIN_QBLOCK, span, g, j).transpose(2, 3, 0, 1)
    band = (rel >= 0) & (rel < WINDOW)

    def block(i):
        start = i * WIN_QBLOCK
        qb = lax.dynamic_slice_in_dim(q, start, WIN_QBLOCK, axis=1)
        kb = lax.dynamic_slice_in_dim(kp, start, span, axis=1)
        vb = lax.dynamic_slice_in_dim(vp, start, span, axis=1)
        mask = band & ((start - WINDOW + kj) >= 0)[None, :]
        logits = jnp.einsum('bqgjd,bkgd->bgjqk', qb, kb) * NSA_HEAD_DIM ** -0.5 + bias
        p = masked_softmax(logits, mask)
        return jnp.einsum('bgjqk,bkgd->bqgjd', p.astype(vb.dtype), vb)

    out = lax.map(block, jnp.arange(n_qb))
    return out.transpose(1, 0, 2, 3, 4, 5).reshape(b, s, g, j, dh)

def causal_depthwise_conv(x, w):
    return lax.conv_general_dilated(
        x, w[:, None, :].astype(x.dtype), window_strides=(1,), padding=[(w.shape[0] - 1, 0)],
        dimension_numbers=('NWC', 'WIO', 'NWC'), feature_group_count=x.shape[-1])

def gated_delta_rule(q, k, v, log_decay, beta):
    f32 = jnp.float32
    b, s, h, dk = q.shape
    dv = v.shape[-1]
    c = DN_CHUNK
    n = s // c

    def chunks(a):
        a = a.astype(f32).reshape((b, n, c, h) + a.shape[3:])
        return jnp.moveaxis(a, 3, 1)

    qc = chunks(q) * dk ** -0.5
    kc, vc = chunks(k), chunks(v)
    gc = jnp.cumsum(chunks(log_decay), axis=-1)
    bc = chunks(beta)
    causal = jnp.tril(jnp.ones((c, c), bool))
    strict = jnp.tril(jnp.ones((c, c), bool), -1)
    decay = jnp.exp(jnp.where(causal, gc[..., :, None] - gc[..., None, :], -jnp.inf))
    kk = jnp.einsum('bhnid,bhnjd->bhnij', kc, kc)
    a_mat = jnp.where(strict, bc[..., :, None] * kk * decay, 0.0) + jnp.eye(c, dtype=f32)
    rhs = jnp.concatenate([vc * bc[..., None], kc * (bc * jnp.exp(gc))[..., None]], axis=-1)
    sol = lax.linalg.triangular_solve(a_mat, rhs, left_side=True, lower=True, unit_diagonal=True)
    u, w = sol[..., :dv], sol[..., dv:]
    qk = jnp.einsum('bhnid,bhnjd->bhnij', qc, kc) * decay
    q_dec = qc * jnp.exp(gc)[..., None]
    k_dec = kc * jnp.exp(gc[..., -1:] - gc)[..., None]
    g_last = jnp.exp(gc[..., -1])

    def step(state, inp):
        qk_n, qd_n, kd_n, u_n, w_n, gl_n = inp
        v_new = u_n - jnp.einsum('bhck,bhkv->bhcv', w_n, state)
        o = jnp.einsum('bhck,bhkv->bhcv', qd_n, state) + jnp.einsum('bhcm,bhmv->bhcv', qk_n, v_new)
        state = state * gl_n[..., None, None] + jnp.einsum('bhck,bhcv->bhkv', kd_n, v_new)
        return state, o

    xs = tuple(jnp.moveaxis(a, 2, 0) for a in (qk, q_dec, k_dec, u, w, g_last))
    _, o = lax.scan(step, jnp.zeros((b, h, dk, dv), f32), xs)
    return o.transpose(1, 0, 3, 2, 4).reshape(b, s, h, dv)

def memory_cross_attention(q, mem_n, w_mem_kv):
    b, m, _ = mem_n.shape
    kv = (mem_n @ w_mem_kv).reshape(b, m, 2, X_HEADS, X_HEAD_DIM)
    k, v = kv[:, :, 0], kv[:, :, 1]
    logits = jnp.einsum('bshd,bmhd->bhsm', q, k) * X_HEAD_DIM ** -0.5
    p = jax.nn.softmax(logits.astype(jnp.float32), axis=-1).astype(v.dtype)
    return jnp.einsum('bhsm,bmhd->bshd', p, v)

def first_inputs(seed: int = 0) -> dict:
    key = jax.random.key(seed)
    keys = iter(jax.random.split(key, 48))
    f32 = jnp.float32
    L, D = DEPTH, D_MODEL

    def normal(shape, scale):
        return jax.random.normal(next(keys), shape, f32) * scale

    def gain(width):
        return 1.0 + 0.02 * jax.random.normal(next(keys), (L, width), f32)

    dt = jnp.exp(jax.random.uniform(next(keys), (L, DN_HEADS), f32, math.log(1e-3), math.log(1e-1)))
    a_log = jnp.log(jax.random.uniform(next(keys), (L, DN_HEADS), f32, 1.0, 16.0))
    return {
        "x": normal((BATCH, SEQ, D), 1.0),
        "mem": normal((BATCH, N_MEM, D), 1.0),
        "ffn1_pre_norm": gain(D),
        "ffn1_w_gate": normal((L, D, D_FF), D ** -0.5),
        "ffn1_w_up": normal((L, D, D_FF), D ** -0.5),
        "ffn1_w_down": normal((L, D_FF, D), D_FF ** -0.5),
        "ffn1_post_norm": gain(D),
        "mix_pre_norm": gain(D),
        "w_in": normal((L, D, IN_WIDTH), D ** -0.5),
        "cmp_pos_k": normal((L, CMP_BLOCK, NSA_HEAD_DIM), 0.1),
        "cmp_pos_v": normal((L, CMP_BLOCK, NSA_HEAD_DIM), 0.1),
        "cmp_k_w1": normal((L, CMP_BLOCK * NSA_HEAD_DIM, CMP_HIDDEN), (CMP_BLOCK * NSA_HEAD_DIM) ** -0.5),
        "cmp_k_w2": normal((L, CMP_HIDDEN, NSA_HEAD_DIM), CMP_HIDDEN ** -0.5),
        "cmp_v_w1": normal((L, CMP_BLOCK * NSA_HEAD_DIM, CMP_HIDDEN), (CMP_BLOCK * NSA_HEAD_DIM) ** -0.5),
        "cmp_v_w2": normal((L, CMP_HIDDEN, NSA_HEAD_DIM), CMP_HIDDEN ** -0.5),
        "rel_bias": normal((REL_BUCKETS, NSA_HEADS), 0.5),
        "dn_conv_w": normal((L, DN_CONV, 3 * DN_W), DN_CONV ** -0.5),
        "dn_a_log": a_log,
        "dn_dt_bias": dt + jnp.log(-jnp.expm1(-dt)),
        "dn_out_norm": gain(DN_HEAD_DIM),
        "mem_norm": gain(D),
        "w_mem_kv": normal((L, D, 2 * X_W), D ** -0.5),
        "w_branch_nsa": normal((L, NSA_Q, D), NSA_Q ** -0.5),
        "w_branch_dn": normal((L, DN_W, D), DN_W ** -0.5),
        "w_branch_mem": normal((L, X_W, D), X_W ** -0.5),
        "w_branch_gate": normal((L, D, N_BRANCH * D), D ** -0.5),
        "w_out": normal((L, D, D), D ** -0.5),
        "mix_post_norm": gain(D),
        "ffn2_pre_norm": gain(D),
        "ffn2_w_gate": normal((L, D, D_FF), D ** -0.5),
        "ffn2_w_up": normal((L, D, D_FF), D ** -0.5),
        "ffn2_w_down": normal((L, D_FF, D), D_FF ** -0.5),
        "ffn2_post_norm": gain(D),
    }

def first_block(x, mem, ffn1_pre_norm, ffn1_w_gate, ffn1_w_up, ffn1_w_down, ffn1_post_norm,
              mix_pre_norm, w_in, cmp_pos_k, cmp_pos_v, cmp_k_w1, cmp_k_w2, cmp_v_w1, cmp_v_w2,
              rel_bias, dn_conv_w, dn_a_log, dn_dt_bias, dn_out_norm, mem_norm, w_mem_kv,
              w_branch_nsa, w_branch_dn, w_branch_mem, w_branch_gate, w_out, mix_post_norm,
              ffn2_pre_norm, ffn2_w_gate, ffn2_w_up, ffn2_w_down, ffn2_post_norm):
    b, s, d = x.shape
    f32 = jnp.float32
    for l in range(DEPTH):
        h = swiglu(rms_norm(x, ffn1_pre_norm[l]), ffn1_w_gate[l], ffn1_w_up[l], ffn1_w_down[l])
        x = x + 0.5 * rms_norm(h, ffn1_post_norm[l])

        u = rms_norm(x, mix_pre_norm[l])
        nsa_q, nsa_kv, nsa_g, dn_qkv, dn_a, dn_b, dn_z, mem_q = split_cols(u @ w_in[l], IN_SPLITS)

        q = nsa_q.reshape(b, s, NSA_GROUPS, NSA_HPG, NSA_HEAD_DIM)
        kv = nsa_kv.reshape(b, s, 6, NSA_GROUPS, NSA_HEAD_DIM)
        k_cmp = compress_blocks(kv[:, :, 0], cmp_pos_k[l], cmp_k_w1[l], cmp_k_w2[l])
        v_cmp = compress_blocks(kv[:, :, 1], cmp_pos_v[l], cmp_v_w1[l], cmp_v_w2[l])
        o_cmp, p_cmp = nsa_compressed(q, k_cmp, v_cmp, rel_bias)
        sel_idx, sel_ok = select_blocks(p_cmp, s)
        o_sel = nsa_selected(q, kv[:, :, 2], kv[:, :, 3], sel_idx, sel_ok, rel_bias)
        o_win = nsa_window(q, kv[:, :, 4], kv[:, :, 5], rel_bias)
        g = jax.nn.sigmoid(nsa_g).reshape(b, s, 3, NSA_GROUPS, NSA_HPG, 1)
        o_nsa = (g[:, :, 0] * o_cmp + g[:, :, 1] * o_sel + g[:, :, 2] * o_win).reshape(b, s, NSA_Q)

        qkv = jax.nn.silu(causal_depthwise_conv(dn_qkv, dn_conv_w[l]))
        dq, dk, dv = split_cols(qkv, (DN_W, DN_W, DN_W))
        dq = l2_norm(dq.reshape(b, s, DN_HEADS, DN_HEAD_DIM))
        dk = l2_norm(dk.reshape(b, s, DN_HEADS, DN_HEAD_DIM))
        dv = dv.reshape(b, s, DN_HEADS, DN_HEAD_DIM)
        log_decay = -jnp.exp(dn_a_log[l].astype(f32)) * jax.nn.softplus((dn_a + dn_dt_bias[l]).astype(f32))
        beta = jax.nn.sigmoid(dn_b.astype(f32))
        o_dn = gated_delta_rule(dq, dk, dv, log_decay, beta).astype(x.dtype)
        o_dn = rms_norm(o_dn, dn_out_norm[l]) * jax.nn.silu(dn_z.reshape(b, s, DN_HEADS, DN_HEAD_DIM))
        o_dn = o_dn.reshape(b, s, DN_W)

        o_mem = memory_cross_attention(mem_q.reshape(b, s, X_HEADS, X_HEAD_DIM),
                                       rms_norm(mem, mem_norm[l]), w_mem_kv[l]).reshape(b, s, X_W)

        gates = jax.nn.sigmoid(u @ w_branch_gate[l]).reshape(b, s, N_BRANCH, d)
        merged = (gates[:, :, 0] * (o_nsa @ w_branch_nsa[l])
                  + gates[:, :, 1] * (o_dn @ w_branch_dn[l])
                  + gates[:, :, 2] * (o_mem @ w_branch_mem[l]))
        x = x + rms_norm(merged @ w_out[l], mix_post_norm[l])

        h = swiglu(rms_norm(x, ffn2_pre_norm[l]), ffn2_w_gate[l], ffn2_w_up[l], ffn2_w_down[l])
        x = x + 0.5 * rms_norm(h, ffn2_post_norm[l])
    return x


DEPTH_2 = 2

D_CONV = D_MODEL // 2
D_POOL = D_MODEL // 2
CONV_K = 31
POOL_WINDOWS = (2, 4, 8, 16)
N_POOL_GROUPS = len(POOL_WINDOWS)
POOL_GROUP = D_POOL // N_POOL_GROUPS
POOL_OUT_GROUP = D_MODEL // N_POOL_GROUPS
N_BRANCHES = 2
D_IN = 2 * D_CONV + D_POOL + N_BRANCHES * D_MODEL

N_EXPERT_GROUPS = 4
EXPERTS_PER_GROUP = 8
N_EXPERTS = N_EXPERT_GROUPS * EXPERTS_PER_GROUP
TOP_K = 2
D_EXPERT = D_MODEL // 4

N_MOD = 6
EPS = 1e-6


def rms_norm_2(x, g):
    xf = x.astype(jnp.float32)
    y = xf * lax.rsqrt(jnp.mean(xf * xf, axis=-1, keepdims=True) + EPS)
    return (y * g.astype(jnp.float32)).astype(x.dtype)

def layer_norm(x, g, b):
    xf = x.astype(jnp.float32)
    mu = jnp.mean(xf, axis=-1, keepdims=True)
    var = jnp.mean(jnp.square(xf - mu), axis=-1, keepdims=True)
    y = (xf - mu) * lax.rsqrt(var + EPS)
    return (y * g.astype(jnp.float32) + b.astype(jnp.float32)).astype(x.dtype)

def modulate(h, shift, scale):
    return h * (1 + scale[:, None, :]) + shift[:, None, :]

def conformer_conv_branch(u, conv_w, conv_b, ln_g, ln_b, w_pw, b_pw):
    a, g = jnp.split(u, 2, axis=-1)
    v = a * jax.nn.sigmoid(g)
    v = lax.conv_general_dilated(
        v, conv_w[:, None, :], window_strides=(1,), padding=[(CONV_K - 1, 0)],
        dimension_numbers=("NWC", "WIO", "NWC"), feature_group_count=D_CONV) + conv_b
    v = jax.nn.silu(layer_norm(v, ln_g, ln_b))
    return v @ w_pw + b_pw

def causal_window_mean(u, w):
    s_len = u.shape[1]
    cs = jnp.cumsum(u.astype(jnp.float32), axis=1)
    shifted = jnp.pad(cs, ((0, 0), (w, 0), (0, 0)))[:, :s_len]
    count = jnp.minimum(jnp.arange(1, s_len + 1), w).astype(jnp.float32)
    return ((cs - shifted) / count[None, :, None]).astype(u.dtype)

def pool_branch(u, pool_w, pool_scale):
    b, s, _ = u.shape
    ug = u.reshape(b, s, N_POOL_GROUPS, POOL_GROUP)
    pooled = jnp.stack([causal_window_mean(ug[:, :, gi], w)
                        for gi, w in enumerate(POOL_WINDOWS)], axis=2) - ug
    y = jnp.einsum("bsgc,gco->bsgo", pooled, pool_w).reshape(b, s, D_MODEL)
    return y * pool_scale

def hierarchical_moe(h, w_rg, b_rg, w_re, b_re, w_g, w_u, w_d):
    b, s, d = h.shape
    t = h.reshape(b * s, d)
    n_tok = t.shape[0]
    group_probs = jax.nn.softmax((t @ w_rg + b_rg).astype(jnp.float32), axis=-1)
    p_group, g_idx = lax.top_k(group_probs, 1)
    exp_logits = (t @ w_re + b_re).astype(jnp.float32).reshape(n_tok, N_EXPERT_GROUPS, EXPERTS_PER_GROUP)
    in_group = jnp.take_along_axis(exp_logits, g_idx[:, :, None], axis=1)[:, 0]
    p_exp, e_idx = lax.top_k(jax.nn.softmax(in_group, axis=-1), TOP_K)
    weights = p_group * p_exp / jnp.sum(p_exp, axis=-1, keepdims=True)
    expert_id = g_idx * EXPERTS_PER_GROUP + e_idx
    combine = jnp.sum(jax.nn.one_hot(expert_id, N_EXPERTS, dtype=jnp.float32) * weights[..., None],
                      axis=1).astype(h.dtype)
    out = jnp.zeros_like(t)
    for gi in range(N_EXPERT_GROUPS):
        sl = slice(gi * EXPERTS_PER_GROUP, (gi + 1) * EXPERTS_PER_GROUP)
        act = jax.nn.silu(jnp.einsum("td,edh->teh", t, w_g[sl])) * jnp.einsum("td,edh->teh", t, w_u[sl])
        out = out + jnp.einsum("teh,ehd->td", act * combine[:, sl, None], w_d[sl])
    return out.reshape(b, s, d)

def second_inputs(seed: int = 0) -> dict:
    key = jax.random.key(seed)
    ks = jax.random.split(key, 24)
    f32 = jnp.float32
    nrm = lambda k, shape, scale: (jax.random.normal(k, shape, f32) * scale)
    return {
        "x": nrm(ks[0], (BATCH, SEQ, D_MODEL), 1.0),
        "c": nrm(ks[1], (BATCH, D_MODEL), 1.0),
        "mixer_norm_g": 1.0 + nrm(ks[2], (DEPTH_2, D_MODEL), 0.05),
        "w_ada": nrm(ks[3], (DEPTH_2, D_MODEL, N_MOD * D_MODEL), 0.5 * D_MODEL ** -0.5),
        "b_ada": nrm(ks[4], (DEPTH_2, N_MOD * D_MODEL), 0.02),
        "w_in": nrm(ks[5], (DEPTH_2, D_MODEL, D_IN), D_MODEL ** -0.5),
        "conv_w": nrm(ks[6], (DEPTH_2, CONV_K, D_CONV), CONV_K ** -0.5),
        "conv_b": nrm(ks[7], (DEPTH_2, D_CONV), 0.02),
        "conv_ln_g": 1.0 + nrm(ks[8], (DEPTH_2, D_CONV), 0.05),
        "conv_ln_b": nrm(ks[9], (DEPTH_2, D_CONV), 0.02),
        "w_conv_out": nrm(ks[10], (DEPTH_2, D_CONV, D_MODEL), D_CONV ** -0.5),
        "b_conv_out": nrm(ks[11], (DEPTH_2, D_MODEL), 0.02),
        "pool_w": nrm(ks[12], (DEPTH_2, N_POOL_GROUPS, POOL_GROUP, POOL_OUT_GROUP), POOL_GROUP ** -0.5),
        "pool_scale": 1.0 + nrm(ks[13], (DEPTH_2, D_MODEL), 0.1),
        "w_out": nrm(ks[14], (DEPTH_2, D_MODEL, D_MODEL), D_MODEL ** -0.5),
        "ffn_norm_g": 1.0 + nrm(ks[15], (DEPTH_2, D_MODEL), 0.05),
        "w_router_group": nrm(ks[16], (DEPTH_2, D_MODEL, N_EXPERT_GROUPS), D_MODEL ** -0.5),
        "b_router_group": nrm(ks[17], (DEPTH_2, N_EXPERT_GROUPS), 0.01),
        "w_router_expert": nrm(ks[18], (DEPTH_2, D_MODEL, N_EXPERTS), D_MODEL ** -0.5),
        "b_router_expert": nrm(ks[19], (DEPTH_2, N_EXPERTS), 0.01),
        "w_expert_gate": nrm(ks[20], (DEPTH_2, N_EXPERTS, D_MODEL, D_EXPERT), D_MODEL ** -0.5),
        "w_expert_up": nrm(ks[21], (DEPTH_2, N_EXPERTS, D_MODEL, D_EXPERT), D_MODEL ** -0.5),
        "w_expert_down": nrm(ks[22], (DEPTH_2, N_EXPERTS, D_EXPERT, D_MODEL), D_EXPERT ** -0.5),
        "final_norm_g": 1.0 + nrm(ks[23], (D_MODEL,), 0.05),
    }

def second_block(x, c, mixer_norm_g, w_ada, b_ada, w_in, conv_w, conv_b, conv_ln_g, conv_ln_b,
              w_conv_out, b_conv_out, pool_w, pool_scale, w_out, ffn_norm_g,
              w_router_group, b_router_group, w_router_expert, b_router_expert,
              w_expert_gate, w_expert_up, w_expert_down, final_norm_g):
    c_act = jax.nn.silu(c)
    for l in range(DEPTH_2):
        mod = c_act @ w_ada[l] + b_ada[l]
        sh1, sc1, g1, sh2, sc2, g2 = jnp.split(mod, N_MOD, axis=-1)
        h = modulate(rms_norm_2(x, mixer_norm_g[l]), sh1, sc1)
        proj = h @ w_in[l]
        u_conv = proj[..., :2 * D_CONV]
        u_pool = proj[..., 2 * D_CONV:2 * D_CONV + D_POOL]
        gate_a, gate_b = jnp.split(jax.nn.sigmoid(proj[..., 2 * D_CONV + D_POOL:]), N_BRANCHES, axis=-1)
        y_a = conformer_conv_branch(u_conv, conv_w[l], conv_b[l], conv_ln_g[l], conv_ln_b[l],
                                    w_conv_out[l], b_conv_out[l])
        y_b = pool_branch(u_pool, pool_w[l], pool_scale[l])
        mixed = gate_a * y_a + gate_b * y_b
        x = x + g1[:, None, :] * (mixed @ w_out[l])
        h2 = modulate(rms_norm_2(x, ffn_norm_g[l]), sh2, sc2)
        x = x + g2[:, None, :] * hierarchical_moe(h2, w_router_group[l], b_router_group[l],
                                                  w_router_expert[l], b_router_expert[l],
                                                  w_expert_gate[l], w_expert_up[l], w_expert_down[l])
    return rms_norm_2(x, final_norm_g)


def setup_inputs(seed=0):
    out = dict(first_inputs(seed))
    for name, value in second_inputs(seed + 1).items():
        if name != "x":
            out[name + "_2"] = value
    return out


def reference(
    x, mem, ffn1_pre_norm, ffn1_w_gate, ffn1_w_up, ffn1_w_down, ffn1_post_norm, mix_pre_norm,
    w_in, cmp_pos_k, cmp_pos_v, cmp_k_w1, cmp_k_w2, cmp_v_w1, cmp_v_w2, rel_bias, dn_conv_w,
    dn_a_log, dn_dt_bias, dn_out_norm, mem_norm, w_mem_kv, w_branch_nsa, w_branch_dn,
    w_branch_mem, w_branch_gate, w_out, mix_post_norm, ffn2_pre_norm, ffn2_w_gate, ffn2_w_up,
    ffn2_w_down, ffn2_post_norm, c_2, mixer_norm_g_2, w_ada_2, b_ada_2, w_in_2, conv_w_2,
    conv_b_2, conv_ln_g_2, conv_ln_b_2, w_conv_out_2, b_conv_out_2, pool_w_2, pool_scale_2,
    w_out_2, ffn_norm_g_2, w_router_group_2, b_router_group_2, w_router_expert_2,
    b_router_expert_2, w_expert_gate_2, w_expert_up_2, w_expert_down_2, final_norm_g_2,
):
    x = first_block(
        x, mem, ffn1_pre_norm, ffn1_w_gate, ffn1_w_up, ffn1_w_down, ffn1_post_norm,
        mix_pre_norm, w_in, cmp_pos_k, cmp_pos_v, cmp_k_w1, cmp_k_w2, cmp_v_w1, cmp_v_w2,
        rel_bias, dn_conv_w, dn_a_log, dn_dt_bias, dn_out_norm, mem_norm, w_mem_kv,
        w_branch_nsa, w_branch_dn, w_branch_mem, w_branch_gate, w_out, mix_post_norm,
        ffn2_pre_norm, ffn2_w_gate, ffn2_w_up, ffn2_w_down, ffn2_post_norm,
    )
    return second_block(
        x, c_2, mixer_norm_g_2, w_ada_2, b_ada_2, w_in_2, conv_w_2, conv_b_2, conv_ln_g_2,
        conv_ln_b_2, w_conv_out_2, b_conv_out_2, pool_w_2, pool_scale_2, w_out_2, ffn_norm_g_2,
        w_router_group_2, b_router_group_2, w_router_expert_2, b_router_expert_2,
        w_expert_gate_2, w_expert_up_2, w_expert_down_2, final_norm_g_2,
    )


_drawn_inputs = setup_inputs


def setup_inputs(seed=0):
    import zlib

    import numpy as np

    out = dict(_drawn_inputs(seed))
    spreads = {}
    factors = {'ffn1_pre_norm': 2.872,
     'ffn1_post_norm': 4.124,
     'cmp_pos_k': 8.0,
     'dn_out_norm': 3.703,
     'mem_norm': 8.0,
     'mix_post_norm': 4.019,
     'ffn2_pre_norm': 4.852,
     'ffn2_post_norm': 6.469,
     'mixer_norm_g_2': 5.493,
     'b_ada_2': 3.068,
     'conv_b_2': 8.0,
     'conv_ln_g_2': 8.0,
     'conv_ln_b_2': 8.0,
     'b_conv_out_2': 8.0,
     'pool_scale_2': 3.626,
     'ffn_norm_g_2': 3.329,
     'b_router_group_2': 8.0,
     'b_router_expert_2': 8.0}
    for name, (base, spread) in spreads.items():
        noise = np.random.default_rng([zlib.crc32(name.encode()), seed]).standard_normal(out[name].shape)
        drawn = base * np.exp(spread * noise) if base else spread * noise
        out[name] = jnp.asarray(drawn.astype(out[name].dtype))
    for name, factor in factors.items():
        out[name] = (out[name] * factor).astype(out[name].dtype)
    return out
```

```python
from contextlib import ExitStack

import numpy as np

import concourse.bass as bass
from concourse import mybir
from concourse.alu_op_type import AluOpType as ALU

F32 = mybir.dt.float32
F32R = mybir.dt.float32r
BF16 = mybir.dt.bfloat16
ACT = mybir.ActivationFunctionType
X_AXIS = mybir.AxisListType.X

P = 128
T = 256
QT = T // P
D = 1024
DC = D // P
FF = 2816
FC = FF // P
EPS = 1e-6
TILE = 1024
RAW = 6
AHEAD = 3
NEG = -1e30

HEADS, GROUPS, HPG, DH = 8, 2, 4, 64
CMP_BLOCK, CMP_STRIDE, CMP_HIDDEN = 32, 16, 256
NCMP = T // CMP_STRIDE - 1
NCMP0 = 7
BUCKETS, MAX_DIST = 32, 128
BROW = 384
DNH = 4
LEVELS = 7
LAYERS = 2
EXPERTS, EGROUPS, EPG, EH = 32, 4, 8, 256
CONV_K = 31
WINDOWS = (2, 4, 8, 16)
IN_W = 3864


def columns(widths):
    out, at = {}, 0
    for name, n in widths:
        out[name] = (at, at + n)
        at += n
    return out, at


CONST_W = [("ident", P), ("ones", P), ("upper", P), ("levels", LEVELS * P),
           ("onehot", BROW), ("maskrow", BROW), ("has_block", QT), ("iota4", 4), ("iota8", 8),
           ("inv_count", len(WINDOWS) * 16)]
CONST, NCONST = columns(CONST_W)
LAYER_W = [("norm", DC), ("b_ada", 48), ("conv_w", 4 * CONV_K), ("conv_b", 4), ("ln_g", 4), ("ln_b", 4),
           ("b_out", DC), ("pool_scale", DC), ("ffn_norm", DC), ("router", DC * 36), ("router_b", 36)]
PARAM_W = [("ffn1_pre", DC), ("ffn1_post", DC), ("mix_pre", DC), ("mix_post", DC), ("ffn2_pre", DC),
           ("ffn2_post", DC), ("mem_norm", DC), ("final", DC), ("dn_conv", 48), ("dn_norm", 1),
           ("a_log", DNH), ("dt_bias", DNH), ("w_small", DC * 32), ("w2k", 2 * DH), ("w2v", 2 * DH),
           ("posk", 16), ("posv", 16), ("rel", HEADS), ("c", DC)]
PARAM_W += [(f"{n}{l}", w) for l in range(LAYERS) for n, w in LAYER_W]
PARAM, NPARAM = columns(PARAM_W)


def swiglu_order(n):
    out = [("g", 0), ("u", 0)]
    for f in range(1, n):
        out += [("g", f), ("u", f), ("d", f - 1)]
    return out + [("d", n - 1)]


def stream():
    out = [("ffn1", w, True) for w in swiglu_order(FC)]
    out += [("memk", m, True) for m in range(4)] + [("memv", m, True) for m in range(4)]
    out += [("dn", m, True) for m in range(12)] + [("z", m, True) for m in range(4)]
    out += [("v", m, True) for m in range(2)] + [("q", m, True) for m in range(4)]
    out += [("kv", m, True) for m in range(4)] + [("memq", m, True) for m in range(4)]
    out += [("w1", m, False) for m in range(8)]
    out += [("ada", m, False) for m in range(LAYERS * 48)]
    out += [("gate", m, True) for m in range(24)]
    out += [("branch", (m, b), True) for m in range(4) for b in range(3)]
    out += [("wout", m, True) for m in range(DC)]
    out += [("ffn2", w, True) for w in swiglu_order(FC)]
    for l in range(LAYERS):
        out += [(f"a{l}", m, True) for m in range(8)] + [(f"p{l}", m, True) for m in range(4)]
        out += [(f"G{l}", m, True) for m in range(16)]
        out += [(f"pool{l}", 0, True)] + [(f"conv{l}", m, True) for m in range(4)]
        out += [(f"wout{l}", m, True) for m in range(DC)]
        out += [(f"moe{l}", w, True) for w in swiglu_order(2 * EXPERTS)]
    return out


STREAM = stream()
SPLITS = [r for r, t in enumerate(STREAM) if t[2]]
NUMBER = {r: n for n, r in enumerate(SPLITS)}
START = {}
for _r, _t in enumerate(STREAM):
    START.setdefault(_t[0], _r)


LOOPED = {"ffn1": FC, "ffn2": FC, "moe0": 2 * EXPERTS, "moe1": 2 * EXPERTS}
FIRST_F = {"ffn1": 0, "ffn2": FC, "moe0": 2 * FC, "moe1": 2 * FC + 2 * EXPERTS}


def along(value, i, per):
    return value if i is None else value + per * i


def swiglu_steps(eng, stage, step):
    n, at, order = LOOPED[stage], START[stage], swiglu_order(LOOPED[stage])
    for j in range(2):
        step(at + j, *order[j], None)
    turns = (n - 2) // 2
    with eng.Fori(0, turns) as i:
        for j in range(2, 8):
            step(at + j, *order[j], i)
    for j in range(3 * n - 4, 3 * n):
        step(at + j, *order[j], None)
    return turns


def program(nc, wstream, consts_d, params_d, x_d, mem_d, rows_d, out_d):
    with ExitStack() as ctx:
        sems = {}

        def s(name):
            if name not in sems:
                sems[name] = ctx.enter_context(nc.semaphore(name))
            return sems[name]

        def sb(name, shape, dt=F32, where=ctx):
            return where.enter_context(nc.sbuf_tensor(name, shape, dt))

        raw = [sb(f"raw{i}", [P, TILE]) for i in range(RAW)]
        whi = [sb(f"whi{i}", [P, TILE], F32R) for i in range(AHEAD)]
        wlo = [sb(f"wlo{i}", [P, TILE], F32R) for i in range(AHEAD)]
        xT = sb("xT", [P, DC, T])
        hf = sb("hf", [P, DC, T])
        hhi = sb("hhi", [P, DC, T], F32R)
        hlo = sb("hlo", [P, DC, T], F32R)
        consts = sb("consts", [P, NCONST])
        params = sb("params", [P, NPARAM])
        var = sb("var", [P, T])
        std = sb("std", [P, T])
        rstd = sb("rstd", [P, T])
        zero = sb("zero", [P, 512], BF16)
        pair_a = sb("pair_a", [P, 2, T])
        pair_b = sb("pair_b", [P, 2, T])
        ahi = sb("ahi", [P, 2, T], F32R)
        alo = sb("alo", [P, 2, T], F32R)
        mod = sb("mod", [P, LAYERS * 48])
        c_act = sb("c_act", [P, DC])
        gscale = sb("gscale", [P, LAYERS * 2 * DC])

        acc = ctx.enter_context(nc.psum_tensor("acc", [P, DC * T], F32))
        work = [ctx.enter_context(nc.psum_tensor(f"work{i}", [P, 512], F32)) for i in range(4)]
        acc_c = acc[:, :].rearrange("p (c t) -> p c t", t=T)

        def const(name):
            return consts[:, CONST[name][0]:CONST[name][1]]

        def par(name):
            return params[:, PARAM[name][0]:PARAM[name][1]]

        def col(name, m):
            return params[:, PARAM[name][0] + m:PARAM[name][0] + m + 1]

        def spread(ap, shape, steps):
            return bass.AP(tensor=ap.tensor, offset=ap.offset, ap=[list(ap.ap[0])] + [[st, n] for st, n in zip(steps, shape)])

        ident, ones, upper = const("ident"), const("ones"), const("upper")

        mixer, att, early, dn, late = (ExitStack() for _ in range(5))
        dnc = sb("dnc", [P, 12, T], F32, mixer)
        zT = sb("zT", [P, DNH, T], F32, mixer)
        ohi = sb("ohi", [P, 3, 4, T], F32R, mixer)
        olo = sb("olo", [P, 3, 4, T], F32R, mixer)
        small = sb("small", [P, QT, 32], F32, mixer)
        sm = sb("sm", [P, 256], F32, mixer)
        kmem = sb("kmem", [P, 4, T], F32, att)
        vmem = sb("vmem", [P, QT, 512], F32, att)
        tb = sb("tb", [P, HEADS, T], F32, att)
        vtok = sb("vtok", [P, QT, 2 * P], F32, att)
        qT = sb("qT", [P, 4, T], F32, att)
        kvT = sb("kvT", [P, 4, T], F32, att)
        qmem = sb("qmem", [P, 4, T], F32, att)
        soft = sb("soft", [P, DC * T], F32, att)
        memhi = sb("memhi", [P, DC, T], F32R, early)
        memlo = sb("memlo", [P, DC, T], F32R, early)
        early.close()
        pt = sb("pt", [P, 16 * P], F32, att)
        convin = sb("convin", [P, 3, 3 + T], F32, att)
        hidden = sb("hidden", [P, 2, 2, 30], F32, att)
        kcmp = sb("kcmp", [P, 16], F32, att)
        vcmp = sb("vcmp", [P, GROUPS, HPG, DH], F32, att)
        scmp = sb("scmp", [P, 16, 16], F32, att)
        pcmp = sb("pcmp", [P, QT * GROUPS, HPG, 32], F32, att)
        att.close()
        pcT = pt[:, 0:GROUPS * T].rearrange("p (g t) -> p g t", t=T)
        dn_el, dn_eu, dn_a, dn_b, dn_inv, dn_invT, dn_z, dn_qk, dn_vb, dn_kb, dn_vn = (
            sb(f"dn_{n}", [P, 8 * P], F32, dn)
            for n in ("el", "eu", "a", "b", "inv", "invT", "z", "qk", "vb", "kb", "vn"))
        dn_kd, dn_w, dn_s, dn_qd = (sb(f"dn_{n}", [P, 4 * P], F32, dn) for n in ("kd", "w", "s", "qd"))
        dn.close()
        gates = sb("gates", [P, 3 * DC, T], F32, late)
        late.close()
        mixer.close()
        gate2 = sb("gate2", [P, 2 * DC, T])
        comb = sb("comb", [P, EXPERTS, T])
        vpad = sb("vpad", [P, 4, 30 + T])
        yconv = sb("yconv", [P, 4, T])
        ppad = sb("ppad", [P, 4, 16 + T])
        yhi = sb("yhi", [P, 4, T], F32R)
        ylo = sb("ylo", [P, 4, T], F32R)
        phi = sb("phi", [P, 4, T], F32R)
        plo = sb("plo", [P, 4, T], F32R)
        rt = sb("rt", [P, 512])

        def tile_loaded(eng, r, i=None):
            eng.wait_ge(s(f"loaded{r % RAW}"), along(16 * (r // RAW + 1), i, 16))

        held = set(range(NUMBER[START["gate"]], NUMBER[START["gate"]] + AHEAD))

        EVAC = {}
        for r, (stage, what, _) in enumerate(STREAM):
            if stage.rstrip("01") in ("memk", "memv", "dn", "z", "v", "q", "kv", "memq", "gate", "a", "p", "G"):
                EVAC[r] = len(EVAC)

        def evacuated(eng, stage, m):
            eng.wait_ge(s("tile_evac"), EVAC[START[stage] + m] + 1)

        block = ctx.enter_context(nc.Block())

        @block.sync
        def _(sp):
            sp.dma_start(params[:], params_d).then_inc(s("params_loaded"), 16)
            sp.dma_start(xT[:], x_d).then_inc(s("x_loaded"), 16)
            sp.dma_start(consts[:], consts_d).then_inc(s("consts_loaded"), 16)
            sp.dma_start(soft[:, :], mem_d.rearrange("p c t -> p (c t)")).then_inc(s("mem_loaded"), 16)

            def load(r, i=None):
                if r >= RAW:
                    if r - RAW in NUMBER:
                        sp.wait_ge(s("lo_done"), along(NUMBER[r - RAW] + 1, i, 6))
                    else:
                        sp.wait_ge(s("pe_tile"), r - RAW + 1)
                src = wstream[r] if i is None else wstream[bass.ds(r + 6 * i, 1)].rearrange("o p c -> (o p) c")
                sp.dma_start(raw[r % RAW][:], src).then_inc(s(f"loaded{r % RAW}"), 16)

            r = 0
            while r < len(STREAM):
                stage = STREAM[r][0]
                if stage in LOOPED and r == START[stage] + RAW:
                    turns = (3 * LOOPED[stage] - RAW) // 6
                    with sp.Fori(0, turns) as i:
                        for j in range(6):
                            load(r + j, i)
                    r += 6 * turns
                else:
                    load(r)
                    r += 1
            sp.wait_ge(s("final_ready"), 1)
            sp.dma_start(out_d, hf[:]).then_inc(s("stored"), 16)
            sp.wait_ge(s("stored"), 16)

        @block.gpsimd
        def _(pool):
            half = HEADS // 2
            rows = rows_d.rearrange("h p c -> p h c")
            for n in range(2):
                pool.wait_ge(s("bias_rows"), half * (n + 1))
                pool.dma_start(rows[:, half * n:half * (n + 1), :],
                               soft[:, 0:half * BROW].rearrange("p (h c) -> p h c", c=BROW)
                               ).then_inc(s("rows_stored"), 16)
                pool.wait_ge(s("rows_stored"), 16 * (n + 1))
            skew = bass.AP(tensor=rows_d.tensor, offset=P - 1, ap=[[BROW - 1, P], [P * BROW, HEADS], [1, T]])
            pool.dma_start(tb[:], skew).then_inc(s("tb_loaded"), 16)

        @block.tensor
        def _(pe):
            reader = {}

            def claim(banks, name, count):
                for b in banks:
                    if b in reader:
                        pe.wait_ge(s(reader[b][0]), reader[b][1])
                    reader[b] = (name, count)

            def norm_sum(k, bank, n=DC, src=hf):
                claim([bank], "norm_var", k + 1)
                pe.wait_ge(s("norm_sq"), k + 1)
                for m in range(n):
                    mm = pe.matmul(work[bank][:, 0:T], ones, src[:, m, :], start=(m == 0), stop=(m == n - 1))
                mm.then_inc(s("norm_sum"), 1)

            def tile_ready(r, i=None):
                if r in NUMBER:
                    pe.wait_ge(s("lo_done"), along(NUMBER[r] + 1, i, 6))
                    return whi[NUMBER[r] % AHEAD], wlo[NUMBER[r] % AHEAD]
                tile_loaded(pe, r)
                return raw[r % RAW], None

            def product(out, terms, start=True, stop=True, skip=False):
                n = 3 * len(terms)
                k = 0
                for (lh, ll), (rh, rl) in terms:
                    for a, b in ((lh, rh), (lh, rl), (ll, rh)):
                        mm = pe.matmul(out, a, b, start=(start and k == 0), stop=(stop and k == n - 1),
                                       skip_group_check=skip)
                        k += 1
                return mm

            def feature_tile(r, xh, xl, bank=None, out=None):
                h, l = tile_ready(r)
                if out is None:
                    claim([bank], "tile_evac", EVAC[r] + 1)
                    out = work[bank][:, 0:T]
                mm = product(out, [((h[:, c * P:(c + 1) * P], l[:, c * P:(c + 1) * P]), (xh[:, c, :], xl[:, c, :]))
                                   for c in range(DC)])
                mm.then_inc(s("pe_tile"), 1)

            def token_tile(r, xh, xl, bank):
                h, l = tile_ready(r)
                claim([bank], "tile_evac", EVAC[r] + 1)
                for q in range(QT):
                    t = slice(q * P, (q + 1) * P)
                    mm = product(work[bank][:, t], [((xh[:, c, t], xl[:, c, t]),
                                                     (h[:, c * P:(c + 1) * P], l[:, c * P:(c + 1) * P]))
                                                    for c in range(DC)])
                mm.then_inc(s("pe_tile"), 1)

            def wide_tile(r, xh, xl, out, kc=4):
                h, l = tile_ready(r)
                for m in range(2):
                    mm = product(out[:, m * T:(m + 1) * T],
                                 [((h[:, c * T + m * P:c * T + (m + 1) * P], l[:, c * T + m * P:c * T + (m + 1) * P]),
                                   (xh[:, c, :], xl[:, c, :])) for c in range(kc)])
                mm.then_inc(s("pe_tile"), 1)

            def clear(banks):
                pe.wait_ge(s("zero_ready"), 1)
                for out in banks:
                    pe.matmul(out, zero[:, 0:P], zero[:, :], start=True, stop=True)

            def swiglu(stage, out_reader, out_count):
                claim(["acc"], out_reader, out_count)
                clear([acc[:, b * 512:(b + 1) * 512] for b in range(4)])
                base = FIRST_F[stage]
                claim(range(4), "act_ready", base + LOOPED[stage])

                def step(r, what, f, i):
                    h, l = tile_ready(r, i)
                    p = f % 2
                    if what == "d":
                        pe.wait_ge(s("act_ready"), along(base + f + 1, i, 2))
                        for m in range(DC):
                            c = slice(m * P, (m + 1) * P)
                            mm = product(acc_c[:, m, :], [((h[:, c], l[:, c]), (ahi[:, p, :], alo[:, p, :]))],
                                         start=False, skip=True)
                    else:
                        bank = work[2 * p + (what == "u")]
                        mm = product(bank[:, 0:T], [((h[:, c * P:(c + 1) * P], l[:, c * P:(c + 1) * P]),
                                                     (hhi[:, c, :], hlo[:, c, :])) for c in range(DC)])
                    mm.then_inc(s("pe_tile"), 1)

                swiglu_steps(pe, stage, step)

            pe.wait_ge(s("consts_loaded"), 16)
            pe.wait_ge(s("params_loaded"), 16)
            norm_sum(0, 0)
            norm_sum(1, 1)
            for h in range(HEADS):
                claim([h % 4], "bias_rows", h + 1)
                rel = params[0:BUCKETS, PARAM["rel"][0] + h:PARAM["rel"][0] + h + 1]
                pe.matmul(work[h % 4][:, 0:BROW], spread(rel, (P,), (0,)), const("onehot")[0:BUCKETS, :],
                          start=True, stop=True).then_inc(s("bias_mm"), 1)
            pe.wait_ge(s("h_ready"), 2)
            swiglu("ffn1", "x_ready", 1)

            norm_sum(2, 0)
            pe.wait_ge(s("mem_ready"), 2)
            for m in range(4):
                feature_tile(START["memk"] + m, memhi, memlo, 1 + m % 3)
            norm_sum(3, 0)
            for m in range(4):
                token_tile(START["memv"] + m, memhi, memlo, 1 + m % 3)

            pe.wait_ge(s("hf_done"), 6)
            claim([0], "small_ready", 1)
            for q in range(QT):
                for c in range(DC):
                    a = PARAM["w_small"][0] + 32 * c
                    mm = pe.matmul(work[0][:, q * 32:(q + 1) * 32], hf[:, c, q * P:(q + 1) * P],
                                   params[:, a:a + 32], start=(c == 0), stop=(c == DC - 1))
            mm.then_inc(s("small_mm"), 1)
            pe.wait_ge(s("h_ready"), 4)
            for m in range(12):
                feature_tile(START["dn"] + m, hhi, hlo, m % 4)
            for m in range(4):
                feature_tile(START["z"] + m, hhi, hlo, m % 4)
            for m in range(2):
                token_tile(START["v"] + m, hhi, hlo, m)
            for n, stage in enumerate(("q", "kv", "memq")):
                for m in range(4):
                    feature_tile(START[stage] + m, hhi, hlo, (2 + m) % 4)

            pe.wait_ge(s("flat_ready"), 1)
            claim(range(4), "hidden_ready", 2)
            flat = hf[:, :, :].rearrange("p c t -> p (c t)")[:, 0:2 * 16 * 30].rearrange("p (v j c) -> p v j c", v=2, j=16)
            for t in range(8):
                v = t // 4
                w, _ = tile_ready(START["w1"] + t)
                for jj in range(4):
                    j = 4 * (t % 4) + jj
                    for m in range(2):
                        mm = pe.matmul(work[2 * v + m][:, 0:30], w[:, jj * T + m * P:jj * T + (m + 1) * P],
                                       flat[:, v, j, :], start=(j == 0), stop=(j == 15), skip_group_check=True)
                mm.then_inc(s("pe_tile"), 1)

            ada_at = [START["ada"]]

            def ada(n):
                for r in range(ada_at[0], min(ada_at[0] + n, START["gate"])):
                    w, _ = tile_ready(r)
                    a = r - START["ada"]
                    if a == 0:
                        pe.wait_ge(s("c_ready"), 1)
                        claim([1], "mod_ready", 1)
                    for c in range(DC):
                        mm = pe.matmul(work[1][:, a:a + 1], w[:, c * P:(c + 1) * P], c_act[:, c:c + 1],
                                       start=(c == 0), stop=(c == DC - 1))
                    mm.then_inc(s("pe_tile"), 1)
                    ada_at[0] += 1

            def scores(g):
                if g == 0:
                    evacuated(pe, "memq", 3)
                    claim(["acc"], "sm_exp", 1)
                    for q in range(QT):
                        for h in range(4):
                            mm = pe.matmul(acc_c[:, 4 * q + h, :], qmem[:, h, q * P:(q + 1) * P], kmem[:, h, :],
                                           start=True, stop=True)
                elif g == 1:
                    claim(["acc"], "sm_bias", 2)
                    for br in range(2):
                        for h in range(HEADS):
                            d = slice(DH * (h // HPG), DH * (h // HPG) + DH)
                            a = (br * HEADS + h) * P
                            mm = pe.matmul(acc[:, a:a + P], qT[d, h % HPG, 0:P], kvT[d, 2 + br, 0:P],
                                           start=True, stop=True)
                else:
                    claim(["acc"], "sm_bias", g + 1)
                    for h in range(HEADS):
                        d = slice(DH * (h // HPG), DH * (h // HPG) + DH)
                        mm = pe.matmul(acc_c[:, h, :], qT[d, h % HPG, P:T], kvT[d, g, :], start=True, stop=True)
                mm.then_inc(s("sm_scores"), 1)

            def transposes(g):
                for r in range(4):
                    if r % 2 == 0:
                        pe.wait_ge(s("sm_probs"), 2 * g + r // 2 + 1)
                    claim([0], "pt_ready", 4 * g + r + 1)
                    for b in range(4):
                        mm = pe.transpose(work[0][:, b * P:(b + 1) * P],
                                          soft[:, (4 * r + b) * P:(4 * r + b + 1) * P], ident)
                    mm.then_inc(s("pt_mm"), 1)

            def values(g):
                pe.wait_ge(s("pt_ready"), 4 * g + 4)
                if g == 0:
                    claim([2, 3], "olo_ready", 2)
                    for h in range(4):
                        for q in range(QT):
                            for k in range(QT):
                                b = ((4 * q + h) * 2 + k) * P
                                mm = pe.matmul(work[2 + h // 2][:, (h % 2) * T + q * P:(h % 2) * T + (q + 1) * P],
                                               vmem[:, k, h * P:(h + 1) * P], pt[:, b:b + P],
                                               start=(k == 0), stop=(k == QT - 1))
                    mm.then_inc(s("o_mm"), 1)
                    return
                for u in range(16):
                    h, k, br, q = (u % HEADS, 0, u // HEADS, 0) if g == 1 else (u // 2, u % 2, g - 2, 1)
                    gr, j = h // HPG, h % HPG
                    out = work[2 + j // 2][DH * gr:DH * gr + DH, (j % 2) * T + q * P:(j % 2) * T + (q + 1) * P]
                    mm = pe.matmul(out, vtok[:, k, br * P + DH * gr:br * P + DH * gr + DH], pt[:, u * P:(u + 1) * P],
                                   start=False, stop=False, skip_group_check=True)
                if g == 3:
                    mm.then_inc(s("o_mm"), 1)

            scores(0)
            pe.wait_ge(s("hidden_ready"), 2)
            claim([0], "cmp_kv", 5)
            for g in range(GROUPS):
                for m in range(2):
                    pe.matmul(work[0][DH * g:DH * g + DH, 0:NCMP], par("w2k")[:, m * DH:(m + 1) * DH],
                              hidden[:, 0, m, g * NCMP:(g + 1) * NCMP], start=(m == 0), stop=(m == 1),
                              skip_group_check=True)
            for g in range(GROUPS):
                for j in range(HPG):
                    for m in range(2):
                        mm = pe.matmul(work[0][32 * j:32 * j + NCMP, 64 + g * DH:64 + (g + 1) * DH],
                                       hidden[:, 1, m, g * NCMP:(g + 1) * NCMP], par("w2v")[:, m * DH:(m + 1) * DH],
                                       start=(m == 0), stop=(m == 1), skip_group_check=True)
            mm.then_inc(s("cmp_mm"), 1)
            ada(8)
            transposes(0)
            ada(8)
            values(0)
            pe.wait_ge(s("cmp_kv"), 5)
            claim(["acc"], "cmp_bias", 5)
            for q in range(QT):
                for h in range(HEADS):
                    d = slice(DH * (h // HPG), DH * (h // HPG) + DH)
                    a = (h // HPG) * 512 + (q * HPG + h % HPG) * 16
                    mm = pe.matmul(acc[:, a:a + NCMP], qT[d, h % HPG, q * P:(q + 1) * P], kcmp[d, 0:NCMP],
                                   start=True, stop=True)
            mm.then_inc(s("cmp_scores"), 1)
            pe.wait_ge(s("pt_ready"), 4)
            scores(1)
            claim([2, 3], "olo_ready", 4)
            clear([work[2][:, :], work[3][:, :]])
            ada(8)
            pe.wait_ge(s("cmp_probs"), 1)
            claim([0], "pct_ready", 1)
            for b in range(QT * GROUPS):
                q, g = b // GROUPS, b % GROUPS
                mm = pe.transpose(work[0][:, (g * QT + q) * P:(g * QT + q + 1) * P],
                                  pcmp[:, b, :, :].rearrange("p j c -> p (j c)"), ident)
            mm.then_inc(s("pct_mm"), 1)
            ada(4)
            pe.wait_ge(s("pct_ready"), 1)
            for g in range(GROUPS):
                for j in range(HPG):
                    mm = pe.matmul(work[2 + j // 2][DH * g:DH * g + DH, (j % 2) * T:(j % 2) * T + T],
                                   vcmp[:, g, j, :], pcT[:, g, :],
                                   start=False, stop=False, skip_group_check=True)
            mm.then_inc(s("cmp_values"), 1)
            ada(4)
            transposes(1)
            scores(2)
            values(1)
            ada(8)
            transposes(2)
            scores(3)
            values(2)
            ada(8)
            transposes(3)
            values(3)

            pe.wait_ge(s("dn_squares"), 1)
            claim(["acc"], "dn_var", 1)
            for m in range(8):
                mm = pe.matmul(acc_c[:, m, :], ones, hf[:, m, :], start=True, stop=True)
            mm.then_inc(s("dn_sums"), 1)
            ada(8)
            pe.wait_ge(s("dn_decay"), 1)
            claim([0], "dn_gc", 1)
            for c in range(QT):
                pe.matmul(work[0][:, c * 4:c * 4 + 4], upper, sm[:, 16 + 4 * c:20 + 4 * c], start=True, stop=True)
                mm = pe.matmul(work[0][:, 8 + c * 4:12 + c * 4], ones, sm[:, 16 + 4 * c:20 + 4 * c],
                               start=True, stop=True)
            mm.then_inc(s("dn_gc_mm"), 1)
            claim([2, 3], "dn_eg", 1)
            for u in range(8):
                mm = pe.matmul(work[2 + u // 4][:, (u % 4) * P:(u % 4 + 1) * P], spread(sm[:, 16 + u:17 + u], (P,), (0,)),
                               upper, start=True, stop=True)
            mm.then_inc(s("dn_rows_mm"), 1)
            pe.wait_ge(s("dn_unit"), 1)
            claim(["acc"], "dn_kq", 2)
            for u in range(8):
                c, h = u // 4, u % 4
                t = slice(c * P, (c + 1) * P)
                pe.matmul(acc[:, u * P:(u + 1) * P], dnc[:, 4 + h, t], dnc[:, 4 + h, t], start=True, stop=True)
                mm = pe.matmul(acc[:, (8 + u) * P:(9 + u) * P], dnc[:, 4 + h, t], dnc[:, h, t], start=True, stop=True)
            mm.then_inc(s("dn_kq_mm"), 1)
            ada(8)
            claim(["acc"], "dn_tok", 3)
            for u in range(8):
                c, h = u // 4, u % 4
                t = slice(c * P, (c + 1) * P)
                pe.transpose(acc[:, u * P:(u + 1) * P], dnc[:, 4 + h, t], ident)
                mm = pe.transpose(acc[:, (8 + u) * P:(9 + u) * P], dnc[:, 8 + h, t], ident)
            mm.then_inc(s("dn_tok_mm"), 1)
            ada(8)
            for lv in range(LEVELS):
                pe.wait_ge(s("dn_level"), lv + 1)
                claim(["acc"], "dn_update", 2 * lv + 2)
                claim([2, 3], "dn_update", 2 * lv + 2)
                for u in range(8):
                    a = slice(u * P, (u + 1) * P)
                    mm = pe.matmul(acc[:, a], dn_b[:, a], dn_invT[:, a], start=True, stop=True)
                mm.then_inc(s("dn_z_mm"), 1)
                ada(2)
                pe.wait_ge(s("dn_z"), lv + 1)
                for u in range(8):
                    a = slice(u * P, (u + 1) * P)
                    pe.matmul(acc[:, (8 + u) * P:(9 + u) * P], dn_z[:, a], dn_inv[:, a], start=True, stop=True)
                    mm = pe.matmul(work[2 + u // 4][:, (u % 4) * P:(u % 4 + 1) * P], dn_inv[:, a], dn_z[:, a],
                                   start=True, stop=True)
                mm.then_inc(s("dn_x_mm"), 1)
                ada(2)
            pe.wait_ge(s("dn_update"), 2 * LEVELS)
            claim(["acc"], "dn_vw", 2)
            for h in range(4):
                a, b = slice(h * P, (h + 1) * P), slice((4 + h) * P, (5 + h) * P)
                pe.matmul(acc[:, a], dn_invT[:, a], dn_vb[:, a], start=True, stop=True)
                mm = pe.matmul(acc[:, b], dn_kb[:, b], dn_invT[:, b], start=True, stop=True)
            mm.then_inc(s("dn_vw_mm"), 1)
            ada(4)
            pe.wait_ge(s("dn_vw"), 2)
            claim([0], "dn_state", 1)
            for h in range(4):
                a = slice(h * P, (h + 1) * P)
                mm = pe.matmul(work[0][:, a], dn_kd[:, a], dn_vn[:, a], start=True, stop=True)
            mm.then_inc(s("dn_state_mm"), 1)
            ada(4)
            pe.wait_ge(s("dn_state"), 1)
            claim([2], "dn_v1", 1)
            for h in range(4):
                a, b = slice(h * P, (h + 1) * P), slice((4 + h) * P, (5 + h) * P)
                pe.matmul(work[2][:, a], dn_invT[:, b], dn_vb[:, b], start=True, stop=False)
                mm = pe.matmul(work[2][:, a], dn_w[:, a], dn_s[:, a], start=False, stop=True)
            mm.then_inc(s("dn_v1_mm"), 1)
            pe.wait_ge(s("dn_v1"), 1)
            claim(["acc"], "dn_out", 1)
            for h in range(4):
                a, b = slice(h * P, (h + 1) * P), slice((4 + h) * P, (5 + h) * P)
                pe.matmul(acc_c[:, h, 0:P], dn_vn[:, a], dn_qk[:, a], start=True, stop=True)
                pe.matmul(acc_c[:, h, P:T], dn_s[:, a], dn_qd[:, a], start=True, stop=False)
                mm = pe.matmul(acc_c[:, h, P:T], dn_vn[:, b], dn_qk[:, b], start=False, stop=True)
            mm.then_inc(s("dn_o_mm"), 1)
            ada(96)
            pe.wait_ge(s("dn_osq"), 1)
            for h in range(4):
                mm = pe.matmul(acc_c[:, 4 + h, :], ones, hf[:, h, :], start=True, stop=True)
            mm.then_inc(s("dn_osum"), 1)

            for m in range(24):
                feature_tile(START["gate"] + m, hhi, hlo, m % 4)
            pe.wait_ge(s("olo_ready"), 6)
            for n in range(12):
                r = START["branch"] + n
                b = STREAM[r][1][1]
                claim([n % 4], "branch_read", n + 1)
                wide_tile(r, ohi[:, b], olo[:, b], work[n % 4][:, :])
            claim(["acc"], "x_ready", 2)
            pe.wait_ge(s("merged_ready"), 4)
            for m in range(DC):
                feature_tile(START["wout"] + m, hhi, hlo, out=acc_c[:, m, :])
            norm_sum(4, 0)
            norm_sum(5, 0)
            pe.wait_ge(s("h_ready"), 6)
            swiglu("ffn2", "x_ready", 3)
            norm_sum(6, 0)

            for l in range(LAYERS):
                k = 7 + 3 * l
                norm_sum(k, 0)
                pe.wait_ge(s("h_ready"), 8 + 4 * l)
                for n, (stage, count) in enumerate(((f"a{l}", 8), (f"p{l}", 4), (f"G{l}", 16))):
                    for m in range(count):
                        feature_tile(START[stage] + m, hhi, hlo, m % 4)
                pe.wait_ge(s("pooled"), l + 1)
                claim(["acc"], "pool_read", l + 1)
                h, lo = tile_ready(START[f"pool{l}"])
                for m in range(DC):
                    a = slice(m * P, (m + 1) * P)
                    mm = product(acc_c[:, m, :], [((h[:, a], lo[:, a]), (phi[:, m // 2, :], plo[:, m // 2, :]))])
                mm.then_inc(s("pe_tile"), 1)
                pe.wait_ge(s("conv_done2"), l + 1)
                claim([0], "ln_centred", l + 1)
                for m in range(4):
                    mm = pe.matmul(work[0][:, 0:T], ones, yconv[:, m, :], start=(m == 0), stop=(m == 3))
                mm.then_inc(s("ln_mean"), 1)
                norm_sum(k + 1, 1, 4, hf)
                pe.wait_ge(s("y_ready"), l + 1)
                for m in range(4):
                    claim([m], "conv_read", 4 * l + m + 1)
                    wide_tile(START[f"conv{l}"] + m, yhi, ylo, work[m][:, :])
                pe.wait_ge(s("mixed_ready"), 4 * (l + 1))
                claim(["acc"], "x_ready", 4 + 2 * l)
                for m in range(DC):
                    feature_tile(START[f"wout{l}"] + m, hhi, hlo, out=acc_c[:, m, :])
                norm_sum(k + 2, 0)
                pe.wait_ge(s("hf_done"), 12 + 4 * l)
                claim([1], "router_read", l + 1)
                for q in range(QT):
                    for c in range(DC):
                        a = PARAM[f"router{l}"][0] + 36 * c
                        mm = pe.matmul(work[1][:, q * 36:(q + 1) * 36], hf[:, c, q * P:(q + 1) * P],
                                       params[:, a:a + 36], start=(c == 0), stop=(c == DC - 1))
                mm.then_inc(s("router_mm"), 1)
                pe.wait_ge(s("combine_ready"), l + 1)
                for e in range(EXPERTS // 2):
                    claim([e % 4], "comb_ready", 16 * l + e + 1)
                    for j in range(2):
                        for q in range(QT):
                            cw = rt[:, 256 + q * EXPERTS + 2 * e + j:257 + q * EXPERTS + 2 * e + j]
                            mm = pe.matmul(work[e % 4][:, j * T + q * P:j * T + (q + 1) * P], spread(cw, (P,), (0,)),
                                           ident, start=True, stop=True)
                    mm.then_inc(s("comb_mm"), 1)
                pe.wait_ge(s("h_ready"), 10 + 4 * l)
                swiglu(f"moe{l}", "x_ready", 5 + 2 * l)
            norm_sum(7 + 3 * LAYERS, 0)

        @block.scalar
        def _(act):
            done = [0, 0]

            def hi(n, i=None):
                if n >= len(SPLITS) or n in held:
                    return
                tile_loaded(act, SPLITS[n], i)
                if n >= AHEAD:
                    act.wait_ge(s("pe_tile"), along(SPLITS[n - AHEAD] + 1, i, 6))
                act.activation(whi[n % AHEAD][:], raw[SPLITS[n] % RAW][:], ACT.Copy).then_inc(s("hi_done"), 1)

            def evac(r, out, bank, func=ACT.Copy):
                act.wait_ge(s("pe_tile"), r + 1)
                src = work[bank][:, 0:T]
                if len(out.shape) == 3:
                    src = src.rearrange("p (q f) -> p q f", q=QT)
                assert EVAC[r] == done[0]
                act.activation(out, src, func).then_inc(s("tile_evac"), 1)
                done[0] += 1

            def squares(k, src, ready=None, count=0, out=None):
                if ready:
                    act.wait_ge(s(ready), count)
                dst = hf[:, :, :].rearrange("p c t -> p (c t)") if out is None else out
                act.activation(dst, src, ACT.Square).then_inc(s("norm_sq"), 1)

            def roots(k):
                act.wait_ge(s("norm_var"), k + 1)
                act.activation(std[:], var[:], ACT.Sqrt).then_inc(s("norm_std"), 1)

            def high_h(p, dst=None):
                for j in range(2):
                    act.wait_ge(s("hf_done"), 2 * p + j + 1)
                    act.activation((dst or hhi)[:, 4 * j:4 * j + 4, :], hf[:, 4 * j:4 * j + 4, :], ACT.Copy
                                   ).then_inc(s("h_high"), 1)

            def swiglu(stage):
                base = FIRST_F[stage]

                def step(r, what, f, i):
                    hi(NUMBER[r] + AHEAD, i)
                    if what == "u":
                        act.wait_ge(s("pe_tile"), along(r + 1, i, 6))
                        act.activation(pair_a[:, f % 2, :], work[2 * (f % 2)][:, 0:T], ACT.Silu
                                       ).then_inc(s("silu_done"), 1)
                swiglu_steps(act, stage, step)

            xflat = xT[:, :, :].rearrange("p c t -> p (c t)")
            act.wait_ge(s("x_loaded"), 16)
            squares(0, xflat)
            for n in range(AHEAD):
                hi(n)
            roots(0)
            high_h(0)
            act.wait_ge(s("mem_loaded"), 16)
            act.wait_ge(s("h_ready"), 2)
            squares(1, soft[:, :])
            roots(1)
            high_h(1, memhi)
            act.wait_ge(s("params_loaded"), 16)
            act.activation(c_act[:], par("c"), ACT.Silu).then_inc(s("c_ready"), 1)
            swiglu("ffn1")
            squares(2, acc[:, :], "pe_tile", START["memk"])
            roots(2)
            for m in range(4):
                r = START["memk"] + m
                hi(NUMBER[r] + AHEAD)
                evac(r, kmem[:, m, :], 1 + m % 3)
            squares(3, xflat, "x_ready", 1)
            roots(3)
            for m in range(4):
                r = START["memv"] + m
                hi(NUMBER[r] + AHEAD)
                evac(r, vmem[:, :, m * P:(m + 1) * P], 1 + m % 3)
                if m == 1:
                    high_h(2)
            act.wait_ge(s("small_mm"), 1)
            act.activation(small[:, :, 0:32], work[0][:, 0:64].rearrange("p (q f) -> p q f", q=QT), ACT.Copy
                           ).then_inc(s("small_ready"), 1)
            act.wait_ge(s("pads_ready"), 1)
            for m in range(12):
                r = START["dn"] + m
                hi(NUMBER[r] + AHEAD)
                if m >= 3:
                    act.wait_ge(s("conv_done"), m - 2)
                evac(r, convin[:, m % 3, 3:3 + T], m % 4)
            for m in range(4):
                r = START["z"] + m
                hi(NUMBER[r] + AHEAD)
                evac(r, zT[:, m, :], m % 4)
            for m in range(2):
                r = START["v"] + m
                hi(NUMBER[r] + AHEAD)
                evac(r, vtok[:, :, m * P:(m + 1) * P], m)
            for stage, dst in (("q", qT), ("kv", kvT), ("memq", qmem)):
                for m in range(4):
                    r = START[stage] + m
                    hi(NUMBER[r] + AHEAD)
                    evac(r, dst[:, m, :], (2 + m) % 4)
            for v in range(2):
                act.wait_ge(s("pe_tile"), START["w1"] + 4 * (v + 1))
                for m in range(2):
                    a = act.activation(hidden[:, v, m, :], work[2 * v + m][:, 0:30], ACT.Silu)
                a.then_inc(s("hidden_ready"), 1)
            act.wait_ge(s("conv_done"), 12)
            act.activation(dnc[:, :, :].rearrange("p c t -> p (c t)"), dnc[:, :, :].rearrange("p c t -> p (c t)"),
                           ACT.Silu).then_inc(s("dn_silu"), 1)
            act.activation(zT[:, :, :].rearrange("p c t -> p (c t)"), zT[:, :, :].rearrange("p c t -> p (c t)"),
                           ACT.Silu).then_inc(s("z_silu"), 1)
            act.wait_ge(s("small_ready"), 1)
            act.activation(sm[:, 128:176].rearrange("p (q f) -> p q f", q=QT), small[:, :, 0:24], ACT.Sigmoid
                           ).then_inc(s("nsa_gates"), 1)
            act.activation(sm[:, 184:192].rearrange("p (q f) -> p q f", q=QT), small[:, :, 28:32], ACT.Sigmoid
                           ).then_inc(s("dn_beta"), 1)
            act.wait_ge(s("dn_absz"), 1)
            act.activation(sm[:, 32:40], sm[:, 24:32], ACT.Exp, scale=-1.0).then_inc(s("act_chain"), 1)
            act.wait_ge(s("act_chain"), 1)
            act.activation(sm[:, 40:48], sm[:, 32:40], ACT.Ln, bias=1.0).then_inc(s("act_chain"), 1)
            act.activation(sm[:, 48:52], par("a_log"), ACT.Exp).then_inc(s("dn_logs"), 1)

            def exps(g):
                act.wait_ge(s("sm_max"), g + 1)
                n = 16 if g == 1 else 8
                w = DC * T // n
                for u in range(n):
                    src = acc if g == 0 else soft
                    a = act.activation(soft[:, u * w:(u + 1) * w], src[:, u * w:(u + 1) * w], ACT.Exp,
                                       bias=sm[:, 64 + u:65 + u], scale=128 ** -0.5 if g == 0 else 1.0,
                                       accum_out=sm[:, 80 + u:81 + u])
                a.then_inc(s("sm_exp"), 1)

            def pt_evac(g):
                for r in range(4):
                    act.wait_ge(s("pt_mm"), 4 * g + r + 1)
                    act.activation(pt[:, r * 512:(r + 1) * 512], work[0][:, :], ACT.Copy).then_inc(s("pt_ready"), 1)

            def o_high(b, n):
                act.wait_ge(s("o_mm"), n)
                for j in range(2):
                    a = act.activation(ohi[:, b, 2 * j:2 * j + 2, :].rearrange("p c t -> p (c t)"),
                                       work[2 + j][:, :], ACT.Copy)
                    a.then_inc(s("o_high"), 1)

            act.wait_ge(s("tb_loaded"), 16)
            exps(0)
            act.wait_ge(s("cmp_mm"), 1)
            act.wait_ge(s("pads_ready"), 1)
            act.activation(kcmp[:, 0:NCMP], work[0][:, 0:NCMP], ACT.Copy).then_inc(s("cmp_kv"), 1)
            for j in range(HPG):
                act.activation(vcmp[32 * j:32 * j + NCMP, :, j, :],
                               work[0][32 * j:32 * j + NCMP, 64:64 + 2 * DH].rearrange("p (g d) -> p g d", d=DH),
                               ACT.Copy).then_inc(s("cmp_kv"), 1)
            pt_evac(0)
            o_high(2, 1)
            act.wait_ge(s("cmp_centred"), 1)
            act.activation(scmp[:, :, :].rearrange("p a b -> p (a b)"), scmp[:, :, :].rearrange("p a b -> p (a b)"),
                           ACT.Exp).then_inc(s("cmp_exp"), 1)
            act.wait_ge(s("pct_mm"), 1)
            act.activation(pt[:, 0:512], work[0][:, :], ACT.Copy).then_inc(s("pct_ready"), 1)
            exps(1)
            act.wait_ge(s("cmp_values"), 1)
            pt_evac(1)
            exps(2)
            pt_evac(2)
            exps(3)
            pt_evac(3)
            o_high(0, 2)

            act.wait_ge(s("olo_ready"), 4)
            flat_hf = hf[:, :, :].rearrange("p c t -> p (c t)")
            act.activation(flat_hf, dnc[:, 0:8, :].rearrange("p c t -> p (c t)"), ACT.Square
                           ).then_inc(s("dn_squares"), 1)
            act.wait_ge(s("dn_var"), 1)
            act.activation(flat_hf, flat_hf, ACT.Sqrt).then_inc(s("dn_root"), 1)
            act.wait_ge(s("dn_gc"), 1)
            act.activation(sm[:, 192:200], sm[:, 0:8], ACT.Exp).then_inc(s("dn_exp"), 1)
            act.wait_ge(s("dn_rest"), 1)
            act.activation(sm[:, 200:208], sm[:, 208:216], ACT.Exp).then_inc(s("dn_exp"), 1)
            act.wait_ge(s("dn_diff"), 2)
            act.activation(dn_el[:, :], dn_el[:, :], ACT.Exp, scale=-1.0).then_inc(s("dn_decays"), 1)
            act.activation(dn_eu[:, :], dn_eu[:, :], ACT.Exp).then_inc(s("dn_decays"), 1)
            act.activation(dn_qd[:, :], work[3][:, :], ACT.Exp).then_inc(s("dn_eg"), 1)
            act.wait_ge(s("dn_tok_mm"), 1)
            act.wait_ge(s("dn_scales"), 1)
            for u in range(8):
                a = act.activation(dn_vb[:, u * P:(u + 1) * P], acc[:, (8 + u) * P:(9 + u) * P], ACT.Copy,
                                   scale=sm[:, 184 + u:185 + u])
            a.then_inc(s("dn_vtok"), 1)
            for lv in range(LEVELS):
                act.wait_ge(s("dn_z_mm"), lv + 1)
                act.activation(dn_z[:, :], acc[:, 0:8 * P], ACT.Copy).then_inc(s("dn_z"), 1)
            act.wait_ge(s("dn_vw_mm"), 1)
            act.activation(dn_vn[:, 0:4 * P], acc[:, 0:4 * P], ACT.Copy).then_inc(s("dn_vw"), 1)
            act.activation(dn_w[:, :], acc[:, 4 * P:8 * P], ACT.Copy, scale=-1.0).then_inc(s("dn_vw"), 1)
            act.wait_ge(s("dn_state_mm"), 1)
            act.activation(dn_s[:, :], work[0][:, :], ACT.Copy).then_inc(s("dn_state"), 1)
            act.wait_ge(s("dn_v1_mm"), 1)
            act.activation(dn_vn[:, 4 * P:8 * P], work[2][:, :], ACT.Copy).then_inc(s("dn_v1"), 1)
            act.wait_ge(s("dn_o_mm"), 1)
            act.activation(flat_hf[:, 0:4 * T], acc[:, 0:4 * T], ACT.Square).then_inc(s("dn_osq"), 1)
            act.wait_ge(s("dn_ovar"), 1)
            act.activation(flat_hf[:, 4 * T:8 * T], flat_hf[:, 4 * T:8 * T], ACT.Sqrt).then_inc(s("dn_oroot"), 1)

            first = sorted(held)
            held.clear()
            for n in first:
                hi(n)
            held.update(first)
            for m in range(24):
                r = START["gate"] + m
                hi(NUMBER[r] + AHEAD)
                if m == 0:
                    act.wait_ge(s("dn_o_scaled"), 1)
                evac(r, gates[:, m, :], m % 4, ACT.Sigmoid)
            for n in range(12):
                hi(NUMBER[START["branch"] + n] + AHEAD)
                if n % 3 == 2:
                    act.wait_ge(s("merged"), n // 3 + 1)
                    m = 2 * (n // 3)
                    act.activation(hhi[:, m:m + 2, :], hf[:, m:m + 2, :], ACT.Copy).then_inc(s("merged_high"), 1)
            for m in range(DC):
                hi(NUMBER[START["wout"] + m] + AHEAD)
            squares(4, acc[:, :], "pe_tile", START["wout"] + DC)
            roots(4)
            squares(5, xflat, "x_ready", 2)
            roots(5)
            high_h(3)
            swiglu("ffn2")
            squares(6, acc[:, :], "pe_tile", START["a0"])
            roots(6)
            for l in range(LAYERS):
                k = 7 + 3 * l
                squares(k, xflat, "x_ready", 3 + 2 * l)
                roots(k)
                high_h(4 + 2 * l)
                for m in range(8):
                    r = START[f"a{l}"] + m
                    hi(NUMBER[r] + AHEAD)
                    if m >= 4:
                        act.wait_ge(s("glu_done"), 4 * l + m // 2 - 1)
                    evac(r, (pair_a, pair_b)[m % 2][:, (m // 2) % 2, :], m % 4, (ACT.Copy, ACT.Sigmoid)[m % 2])
                for m in range(4):
                    r = START[f"p{l}"] + m
                    hi(NUMBER[r] + AHEAD)
                    evac(r, ppad[:, m, 16:16 + T], m % 4)
                for m in range(16):
                    r = START[f"G{l}"] + m
                    hi(NUMBER[r] + AHEAD)
                    evac(r, gate2[:, m, :], m % 4, ACT.Sigmoid)
                hi(NUMBER[START[f"pool{l}"]] + AHEAD)
                act.wait_ge(s("ln_centred"), l + 1)
                squares(k + 1, yconv[:, :, :].rearrange("p c t -> p (c t)"), out=flat_hf[:, 0:4 * T])
                roots(k + 1)
                for m in range(4):
                    if m == 0:
                        act.wait_ge(s("ln_scaled"), l + 1)
                    a = act.activation(yconv[:, m, :], yconv[:, m, :], ACT.Silu, bias=col(f"ln_b{l}", m),
                                       scale=col(f"ln_g{l}", m))
                a.then_inc(s("y_silu"), 1)
                act.wait_ge(s("y_silu"), l + 1)
                act.activation(yhi[:, :, :], yconv[:, :, :], ACT.Copy).then_inc(s("y_high"), 1)
                for m in range(4):
                    hi(NUMBER[START[f"conv{l}"] + m] + AHEAD)
                    act.wait_ge(s("mixed"), 4 * l + m + 1)
                    act.activation(hhi[:, 2 * m:2 * m + 2, :], hf[:, 2 * m:2 * m + 2, :], ACT.Copy
                                   ).then_inc(s("mixed_high"), 1)
                for m in range(DC):
                    hi(NUMBER[START[f"wout{l}"] + m] + AHEAD)
                squares(k + 2, xflat, "x_ready", 4 + 2 * l)
                roots(k + 2)
                high_h(5 + 2 * l)
                act.wait_ge(s("router_centred"), 2 * l + 1)
                act.activation(rt[:, 80:88], rt[:, 80:88], ACT.Exp).then_inc(s("router_exp"), 1)
                act.wait_ge(s("router_centred"), 2 * l + 2)
                act.activation(rt[:, 148:150], rt[:, 146:148], ACT.Exp).then_inc(s("router_exp"), 1)
                for e in range(EXPERTS // 2):
                    act.wait_ge(s("comb_mm"), 16 * l + e + 1)
                    act.activation(comb[:, 2 * e:2 * e + 2, :].rearrange("p c t -> p (c t)"), work[e % 4][:, :],
                                   ACT.Copy).then_inc(s("comb_ready"), 1)
                swiglu(f"moe{l}")
            k = 7 + 3 * LAYERS
            squares(k, xflat, "x_ready", 3 + 2 * LAYERS)
            roots(k)

        @block.vector
        def _(dve):
            n_own = [0]

            def own(ins):
                ins.then_inc(s("dve_own"), 1)
                n_own[0] += 1
                dve.wait_ge(s("dve_own"), n_own[0])

            def lo(n, i=None):
                if n >= len(SPLITS) or n in held:
                    return
                dve.wait_ge(s("hi_done"), along(n + 1, i, 6))
                dve.tensor_tensor(wlo[n % AHEAD][:], raw[SPLITS[n] % RAW][:], whi[n % AHEAD][:].bitcast(F32),
                                  ALU.subtract).then_inc(s("lo_done"), 1)

            def variance(k, n, times=1.0, src=None):
                dve.wait_ge(s("norm_sum"), k + 1)
                dve.tensor_scalar(var[:], src if src is not None else work[0][:, 0:T], times ** 2 / n,
                                  times ** 2 * EPS, ALU.mult, ALU.add).then_inc(s("norm_var"), 1)

            def root_done(k):
                dve.wait_ge(s("norm_std"), k + 1)
                own(dve.reciprocal(rstd[:], std[:]))

            def rest_h(p, dst=None, src_hi=None):
                for j in range(2):
                    dve.wait_ge(s("h_high"), 2 * p + j + 1)
                    c = slice(4 * j, 4 * j + 4)
                    ins = dve.tensor_tensor((dst or hlo)[:, c, :], hf[:, c, :],
                                            (src_hi or hhi)[:, c, :].bitcast(F32), ALU.subtract)
                    ins.then_inc(s("mem_ready" if dst is not None else "h_ready"), 1)

            def normalise(src, gain):
                for m in range(DC):
                    ins = dve.scalar_tensor_tensor(hf[:, m, :], src(m), gain(m), rstd[:], ALU.mult, ALU.mult)
                    if m % 4 == 3:
                        ins.then_inc(s("hf_done"), 1)

            def modulated(src, scale, shift):
                for m in range(DC):
                    ins = dve.scalar_tensor_tensor(hf[:, m, :], src(m), scale(m), rstd[:], ALU.mult, ALU.mult)
                own(ins)
                for m in range(DC):
                    ins = dve.tensor_scalar(hf[:, m, :], hf[:, m, :], shift(m), None, ALU.add)
                    if m % 4 == 3:
                        ins.then_inc(s("hf_done"), 1)

            def add_branch(gain):
                for m in range(DC):
                    ins = dve.scalar_tensor_tensor(hf[:, m, :], acc_c[:, m, :], gain(m), rstd[:], ALU.mult, ALU.mult)
                own(ins)
                dve.tensor_tensor(xT[:, :, :], xT[:, :, :], hf[:, :, :], ALU.add).then_inc(s("x_ready"), 1)

            def swiglu(stage, weighted=False):
                base = FIRST_F[stage]
                per = 3 if weighted else 2
                start = n_own[0]

                def step(r, what, f, i):
                    lo(NUMBER[r] + AHEAD, i)
                    if what != "u":
                        return
                    p = f % 2
                    mine = start + per * f

                    def chain(ins, k):
                        ins.then_inc(s("dve_own"), 1)
                        dve.wait_ge(s("dve_own"), along(mine + k, i, 2 * per))
                    dve.wait_ge(s("silu_done"), along(base + f + 1, i, 2))
                    chain(dve.tensor_tensor(pair_b[:, p, :], work[2 * p + 1][:, 0:T], pair_a[:, p, :], ALU.mult), 1)
                    if weighted:
                        cw = comb[:, f // 2, :] if i is None else comb[:, bass.ds(f // 2 + i, 1), :].rearrange("p o t -> p (o t)")
                        chain(dve.tensor_tensor(pair_b[:, p, :], pair_b[:, p, :], cw, ALU.mult), 2)
                    chain(dve.tensor_copy(ahi[:, p, :], pair_b[:, p, :]), per)
                    dve.tensor_tensor(alo[:, p, :], pair_b[:, p, :], ahi[:, p, :].bitcast(F32), ALU.subtract
                                      ).then_inc(s("act_ready"), 1)
                swiglu_steps(dve, stage, step)
                n_own[0] = start + per * LOOPED[stage]

            def x_chunk(m):
                return xT[:, m, :]

            dve.memset(zero[:], 0.0).then_inc(s("zero_ready"), 1)
            dve.wait_ge(s("params_loaded"), 16)
            dve.wait_ge(s("x_loaded"), 16)
            for n in range(AHEAD):
                lo(n)
            variance(0, D)
            root_done(0)
            normalise(x_chunk, lambda m: col("ffn1_pre", m))
            rest_h(0)
            variance(1, D, src=work[1][:, 0:T])
            root_done(1)
            normalise(lambda m: soft[:, m * T:(m + 1) * T], lambda m: col("mem_norm", m))
            rest_h(1, memlo, memhi)
            dve.wait_ge(s("consts_loaded"), 16)
            for h in range(HEADS):
                dve.wait_ge(s("bias_mm"), h + 1)
                if h == HEADS // 2:
                    dve.wait_ge(s("rows_stored"), 16)
                a = (h % 4) * BROW
                dve.tensor_tensor(soft[:, a:a + BROW], work[h % 4][:, 0:BROW], const("maskrow"), ALU.add
                                  ).then_inc(s("bias_rows"), 1)
            swiglu("ffn1")
            variance(2, D, 2.0)
            root_done(2)
            add_branch(lambda m: col("ffn1_post", m))
            for m in range(4):
                lo(NUMBER[START["memk"] + m] + AHEAD)
            variance(3, D)
            root_done(3)
            normalise(x_chunk, lambda m: col("mix_pre", m))
            for m in range(4):
                lo(NUMBER[START["memv"] + m] + AHEAD)
                if m == 1:
                    rest_h(2)
            dve.wait_ge(s("tile_evac"), EVAC[START["memv"] + 3] + 1)
            dve.memset(convin[:, :, 0:3], 0.0)
            dve.memset(scmp[:], NEG)
            dve.memset(vcmp[:], 0.0)
            dve.memset(pcmp[:], 0.0).then_inc(s("pads_ready"), 1)
            for m in range(12):
                lo(NUMBER[START["dn"] + m] + AHEAD)
                evacuated(dve, "dn", m)
                src = convin[:, m % 3, :]
                own(dve.tensor_scalar(dnc[:, m, :], src[:, 3:3 + T], col("dn_conv", 4 * m + 3), None, ALU.mult))
                for i in range(3):
                    ins = dve.scalar_tensor_tensor(dnc[:, m, :], src[:, i:i + T], col("dn_conv", 4 * m + i),
                                                   dnc[:, m, :], ALU.mult, ALU.add)
                    if i < 2:
                        own(ins)
                ins.then_inc(s("conv_done"), 1)
            for stage, count in (("z", 4), ("v", 2), ("q", 4), ("kv", 4), ("memq", 4)):
                for m in range(count):
                    lo(NUMBER[START[stage] + m] + AHEAD)
            evacuated(dve, "kv", 1)
            flat = hf[:, :, :].rearrange("p c t -> p (c t)")[:, 0:2 * 16 * 30].rearrange(
                "p (v j g c) -> p v j g c", v=2, j=16, g=GROUPS)
            for v in range(2):
                for g in range(GROUPS):
                    for jp in range(2):
                        base = kvT[DH * g:DH * g + DH, v, jp:jp + 1]
                        src = spread(base, (16, NCMP), (2, CMP_STRIDE))
                        ins = dve.tensor_copy(flat[DH * jp:DH * jp + DH, v, :, g, :], src)
            own(ins)
            for v in range(2):
                pos = spread(par(("posk", "posv")[v])[:, 0:1], (16, 2 * NCMP), (1, 0))
                out = flat[:, v, :, :, :].rearrange("p j g c -> p j (g c)")
                ins = dve.tensor_tensor(out, out, pos, ALU.add)
            ins.then_inc(s("flat_ready"), 1)
            dve.wait_ge(s("small_ready"), 1)
            own(dve.tensor_tensor(sm[:, 52:60].rearrange("p (q f) -> p q f", q=QT), small[:, :, 24:28],
                                  spread(par("dt_bias"), (QT, 4), (0, 1)), ALU.add))
            own(dve.tensor_scalar(sm[:, 216:224], sm[:, 52:60], -1.0, None, ALU.mult))
            dve.tensor_tensor(sm[:, 24:32], sm[:, 52:60], sm[:, 216:224], ALU.max).then_inc(s("dn_absz"), 1)
            dve.wait_ge(s("dn_logs"), 1)
            own(dve.scalar_tensor_tensor(sm[:, 216:224], sm[:, 52:60], 0.0, sm[:, 40:48], ALU.max, ALU.add))
            dve.scalar_tensor_tensor(sm[:, 16:24].rearrange("p (q f) -> p q f", q=QT),
                                     sm[:, 216:224].rearrange("p (q f) -> p q f", q=QT), -1.0,
                                     spread(sm[:, 48:49], (QT, 4), (0, 1)), ALU.mult, ALU.mult
                                     ).then_inc(s("dn_decay"), 1)

            def maxima(g):
                dve.wait_ge(s("sm_scores"), g + 1)
                n = 16 if g == 1 else 8
                if g == 0:
                    own(dve.tensor_reduce(sm[:, 96:104], acc_c, X_AXIS, ALU.max))
                    dve.tensor_scalar(sm[:, 64:72], sm[:, 96:104], -(128 ** -0.5), None, ALU.mult
                                      ).then_inc(s("sm_max"), 1)
                    return
                if g == 1:
                    dve.wait_ge(s("tb_loaded"), 16)
                dve.wait_ge(s("pt_mm"), 4 * g)
                if g == 1:
                    for br in range(2):
                        a = slice(br * HEADS * P, (br + 1) * HEADS * P)
                        ins = dve.scalar_tensor_tensor(soft[:, a].rearrange("p (h k) -> p h k", k=P),
                                                       acc[:, a].rearrange("p (h k) -> p h k", k=P), DH ** -0.5,
                                                       tb[:, :, P:T], ALU.mult, ALU.add)
                        ins.then_inc(s("sm_bias"), 1)
                else:
                    dve.scalar_tensor_tensor(soft[:, :], acc[:, :], DH ** -0.5,
                                             tb[:, :, :].rearrange("p h t -> p (h t)"), ALU.mult, ALU.add
                                             ).then_inc(s("sm_bias"), 1)
                dve.wait_ge(s("sm_bias"), g + 1)
                dve.tensor_reduce(sm[:, 64:64 + n], soft[:, :].rearrange("p (u k) -> p u k", u=n), X_AXIS, ALU.max,
                                  negate=True).then_inc(s("sm_max"), 1)

            def probs(g, gate):
                dve.wait_ge(s("sm_exp"), g + 1)
                n = 16 if g == 1 else 8
                own(dve.reciprocal(sm[:, 96:96 + n], sm[:, 80:80 + n]))
                if gate is not None:
                    own(dve.tensor_tensor(sm[:, 96:96 + n], sm[:, 96:96 + n], gate, ALU.mult))
                for j in range(2):
                    a = soft[:, j * 1024:(j + 1) * 1024].rearrange("p (u k) -> p u k", u=n // 2)
                    r = spread(sm[:, 96 + j * n // 2:97 + j * n // 2], (n // 2, DC * T // n), (1, 0))
                    dve.tensor_tensor(a, a, r, ALU.mult).then_inc(s("sm_probs"), 1)

            def o_low(b, k):
                for j in range(2):
                    dve.wait_ge(s("o_high"), k + j + 1)
                    dve.tensor_tensor(olo[:, b, 2 * j:2 * j + 2, :].rearrange("p c t -> p (c t)"), work[2 + j][:, :],
                                      ohi[:, b, 2 * j:2 * j + 2, :].rearrange("p c t -> p (c t)").bitcast(F32),
                                      ALU.subtract).then_inc(s("olo_ready"), 1)

            maxima(0)
            probs(0, None)
            o_low(2, 0)
            dve.wait_ge(s("tb_loaded"), 16)
            dve.wait_ge(s("cmp_scores"), 1)
            for q in range(QT):
                for g in range(GROUPS):
                    n, at = (NCMP0, P + 31) if q == 0 else (NCMP, 31)
                    u = q * HEADS + g * HPG
                    cs = acc[:, g * 512 + q * 64:g * 512 + (q + 1) * 64].rearrange("p (j c) -> p j c", c=16)
                    dve.scalar_tensor_tensor(scmp[:, u:u + HPG, 0:n], cs[:, :, 0:n], DH ** -0.5,
                                             spread(tb[:, g * HPG, at:at + 1], (HPG, n), (T, CMP_STRIDE)),
                                             ALU.mult, ALU.add).then_inc(s("cmp_bias"), 1)
            dve.wait_ge(s("cmp_bias"), 4)
            dve.tensor_reduce(sm[:, 112:128], scmp[:], X_AXIS, ALU.max).then_inc(s("cmp_bias"), 1)
            dve.wait_ge(s("cmp_bias"), 5)
            dve.tensor_tensor(scmp[:], scmp[:], spread(sm[:, 112:113], (16, 16), (1, 0)), ALU.subtract
                              ).then_inc(s("cmp_centred"), 1)
            dve.wait_ge(s("cmp_exp"), 1)
            own(dve.tensor_reduce(sm[:, 224:240], scmp[:], X_AXIS, ALU.add))
            own(dve.reciprocal(sm[:, 112:128], sm[:, 224:240]))
            dve.wait_ge(s("nsa_gates"), 1)
            gv = sm[:, 128:176].rearrange("p (q f) -> p q f", q=QT)
            r16 = sm[:, 112:128].rearrange("p (q h) -> p q h", q=QT)
            own(dve.tensor_tensor(r16, r16, gv[:, :, 0:HEADS], ALU.mult))
            own(dve.tensor_tensor(r16, r16, spread(const("has_block")[:, 0:1], (QT, HEADS), (1, 0)), ALU.mult))
            dve.tensor_tensor(pcmp[:, :, :, 0:16].rearrange("p a j c -> p (a j) c"), scmp[:],
                              spread(sm[:, 112:113], (16, 16), (1, 0)), ALU.mult).then_inc(s("cmp_probs"), 1)
            maxima(1)
            probs(1, gv[:, 0, 8:24])
            maxima(2)
            probs(2, gv[:, 1, 8:16])
            maxima(3)
            probs(3, gv[:, 1, 16:24])
            o_low(0, 2)

            dve.wait_ge(s("dn_sums"), 1)
            flat_hf = hf[:, :, :].rearrange("p c t -> p (c t)")
            dve.tensor_scalar(flat_hf, acc[:, :], EPS, None, ALU.add).then_inc(s("dn_var"), 1)
            dve.wait_ge(s("dn_root"), 1)
            own(dve.reciprocal(flat_hf, flat_hf))
            dqk = dnc[:, 0:8, :].rearrange("p c t -> p (c t)")
            dve.tensor_tensor(dqk, dqk, flat_hf, ALU.mult).then_inc(s("dn_unit"), 1)
            dve.wait_ge(s("dn_gc_mm"), 1)
            dve.tensor_copy(sm[:, 0:16], work[0][:, 0:16]).then_inc(s("dn_gc"), 1)
            dve.wait_ge(s("dn_gc"), 1)
            dve.tensor_tensor(sm[:, 208:216], sm[:, 8:16], sm[:, 0:8], ALU.subtract).then_inc(s("dn_rest"), 1)
            dve.wait_ge(s("dn_rows_mm"), 1)
            for dst, op in ((dn_el, ALU.max), (dn_eu, ALU.min)):
                for u in range(8):
                    ins = dve.tensor_scalar(dst[:, u * P:(u + 1) * P], work[2 + u // 4][:, (u % 4) * P:(u % 4 + 1) * P],
                                            sm[:, u:u + 1], 0.0, ALU.subtract, op)
                ins.then_inc(s("dn_diff"), 1)
            idn = spread(ident[:, 0:1], (8, P), (0, 1))
            dve.tensor_copy(dn_inv[:, :].rearrange("p (u k) -> p u k", k=P), idn)
            dve.tensor_copy(dn_invT[:, :].rearrange("p (u k) -> p u k", k=P), idn).then_inc(s("dn_ident"), 1)
            dve.wait_ge(s("dn_exp"), 2)
            dve.wait_ge(s("dn_beta"), 1)
            dve.tensor_tensor(sm[:, 216:224], sm[:, 184:192], sm[:, 192:200], ALU.mult).then_inc(s("dn_scales"), 1)
            dve.wait_ge(s("dn_decays"), 2)
            dve.wait_ge(s("dn_kq_mm"), 1)
            for u in range(8):
                a = slice(u * P, (u + 1) * P)
                ins = dve.scalar_tensor_tensor(dn_a[:, a], acc[:, a], sm[:, 184 + u:185 + u], dn_el[:, a],
                                               ALU.mult, ALU.mult)
            ins.then_inc(s("dn_kq"), 1)
            dve.scalar_tensor_tensor(dn_qk[:, :], acc[:, 8 * P:16 * P], P ** -0.5, dn_eu[:, :], ALU.mult, ALU.mult
                                     ).then_inc(s("dn_kq"), 1)
            dve.wait_ge(s("dn_kq"), 2)
            qk3 = dn_qk[:, :].rearrange("p (u k) -> p u k", k=P)
            own(dve.tensor_tensor(qk3, qk3, spread(upper[:, 0:1], (8, P), (0, 1)), ALU.mult))
            dve.wait_ge(s("dn_eg"), 1)
            own(dve.scalar_tensor_tensor(dn_qd[:, :].rearrange("p (h t) -> p h t", t=P),
                                         dn_qd[:, :].rearrange("p (h t) -> p h t", t=P), P ** -0.5,
                                         dnc[:, 0:4, P:T], ALU.mult, ALU.mult))
            dve.wait_ge(s("dn_tok_mm"), 1)
            for u in range(8):
                ins = dve.tensor_scalar(dn_kb[:, u * P:(u + 1) * P], acc[:, u * P:(u + 1) * P],
                                        sm[:, 216 + u:217 + u], None, ALU.mult)
            ins.then_inc(s("dn_tok"), 1)
            for u in range(4):
                ins = dve.tensor_scalar(dn_kd[:, u * P:(u + 1) * P], acc[:, u * P:(u + 1) * P],
                                        sm[:, 200 + u:201 + u], None, ALU.mult)
            ins.then_inc(s("dn_tok"), 1)
            dve.wait_ge(s("dn_vtok"), 1)
            dve.nop().then_inc(s("dn_tok"), 1)
            for lv in range(LEVELS):
                mask = spread(const("levels")[:, lv * P:lv * P + 1], (8, P), (0, 1))
                dve.wait_ge(s("dn_kq"), 2)
                if lv == 0:
                    dve.wait_ge(s("dn_ident"), 1)
                dve.tensor_tensor(dn_b[:, :].rearrange("p (u k) -> p u k", k=P),
                                  dn_a[:, :].rearrange("p (u k) -> p u k", k=P), mask, ALU.mult
                                  ).then_inc(s("dn_level"), 1)
                dve.wait_ge(s("dn_x_mm"), lv + 1)
                dve.tensor_tensor(dn_inv[:, :], dn_inv[:, :], acc[:, 8 * P:16 * P], ALU.subtract
                                  ).then_inc(s("dn_update"), 1)
                for j in range(2):
                    a = slice(j * 512, (j + 1) * 512)
                    ins = dve.tensor_tensor(dn_invT[:, a], dn_invT[:, a], work[2 + j][:, :], ALU.subtract)
                ins.then_inc(s("dn_update"), 1)
                dve.wait_ge(s("dn_update"), 2 * lv + 2)
            dve.wait_ge(s("dn_osum"), 1)
            dve.tensor_scalar(flat_hf[:, 4 * T:8 * T], acc[:, 4 * T:8 * T], 1.0 / P, EPS, ALU.mult, ALU.add
                              ).then_inc(s("dn_ovar"), 1)
            dve.wait_ge(s("dn_oroot"), 1)
            own(dve.reciprocal(flat_hf[:, 4 * T:8 * T], flat_hf[:, 4 * T:8 * T]))
            own(dve.scalar_tensor_tensor(flat_hf[:, 0:4 * T], acc[:, 0:4 * T], col("dn_norm", 0),
                                         flat_hf[:, 4 * T:8 * T], ALU.mult, ALU.mult))
            dve.wait_ge(s("z_silu"), 1)
            own(dve.tensor_tensor(flat_hf[:, 0:4 * T], flat_hf[:, 0:4 * T],
                                  zT[:, :, :].rearrange("p c t -> p (c t)"), ALU.mult))
            own(dve.tensor_copy(ohi[:, 1, :, :].rearrange("p c t -> p (c t)"), flat_hf[:, 0:4 * T]))
            dve.tensor_tensor(olo[:, 1, :, :].rearrange("p c t -> p (c t)"), flat_hf[:, 0:4 * T],
                              ohi[:, 1, :, :].rearrange("p c t -> p (c t)").bitcast(F32), ALU.subtract
                              ).then_inc(s("olo_ready"), 1)
            dve.wait_ge(s("olo_ready"), 5)
            dve.nop().then_inc(s("olo_ready"), 1)
            dve.nop().then_inc(s("dn_out"), 1)
            dve.nop().then_inc(s("dn_o_scaled"), 1)

            dve.wait_ge(s("pe_tile"), START["gate"])
            for l in range(LAYERS):
                ins = dve.tensor_tensor(mod[:, l * 48:(l + 1) * 48], work[1][:, l * 48:(l + 1) * 48],
                                        par(f"b_ada{l}"), ALU.add)
            ins.then_inc(s("mod_ready"), 1)
            dve.wait_ge(s("mod_ready"), 1)
            for l in range(LAYERS):
                for j, name in enumerate(("norm", "ffn_norm")):
                    a = l * 48 + (1, 4)[j] * DC
                    ins = dve.scalar_tensor_tensor(gscale[:, (2 * l + j) * DC:(2 * l + j + 1) * DC], mod[:, a:a + DC],
                                                   1.0, par(f"{name}{l}"), ALU.add, ALU.mult)
            own(ins)

            def mod_col(l, part, m):
                a = l * 48 + part * DC + m
                return mod[:, a:a + 1]

            def gs_col(l, j, m):
                a = (2 * l + j) * DC + m
                return gscale[:, a:a + 1]

            first = sorted(held)
            held.clear()
            for n in first:
                lo(n)
            held.update(first)
            for m in range(24):
                lo(NUMBER[START["gate"] + m] + AHEAD)
            for n in range(12):
                r = START["branch"] + n
                m, b = STREAM[r][1]
                lo(NUMBER[r] + AHEAD)
                dve.wait_ge(s("pe_tile"), r + 1)
                evacuated(dve, "gate", 23)
                g = gates[:, b * DC + 2 * m:b * DC + 2 * m + 2, :].rearrange("p c t -> p (c t)")
                out = hf[:, 2 * m:2 * m + 2, :].rearrange("p c t -> p (c t)")
                if b == 0:
                    dve.tensor_tensor(out, work[n % 4][:, :], g, ALU.mult).then_inc(s("branch_read"), 1)
                    dve.wait_ge(s("branch_read"), n + 1)
                    continue
                dve.tensor_tensor(g, work[n % 4][:, :], g, ALU.mult).then_inc(s("branch_read"), 1)
                dve.wait_ge(s("branch_read"), n + 1)
                ins = dve.tensor_tensor(out, out, g, ALU.add)
                if b == 1:
                    own(ins)
                    continue
                ins.then_inc(s("merged"), 1)
                dve.wait_ge(s("merged_high"), m + 1)
                dve.tensor_tensor(hlo[:, 2 * m:2 * m + 2, :], hf[:, 2 * m:2 * m + 2, :],
                                  hhi[:, 2 * m:2 * m + 2, :].bitcast(F32), ALU.subtract).then_inc(s("merged_ready"), 1)
            for m in range(DC):
                lo(NUMBER[START["wout"] + m] + AHEAD)
            variance(4, D)
            root_done(4)
            add_branch(lambda m: col("mix_post", m))
            variance(5, D)
            root_done(5)
            normalise(x_chunk, lambda m: col("ffn2_pre", m))
            rest_h(3)
            swiglu("ffn2")
            variance(6, D, 2.0)
            root_done(6)
            add_branch(lambda m: col("ffn2_post", m))

            dve.memset(vpad[:, :, 0:30], 0.0)
            own(dve.memset(ppad[:, :, 0:16], 0.0))
            for l in range(LAYERS):
                k = 7 + 3 * l
                variance(k, D)
                root_done(k)
                modulated(x_chunk, lambda m: gs_col(l, 0, m), lambda m: mod_col(l, 0, m))
                rest_h(4 + 2 * l)
                taps = []

                def tap_ops(c):
                    def tap(i):
                        def run():
                            w = col(f"conv_w{l}", c * CONV_K + i)
                            if i == 0:
                                own(dve.tensor_scalar(yconv[:, c, :], vpad[:, c, 0:T], w, col(f"conv_b{l}", c),
                                                      ALU.mult, ALU.add))
                            else:
                                own(dve.scalar_tensor_tensor(yconv[:, c, :], vpad[:, c, i:i + T], w, yconv[:, c, :],
                                                             ALU.mult, ALU.add))
                        return run
                    return [tap(i) for i in range(CONV_K)]

                def some_taps(n):
                    for _ in range(min(n, len(taps))):
                        taps.pop(0)()

                for m in range(8):
                    lo(NUMBER[START[f"a{l}"] + m] + AHEAD)
                    if m % 2:
                        c = m // 2
                        evacuated(dve, f"a{l}", m)
                        dve.tensor_tensor(vpad[:, c, 30:30 + T], pair_a[:, c % 2, :], pair_b[:, c % 2, :], ALU.mult
                                          ).then_inc(s("glu_done"), 1)
                        dve.wait_ge(s("glu_done"), 4 * l + c + 1)
                        taps += tap_ops(c)
                    some_taps(4)
                for m in range(4):
                    lo(NUMBER[START[f"p{l}"] + m] + AHEAD)
                    some_taps(5)
                evacuated(dve, f"p{l}", 3)
                for g, w in enumerate(WINDOWS):
                    src, reach = ppad[:, g, :], 1
                    bufs = [flat_hf[:, 0:16 + T], flat_hf[:, 512:528 + T]]
                    while reach < w:
                        a = 2 * reach - 1
                        dst = bufs.pop(0)
                        bufs.append(dst)
                        own(dve.tensor_tensor(dst[:, a:16 + T], src[:, a:16 + T], src[:, a - reach:16 + T - reach],
                                              ALU.add))
                        src, reach = dst, 2 * reach
                    mean = flat_hf[:, 1024:1024 + T]
                    own(dve.tensor_scalar(mean, src[:, 16:16 + T], 1.0 / w, None, ALU.mult))
                    own(dve.tensor_tensor(mean[:, 0:16], src[:, 16:32], const("inv_count")[:, 16 * g:16 * g + 16], ALU.mult))
                    own(dve.tensor_tensor(mean, mean, ppad[:, g, 16:16 + T], ALU.subtract))
                    own(dve.tensor_copy(phi[:, g, :], mean))
                    ins = dve.tensor_tensor(plo[:, g, :], mean, phi[:, g, :].bitcast(F32), ALU.subtract)
                    if g < 3:
                        own(ins)
                ins.then_inc(s("pooled"), 1)
                for m in range(16):
                    lo(NUMBER[START[f"G{l}"] + m] + AHEAD)
                    some_taps(6)
                some_taps(len(taps))
                dve.nop().then_inc(s("conv_done2"), 1)
                lo(NUMBER[START[f"pool{l}"]] + AHEAD)
                dve.wait_ge(s("ln_mean"), l + 1)
                dve.scalar_tensor_tensor(yconv[:], spread(work[0][:, 0:1], (4, T), (0, 1)), -1.0 / 512, yconv[:],
                                         ALU.mult, ALU.add).then_inc(s("ln_centred"), 1)
                variance(k + 1, 512, src=work[1][:, 0:T])
                root_done(k + 1)
                dve.tensor_tensor(yconv[:], yconv[:], spread(rstd[:, 0:1], (4, T), (0, 1)), ALU.mult
                                  ).then_inc(s("ln_scaled"), 1)
                dve.wait_ge(s("pe_tile"), START[f"pool{l}"] + 1)
                evacuated(dve, f"G{l}", 15)
                for m in range(DC):
                    ins = dve.scalar_tensor_tensor(hf[:, m, :], acc_c[:, m, :], col(f"pool_scale{l}", m),
                                                   gate2[:, DC + m, :], ALU.mult, ALU.mult)
                ins.then_inc(s("pool_read"), 1)
                dve.wait_ge(s("y_high"), l + 1)
                dve.tensor_tensor(ylo[:], yconv[:], yhi[:].bitcast(F32), ALU.subtract).then_inc(s("y_ready"), 1)
                for m in range(4):
                    lo(NUMBER[START[f"conv{l}"] + m] + AHEAD)
                    dve.wait_ge(s("pe_tile"), START[f"conv{l}"] + m + 1)
                    for j in range(2):
                        c = 2 * m + j
                        ins = dve.scalar_tensor_tensor(gate2[:, c, :], work[m][:, j * T:(j + 1) * T],
                                                       col(f"b_out{l}", c), gate2[:, c, :], ALU.add, ALU.mult)
                    ins.then_inc(s("conv_read"), 1)
                    dve.wait_ge(s("conv_read"), 4 * l + m + 1)
                    c = slice(2 * m, 2 * m + 2)
                    dve.tensor_tensor(hf[:, c, :], hf[:, c, :], gate2[:, c, :], ALU.add).then_inc(s("mixed"), 1)
                    dve.wait_ge(s("mixed_high"), 4 * l + m + 1)
                    dve.tensor_tensor(hlo[:, c, :], hf[:, c, :], hhi[:, c, :].bitcast(F32), ALU.subtract
                                      ).then_inc(s("mixed_ready"), 1)
                for m in range(DC):
                    lo(NUMBER[START[f"wout{l}"] + m] + AHEAD)
                dve.wait_ge(s("pe_tile"), START[f"wout{l}"] + DC)
                for m in range(DC):
                    ins = dve.scalar_tensor_tensor(xT[:, m, :], acc_c[:, m, :], mod_col(l, 2, m), xT[:, m, :],
                                                   ALU.mult, ALU.add)
                ins.then_inc(s("x_ready"), 1)
                variance(k + 2, D)
                root_done(k + 2)
                modulated(x_chunk, lambda m: gs_col(l, 1, m), lambda m: mod_col(l, 3, m))
                rest_h(5 + 2 * l)

                def v3(a, n, w=QT):
                    return rt[:, a:a + w * n].rearrange("p (q f) -> p q f", q=w)
                rl = v3(0, 36)
                dve.wait_ge(s("router_mm"), l + 1)
                dve.tensor_tensor(rl, work[1][:, 0:72].rearrange("p (q f) -> p q f", q=QT),
                                  spread(par(f"router_b{l}"), (QT, 36), (0, 1)), ALU.add).then_inc(s("router_read"), 1)
                dve.wait_ge(s("router_read"), l + 1)

                def first_max(out, scores, top, iota, n, eq, at):
                    own(dve.tensor_tensor(v3(eq, n), scores, spread(top, (QT, n), (1, 0)), ALU.is_equal))
                    own(dve.tensor_tensor(v3(eq, n), v3(eq, n), spread(iota[:, 0:1], (QT, n), (0, 1)), ALU.mult))
                    own(dve.tensor_reduce(rt[:, at:at + QT], v3(eq, n), X_AXIS, ALU.min))
                    own(dve.tensor_tensor(v3(out, n), spread(iota[:, 0:1], (QT, n), (0, 1)),
                                          spread(rt[:, at:at + 1], (QT, n), (1, 0)), ALU.is_equal))

                own(dve.tensor_reduce(rt[:, 72:74], rl[:, :, 0:4], X_AXIS, ALU.max))
                dve.tensor_tensor(v3(80, 4), rl[:, :, 0:4], spread(rt[:, 72:73], (QT, 4), (1, 0)), ALU.subtract
                                  ).then_inc(s("router_centred"), 1)
                first_max(88, rl[:, :, 0:4], rt[:, 72:73], const("iota4"), 4, 96, 74)
                for q in range(QT):
                    el = rt[:, q * 36 + 4:q * 36 + 36].rearrange("p (g e) -> p g e", e=EPG)
                    ins = dve.tensor_tensor(rt[:, 320 + 32 * q:352 + 32 * q].rearrange("p (g e) -> p g e", e=EPG), el,
                                            spread(rt[:, 88 + 4 * q:89 + 4 * q], (EGROUPS, EPG), (1, 0)), ALU.mult)
                own(ins)
                for q in range(QT):
                    ins = dve.tensor_reduce(rt[:, 104 + 8 * q:112 + 8 * q],
                                            spread(rt[:, 320 + 32 * q:321 + 32 * q], (EPG, EGROUPS), (1, EPG)),
                                            X_AXIS, ALU.add)
                own(ins)
                ig = v3(104, 8)
                own(dve.tensor_reduce(rt[:, 142:144], ig, X_AXIS, ALU.max))
                first_max(120, ig, rt[:, 142:143], const("iota8"), 8, 160, 76)
                own(dve.scalar_tensor_tensor(rt[:, 176:192], rt[:, 120:136], NEG, rt[:, 104:120], ALU.mult, ALU.add))
                own(dve.tensor_reduce(rt[:, 144:146], v3(176, 8), X_AXIS, ALU.max))
                dve.tensor_tensor(rt[:, 146:148], rt[:, 144:146], rt[:, 142:144], ALU.subtract
                                  ).then_inc(s("router_centred"), 1)
                first_max(192, v3(176, 8), rt[:, 144:145], const("iota8"), 8, 160, 78)
                dve.wait_ge(s("router_exp"), 2 * l + 2)
                own(dve.tensor_reduce(rt[:, 150:152], v3(80, 4), X_AXIS, ALU.add))
                own(dve.scalar_tensor_tensor(rt[:, 152:154], rt[:, 148:150], 1.0, rt[:, 150:152], ALU.add, ALU.mult))
                own(dve.reciprocal(rt[:, 154:156], rt[:, 152:154]))
                own(dve.tensor_tensor(v3(192, 8), v3(192, 8), spread(rt[:, 148:149], (QT, 8), (1, 0)), ALU.mult))
                own(dve.tensor_tensor(rt[:, 120:136], rt[:, 120:136], rt[:, 192:208], ALU.add))
                own(dve.tensor_tensor(v3(120, 8), v3(120, 8), spread(rt[:, 154:155], (QT, 8), (1, 0)), ALU.mult))
                for q in range(QT):
                    ins = dve.tensor_tensor(rt[:, 256 + 32 * q:288 + 32 * q].rearrange("p (g e) -> p g e", e=EPG),
                                            spread(rt[:, 88 + 4 * q:89 + 4 * q], (EGROUPS, EPG), (1, 0)),
                                            spread(rt[:, 120 + 8 * q:121 + 8 * q], (EGROUPS, EPG), (0, 1)), ALU.mult)
                ins.then_inc(s("combine_ready"), 1)
                dve.wait_ge(s("comb_ready"), 16 * (l + 1))
                swiglu(f"moe{l}", weighted=True)
                dve.wait_ge(s("pe_tile"), START[f"moe{l}"] + 3 * LOOPED[f"moe{l}"])
                for m in range(DC):
                    ins = dve.scalar_tensor_tensor(xT[:, m, :], acc_c[:, m, :], mod_col(l, 5, m), xT[:, m, :],
                                                   ALU.mult, ALU.add)
                ins.then_inc(s("x_ready"), 1)
            k = 7 + 3 * LAYERS
            variance(k, D)
            root_done(k)
            for m in range(DC):
                ins = dve.scalar_tensor_tensor(hf[:, m, :], xT[:, m, :], col("final", m), rstd[:], ALU.mult, ALU.mult)
            ins.then_inc(s("final_ready"), 1)


def features(v):
    return np.ascontiguousarray(np.reshape(v, (-1, P)).T)


def rel_bucket(dist):
    d = np.maximum(dist, 1).astype(np.float32)
    exact = BUCKETS // 2
    log = exact + (np.log(d / np.float32(exact)) / np.float32(np.log(MAX_DIST / exact))
                   * np.float32(BUCKETS - exact)).astype(np.int32)
    return np.where(dist < exact, dist, np.minimum(log, BUCKETS - 1))


def host_consts():
    out = np.zeros((P, NCONST), np.float32)

    def put(name, a):
        a = np.asarray(a, np.float32)
        out[:a.shape[0], CONST[name][0]:CONST[name][1]] = a
    i, j = np.arange(P)[:, None], np.arange(P)[None, :]
    put("ident", i == j)
    put("ones", np.ones((P, P)))
    put("upper", i <= j)
    put("levels", np.concatenate([(i // (2 << n) == j // (2 << n)) & (i >> n & 1 == 1) & (j >> n & 1 == 0)
                                  for n in range(LEVELS)], axis=1))
    dist = (T - 1) - np.arange(BROW)
    put("onehot", (rel_bucket(np.maximum(dist, 0))[None, :] == np.arange(BUCKETS)[:, None]) & (dist >= 0)[None, :])
    put("maskrow", np.broadcast_to(np.where(dist < 0, NEG, 0.0), (P, BROW)))
    put("has_block", (np.arange(P)[:, None] + P * np.arange(QT)[None, :]) >= CMP_BLOCK - 1)
    put("iota4", np.broadcast_to(np.arange(4) - 4, (P, 4)))
    put("iota8", np.broadcast_to(np.arange(8) - 8, (P, 8)))
    put("inv_count", np.broadcast_to(np.concatenate([1.0 / np.minimum(np.arange(1, 17), w) for w in WINDOWS]), (P, 64)))
    return out


def host_params(a):
    out = np.zeros((P, NPARAM), np.float32)

    def put(name, v):
        lo, hi = PARAM[name]
        v = np.asarray(v).reshape(v.shape[0], -1)
        out[:v.shape[0], lo:hi] = v

    def wide(v):
        return np.broadcast_to(v, (P, v.shape[-1]))
    for name, key in (("ffn1_pre", "ffn1_pre_norm"), ("ffn1_post", "ffn1_post_norm"), ("mix_pre", "mix_pre_norm"),
                      ("mix_post", "mix_post_norm"), ("ffn2_pre", "ffn2_pre_norm"), ("ffn2_post", "ffn2_post_norm"),
                      ("mem_norm", "mem_norm"), ("final", "final_norm_g_2"), ("c", "c_2"), ("dn_norm", "dn_out_norm")):
        put(name, features(a[key]))
    put("dn_conv", a["dn_conv_w"][0].reshape(4, 12, P).transpose(2, 1, 0))
    put("a_log", wide(a["dn_a_log"][0]))
    put("dt_bias", wide(a["dn_dt_bias"][0]))
    w = a["w_in"][0]
    cols = np.concatenate([w[:, 1280:1304], w[:, 2840:2844], w[:, 2844:2848]], axis=1)
    put("w_small", cols.reshape(DC, P, 32).transpose(1, 0, 2))
    put("w2k", a["cmp_k_w2"][0].reshape(2, P, DH).transpose(1, 0, 2))
    put("w2v", a["cmp_v_w2"][0].reshape(2, P, DH).transpose(1, 0, 2))
    for name, key in (("posk", "cmp_pos_k"), ("posv", "cmp_pos_v")):
        put(name, a[key][0].reshape(16, 2 * DH).T)
    put("rel", a["rel_bias"])
    for l in range(LAYERS):
        put(f"norm{l}", features(a["mixer_norm_g_2"][l]))
        put(f"b_ada{l}", features(a["b_ada_2"][l]))
        put(f"conv_w{l}", a["conv_w_2"][l].reshape(CONV_K, 4, P).transpose(2, 1, 0))
        for name, key in (("conv_b", "conv_b_2"), ("ln_g", "conv_ln_g_2"), ("ln_b", "conv_ln_b_2"),
                          ("b_out", "b_conv_out_2"), ("pool_scale", "pool_scale_2"), ("ffn_norm", "ffn_norm_g_2")):
            put(f"{name}{l}", features(a[key][l]))
        r = np.concatenate([a["w_router_group_2"][l], a["w_router_expert_2"][l]], axis=1)
        put(f"router{l}", r.reshape(DC, P, 36).transpose(1, 0, 2))
        put(f"router_b{l}", wide(np.concatenate([a["b_router_group_2"][l], a["b_router_expert_2"][l]])))
    return out


def host_stream(a):
    out = np.empty((len(STREAM), P, TILE), np.float32)

    def cols(w, at, n=P):
        return w[:, at:at + n].reshape(-1, P, n).transpose(1, 0, 2).reshape(P, -1)
    w_in = a["w_in"][0]
    head = np.arange(DH)
    pair = [np.concatenate([j * DH + head, (j + HPG) * DH + head]) for j in range(HPG)]
    kv = HEADS * DH
    dn_at = kv + 6 * P + 24
    z_at = dn_at + 1536 + 8
    nsa_rows = np.concatenate(pair)
    branch = [a["w_branch_nsa"][0][nsa_rows], a["w_branch_dn"][0], a["w_branch_mem"][0]]
    w1 = [a[n][0].reshape(16, P, CMP_HIDDEN) for n in ("cmp_k_w1", "cmp_v_w1")]
    for r, (stage, m, _) in enumerate(STREAM):
        l = int(stage[-1]) if stage[-1] in "01" and stage not in ("ffn1", "w1") else 0
        name = stage.rstrip("01") if stage not in ("ffn1", "w1") else stage
        if name in ("ffn1", "ffn2", "moe"):
            what, f = m
            if name == "moe":
                e, c = f // 2, f % 2
                g, u, d = (a[f"w_expert_{n}_2"][l, e] for n in ("gate", "up", "down"))
            else:
                c = f
                g, u, d = (a[f"{name}_w_{n}"][0] for n in ("gate", "up", "down"))
            tile = {"g": g, "u": u}[what] if what != "d" else d
            out[r] = cols(tile, c * P) if what != "d" else tile[c * P:(c + 1) * P]
        elif name == "memk":
            out[r] = cols(a["w_mem_kv"][0], m * P)
        elif name == "memv":
            out[r] = cols(a["w_mem_kv"][0], 512 + m * P)
        elif name == "dn":
            out[r] = cols(w_in, dn_at + m * P)
        elif name == "z":
            out[r] = cols(w_in, z_at + m * P)
        elif name == "v":
            out[r] = cols(w_in, kv + (3, 5)[m] * P)
        elif name == "q":
            out[r] = cols(w_in[:, pair[m]], 0)
        elif name == "kv":
            out[r] = cols(w_in, kv + (0, 1, 2, 4)[m] * P)
        elif name == "memq":
            out[r] = cols(w_in, z_at + 512 + m * P)
        elif name == "w1":
            out[r] = w1[m // 4][4 * (m % 4):4 * (m % 4) + 4].transpose(1, 0, 2).reshape(P, -1)
        elif name == "ada":
            out[r] = cols(a["w_ada_2"][m // 48], (m % 48) * P)
        elif name == "gate":
            out[r] = cols(a["w_branch_gate"][0], m * P)
        elif name == "branch":
            out[r] = cols(branch[m[1]], m[0] * T, T)
        elif stage == "wout":
            out[r] = cols(a["w_out"][0], m * P)
        elif name == "wout":
            out[r] = cols(a["w_out_2"][l], m * P)
        elif name == "a":
            out[r] = cols(a["w_in_2"][l], (m // 2) * P + 512 * (m % 2))
        elif name == "p":
            out[r] = cols(a["w_in_2"][l], 1024 + m * P)
        elif name == "G":
            out[r] = cols(a["w_in_2"][l], 1536 + m * P)
        elif name == "pool":
            out[r] = a["pool_w_2"][l].transpose(1, 0, 2).reshape(P, -1)
        elif name == "conv":
            out[r] = cols(a["w_conv_out_2"][l], m * T, T)
        else:
            raise ValueError(stage)
    return out


def kernel(**inputs):
    import concourse.bacc as bacc
    from concourse.bass_utils import run_bass_kernel_spmd

    a = {k: np.asarray(v) for k, v in inputs.items()}

    def token_last(v):
        return np.ascontiguousarray(v[0].reshape(T, DC, P).transpose(2, 1, 0))
    arrays = {"wstream_d": host_stream(a), "consts_d": host_consts(), "params_d": host_params(a),
              "x_d": token_last(a["x"]), "mem_d": token_last(a["mem"])}
    nc = bacc.Bacc("TRN2", target_bir_lowering=False, num_devices=1)
    args = [nc.dram_tensor(n, v.shape, F32, kind="ExternalInput").ap() for n, v in arrays.items()]
    rows = nc.dram_tensor("bias_rows_d", (HEADS, P, BROW), F32, kind="Internal").ap()
    out = nc.dram_tensor("out_d", (P, DC, T), F32, kind="ExternalOutput").ap()
    program(nc, *args, rows, out)
    r = run_bass_kernel_spmd(nc, [arrays], core_ids=[0])
    got = r.results[0]["out_d"]
    return np.ascontiguousarray(got.transpose(2, 1, 0)).reshape(1, T, D)
```

```python
from contextlib import ExitStack

import numpy as np

import concourse.bass as bass
from concourse import mybir
from concourse.alu_op_type import AluOpType as ALU

F32 = mybir.dt.float32
F32R = mybir.dt.float32r
BF16 = mybir.dt.bfloat16
ACT = mybir.ActivationFunctionType
X_AXIS = mybir.AxisListType.X

P = 128
T = 256
QT = T // P
D = 1024
DC = D // P
FF = 2816
FC = FF // P
EPS = 1e-6
TILE = 1024
RAW = 6
AHEAD = 3
NEG = -1e30

HEADS, GROUPS, HPG, DH = 8, 2, 4, 64
CMP_BLOCK, CMP_STRIDE, CMP_HIDDEN = 32, 16, 256
NCMP = T // CMP_STRIDE - 1
NCMP0 = 7
BUCKETS, MAX_DIST = 32, 128
BROW = 384
DNH = 4
LEVELS = 7
LAYERS = 2
EXPERTS, EGROUPS, EPG, EH = 32, 4, 8, 256
PAIRS = EXPERTS // 2
SLOTS = P // 2
CAPACITY = SLOTS
CONV_K = 31
WINDOWS = (2, 4, 8, 16)
IN_W = 3864


def columns(widths):
    out, at = {}, 0
    for name, n in widths:
        out[name] = (at, at + n)
        at += n
    return out, at


CONST_W = [("ident", P), ("ones", P), ("upper", P), ("levels", LEVELS * P),
           ("onehot", BROW), ("maskrow", BROW), ("has_block", QT), ("iota4", 4), ("iota8", 8),
           ("inv_count", len(WINDOWS) * 16), ("slots", 64)]
CONST, NCONST = columns(CONST_W)
LAYER_W = [("norm", DC), ("b_ada", 48), ("conv_w", 4 * CONV_K), ("conv_b", 4), ("ln_g", 4), ("ln_b", 4),
           ("b_out", DC), ("pool_scale", DC), ("ffn_norm", DC), ("router", DC * 36), ("router_b", 36)]
PARAM_W = [("ffn1_pre", DC), ("ffn1_post", DC), ("mix_pre", DC), ("mix_post", DC), ("ffn2_pre", DC),
           ("ffn2_post", DC), ("mem_norm", DC), ("final", DC), ("dn_conv", 48), ("dn_norm", 1),
           ("a_log", DNH), ("dt_bias", DNH), ("w_small", DC * 32), ("w2k", 2 * DH), ("w2v", 2 * DH),
           ("posk", 16), ("posv", 16), ("rel", HEADS), ("c", DC)]
PARAM_W += [(f"{n}{l}", w) for l in range(LAYERS) for n, w in LAYER_W]
PARAM, NPARAM = columns(PARAM_W)


def swiglu_order(n):
    out = [("g", 0), ("u", 0)]
    for f in range(1, n):
        out += [("g", f), ("u", f), ("d", f - 1)]
    return out + [("d", n - 1)]


def moe_order():
    def some(what, p):
        return [(what, p, k) for k in range(8 if what == "gu" else 4)]
    out = some("gu", 0)
    for p in range(1, PAIRS):
        out += some("gu", p) + some("d", p - 1)
    return out + some("d", PAIRS - 1)


MOE_ORDER = {t: n for n, t in enumerate(moe_order())}


def moe_place(what, p, k):
    return MOE_ORDER[(what, p, k)]


def moe_events(eng, event):
    def turn(p, i):
        for k in range(2):
            event("gu", p, k, i)
        if p >= 2:
            event("S", p - 2, 0, i)
        for k in range(2, 8):
            event("gu", p, k, i)
        event("A", p, 0, i)
        for half in range(2):
            if p + 1 < PAIRS:
                event("G", p + 1, half, i)
            if p >= 1:
                event("d", p - 1, 2 * half, i)
                event("d", p - 1, 2 * half + 1, i)
        if p >= 1:
            event("Y", p - 1, 0, i)
        event("T", p, 0, i)
    for half in range(2):
        event("G", 0, half, None)
    turn(0, None)
    turn(1, None)
    with eng.Fori(0, PAIRS - 3) as i:
        turn(2, i)
    turn(PAIRS - 1, None)
    event("S", PAIRS - 2, 0, None)
    for k in range(4):
        event("d", PAIRS - 1, k, None)
    event("Y", PAIRS - 1, 0, None)
    event("S", PAIRS - 1, 0, None)


def stream():
    out = [("ffn1", w, True) for w in swiglu_order(FC)]
    out += [("memk", m, True) for m in range(4)] + [("memv", m, True) for m in range(4)]
    out += [("dn", m, True) for m in range(12)] + [("z", m, True) for m in range(4)]
    out += [("v", m, True) for m in range(2)] + [("q", m, True) for m in range(4)]
    out += [("kv", m, True) for m in range(4)] + [("memq", m, True) for m in range(4)]
    out += [("w1", m, False) for m in range(8)]
    out += [("ada", m, False) for m in range(LAYERS * 48)]
    out += [("gate", m, True) for m in range(24)]
    out += [("branch", (m, b), True) for m in range(4) for b in range(3)]
    out += [("wout", m, True) for m in range(DC)]
    out += [("ffn2", w, True) for w in swiglu_order(FC)]
    for l in range(LAYERS):
        out += [(f"a{l}", m, True) for m in range(8)] + [(f"p{l}", m, True) for m in range(4)]
        out += [(f"G{l}", m, True) for m in range(16)]
        out += [(f"pool{l}", 0, True)] + [(f"conv{l}", m, True) for m in range(4)]
        out += [(f"wout{l}", m, True) for m in range(DC)]
        out += [(f"moe{l}", w, True) for w in moe_order()]
    return out


STREAM = stream()
SPLITS = [r for r, t in enumerate(STREAM) if t[2]]
NUMBER = {r: n for n, r in enumerate(SPLITS)}
START = {}
for _r, _t in enumerate(STREAM):
    START.setdefault(_t[0], _r)


LOOPED = {"ffn1": FC, "ffn2": FC}
FIRST_F = {"ffn1": 0, "ffn2": FC}
TILES_OF = {"ffn1": 3 * FC, "ffn2": 3 * FC, "moe0": 6 * EXPERTS, "moe1": 6 * EXPERTS}


def moe_tile(l, what, p, k):
    return START[f"moe{l}"] + moe_place(what, p, k)


def along(value, i, per):
    return value if i is None else value + per * i


def swiglu_steps(eng, stage, step):
    n, at, order = LOOPED[stage], START[stage], swiglu_order(LOOPED[stage])
    for j in range(2):
        step(at + j, *order[j], None)
    turns = (n - 2) // 2
    with eng.Fori(0, turns) as i:
        for j in range(2, 8):
            step(at + j, *order[j], i)
    for j in range(3 * n - 4, 3 * n):
        step(at + j, *order[j], None)
    return turns


def shared(semaphore, events):
    out, at = {}, 0
    for name, count in events:
        out[name] = (semaphore, at)
        at += count
    return out


SHARED = {
    **shared("dn_products", [(n, 1) for n in ("dn_sums", "dn_gc_mm", "dn_rows_mm", "dn_kq_mm", "dn_tok_mm",
                                              "dn_vw_mm", "dn_state_mm", "dn_v1_mm", "dn_o_mm", "dn_osum")]),
    **shared("dn_scalars", [("dn_squares", 1), ("dn_root", 1), ("dn_exp", 2), ("dn_decays", 2), ("dn_eg", 1),
                            ("dn_vtok", 1), ("dn_z", LEVELS), ("dn_vw", 2), ("dn_state", 1), ("dn_v1", 1),
                            ("dn_osq", 1), ("dn_oroot", 1)])}


def program(nc, wstream, consts_d, params_d, x_d, mem_d, rows_d, out_d):
    with ExitStack() as ctx:
        sems = {}

        def s(name):
            name = SHARED.get(name, (name, 0))[0]
            if name not in sems:
                sems[name] = ctx.enter_context(nc.semaphore(name))
            return sems[name]

        def after(name, count):
            return SHARED.get(name, (name, 0))[1] + count

        def sb(name, shape, dt=F32, where=ctx):
            return where.enter_context(nc.sbuf_tensor(name, shape, dt))

        raw = [sb(f"raw{i}", [P, TILE]) for i in range(RAW)]
        whi = [sb(f"whi{i}", [P, TILE], F32R) for i in range(AHEAD)]
        wlo = [sb(f"wlo{i}", [P, TILE], F32R) for i in range(AHEAD)]
        xT = sb("xT", [P, DC, T])
        hf = sb("hf", [P, DC, T])
        hhi = sb("hhi", [P, DC, T], F32R)
        hlo = sb("hlo", [P, DC, T], F32R)
        consts = sb("consts", [P, NCONST])
        params = sb("params", [P, NPARAM])
        var = sb("var", [P, T])
        std = sb("std", [P, T])
        rstd = sb("rstd", [P, T])
        zero = sb("zero", [P, 512], BF16)
        pair_a = sb("pair_a", [P, 2, T])
        pair_b = sb("pair_b", [P, 2, T])
        ahi = sb("ahi", [P, 2, T], F32R)
        alo = sb("alo", [P, 2, T], F32R)
        mod = sb("mod", [P, LAYERS * 48])
        c_act = sb("c_act", [P, DC])
        gscale = sb("gscale", [P, LAYERS * 2 * DC])

        acc = ctx.enter_context(nc.psum_tensor("acc", [P, DC * T], F32))
        work = [ctx.enter_context(nc.psum_tensor(f"work{i}", [P, 512], F32)) for i in range(4)]
        acc_c = acc[:, :].rearrange("p (c t) -> p c t", t=T)

        def const(name):
            return consts[:, CONST[name][0]:CONST[name][1]]

        def par(name):
            return params[:, PARAM[name][0]:PARAM[name][1]]

        def col(name, m):
            return params[:, PARAM[name][0] + m:PARAM[name][0] + m + 1]

        def spread(ap, shape, steps):
            return bass.AP(tensor=ap.tensor, offset=ap.offset, ap=[list(ap.ap[0])] + [[st, n] for st, n in zip(steps, shape)])

        ident, ones, upper = const("ident"), const("ones"), const("upper")

        mixer, att, early, dn, late = (ExitStack() for _ in range(5))
        dnc = sb("dnc", [P, 12, T], F32, mixer)
        zT = sb("zT", [P, DNH, T], F32, mixer)
        ohi = sb("ohi", [P, 3, 4, T], F32R, mixer)
        olo = sb("olo", [P, 3, 4, T], F32R, mixer)
        small = sb("small", [P, QT, 32], F32, mixer)
        sm = sb("sm", [P, 256], F32, mixer)
        kmem = sb("kmem", [P, 4, T], F32, att)
        vmem = sb("vmem", [P, QT, 512], F32, att)
        tb = sb("tb", [P, HEADS, T], F32, att)
        vtok = sb("vtok", [P, QT, 2 * P], F32, att)
        qT = sb("qT", [P, 4, T], F32, att)
        kvT = sb("kvT", [P, 4, T], F32, att)
        qmem = sb("qmem", [P, 4, T], F32, att)
        soft = sb("soft", [P, DC * T], F32, att)
        memhi = sb("memhi", [P, DC, T], F32R, early)
        memlo = sb("memlo", [P, DC, T], F32R, early)
        early.close()
        pt = sb("pt", [P, 16 * P], F32, att)
        convin = sb("convin", [P, 3, 3 + T], F32, att)
        hidden = sb("hidden", [P, 2, 2, 30], F32, att)
        kcmp = sb("kcmp", [P, 16], F32, att)
        vcmp = sb("vcmp", [P, GROUPS, HPG, DH], F32, att)
        scmp = sb("scmp", [P, 16, 16], F32, att)
        pcmp = sb("pcmp", [P, QT * GROUPS, HPG, 32], F32, att)
        att.close()
        pcT = pt[:, 0:GROUPS * T].rearrange("p (g t) -> p g t", t=T)
        dn_el, dn_eu, dn_a, dn_b, dn_inv, dn_invT, dn_z, dn_qk, dn_vb, dn_kb, dn_vn = (
            sb(f"dn_{n}", [P, 8 * P], F32, dn)
            for n in ("el", "eu", "a", "b", "inv", "invT", "z", "qk", "vb", "kb", "vn"))
        dn_kd, dn_w, dn_s, dn_qd = (sb(f"dn_{n}", [P, 4 * P], F32, dn) for n in ("kd", "w", "s", "qd"))
        dn.close()
        gates = sb("gates", [P, 3 * DC, T], F32, late)
        late.close()
        mixer.close()
        gate2 = sb("gate2", [P, 2 * DC, T])
        select = sb("select", [P, QT, PAIRS, P], F32R)
        selectT = sb("selectT", [P, PAIRS, T], F32R)
        vpad = sb("vpad", [P, 4, 30 + T])
        yconv = sb("yconv", [P, 4, T])
        ppad = sb("ppad", [P, 4, 16 + T])
        xghi = sb("xghi", [P, DC * 2 * P], F32R)
        xglo = sb("xglo", [P, DC * 2 * P], F32R)
        yhi, phi = (xghi[:, j * 1024:(j + 1) * 1024].rearrange("p (c t) -> p c t", t=T) for j in range(2))
        ylo, plo = (xglo[:, j * 1024:(j + 1) * 1024].rearrange("p (c t) -> p c t", t=T) for j in range(2))
        yshi = sb("yshi", [P, D], F32R)
        yslo = sb("yslo", [P, D], F32R)
        rt = sb("rt", [P, 640])
        chi = sb("chi", [P, QT * EXPERTS], F32R)
        clo = sb("clo", [P, QT * EXPERTS], F32R)
        identr = sb("identr", [P, P], F32R)
        spare_d = sb("spare_d", [P, 2, TILE])
        overflow = sb("overflow", [1, LAYERS], mybir.dt.int32)

        def tile_loaded(eng, r, i=None, turn=6):
            eng.wait_ge(s(f"loaded{r % RAW}"), along(16 * (r // RAW + 1), i, 16 * (turn // RAW)))

        held = set(range(NUMBER[START["gate"]], NUMBER[START["gate"]] + AHEAD))

        EVAC = {}
        for r, (stage, what, _) in enumerate(STREAM):
            if stage.rstrip("01") in ("memk", "memv", "dn", "z", "v", "q", "kv", "memq", "gate", "a", "p", "G"):
                EVAC[r] = len(EVAC)

        def evacuated(eng, stage, m):
            eng.wait_ge(s("tile_evac"), EVAC[START[stage] + m] + 1)

        def own_slots(t, c, n):
            a = t[:, c * T:c * T + 1]
            return spread(a, (n, 2, SLOTS), (T, P + SLOTS, 1))

        def spare_units(eng, unit):
            def pair(p, i):
                for j in range(2):
                    gu, d = moe_place("gu", p, 4 * j), moe_place("d", p, 2 * j)
                    unit(2 * p + j, gu, d, i)
            pair(0, None)
            with eng.Fori(0, PAIRS - 2) as i:
                pair(1, i)
            pair(PAIRS - 1, None)

        block = ctx.enter_context(nc.Block())

        @block.sync
        def _(sp):
            sp.dma_start(params[:], params_d).then_inc(s("params_loaded"), 16)
            sp.dma_start(xT[:], x_d).then_inc(s("x_loaded"), 16)
            sp.dma_start(consts[:], consts_d).then_inc(s("consts_loaded"), 16)
            sp.dma_start(soft[:, :], mem_d.rearrange("p c t -> p (c t)")).then_inc(s("mem_loaded"), 16)

            def load(r, i=None):
                if r >= RAW:
                    if r - RAW in NUMBER:
                        sp.wait_ge(s("lo_done"), along(NUMBER[r - RAW] + 1, i, 6))
                    else:
                        sp.wait_ge(s("pe_tile"), r - RAW + 1)
                src = wstream[r] if i is None else wstream[bass.ds(r + 6 * i, 1)].rearrange("o p c -> (o p) c")
                sp.dma_start(raw[r % RAW][:], src).then_inc(s(f"loaded{r % RAW}"), 16)

            r = 0
            while r < len(STREAM):
                stage = STREAM[r][0]
                if stage in TILES_OF and r == START[stage] + RAW:
                    turns = (TILES_OF[stage] - RAW) // 6
                    with sp.Fori(0, turns) as i:
                        for j in range(6):
                            load(r + j, i)
                    r += 6 * turns
                else:
                    load(r)
                    r += 1
            sp.wait_ge(s("final_ready"), 1)
            sp.dma_start(out_d, hf[:]).then_inc(s("stored"), 16)
            sp.wait_ge(s("stored"), 16)

        @block.gpsimd
        def _(pool):
            half = HEADS // 2
            rows = rows_d.rearrange("h p c -> p h c")
            for n in range(2):
                pool.wait_ge(s("bias_rows"), half * (n + 1))
                pool.dma_start(rows[:, half * n:half * (n + 1), :],
                               soft[:, 0:half * BROW].rearrange("p (h c) -> p h c", c=BROW)
                               ).then_inc(s("rows_stored"), 16)
                pool.wait_ge(s("rows_stored"), 16 * (n + 1))
            skew = bass.AP(tensor=rows_d.tensor, offset=P - 1, ap=[[BROW - 1, P], [P * BROW, HEADS], [1, T]])
            pool.dma_start(tb[:], skew).then_inc(s("tb_loaded"), 16)
            for l in range(LAYERS):
                pool.wait_ge(s("flag_ready"), l + 1)
                with pool.If(pool.value_load(overflow[0:1, l:l + 1], min_val=0, max_val=1) > 0):
                    def unit(u, gu, d, i):
                        if u > 0:
                            pool.wait_ge(s(f"spare_free{l}"), along(u, i, 2))

                        def tiles(r, n):
                            at = START[f"moe{l}"] + r
                            src = wstream[at:at + n] if i is None else wstream[bass.ds(at + 12 * i, n)]
                            return src.rearrange("t p c -> p t c")
                        pool.dma_start(gate2[:, :, :].rearrange("p (t c) k -> p t (c k)", t=4), tiles(gu, 4)
                                       ).then_inc(s(f"spare_loaded{l}"), 16)
                        pool.dma_start(spare_d[:], tiles(d, 2)).then_inc(s(f"spare_loaded{l}"), 16)
                    spare_units(pool, unit)

        @block.tensor
        def _(pe):
            reader = {}

            def claim(banks, name, count):
                for b in banks:
                    if b in reader:
                        pe.wait_ge(s(reader[b][0]), after(*reader[b]))
                    reader[b] = (name, count)

            def norm_sum(k, bank, n=DC, src=hf):
                claim([bank], "norm_var", k + 1)
                pe.wait_ge(s("norm_sq"), k + 1)
                for m in range(n):
                    mm = pe.matmul(work[bank][:, 0:T], ones, src[:, m, :], start=(m == 0), stop=(m == n - 1))
                mm.then_inc(s("norm_sum"), 1)

            def tile_ready(r, i=None, turn=6):
                if r in NUMBER:
                    pe.wait_ge(s("lo_done"), along(NUMBER[r] + 1, i, turn))
                    return whi[NUMBER[r] % AHEAD], wlo[NUMBER[r] % AHEAD]
                tile_loaded(pe, r)
                return raw[r % RAW], None

            def product(out, terms, start=True, stop=True, skip=False):
                n = 3 * len(terms)
                k = 0
                for (lh, ll), (rh, rl) in terms:
                    for a, b in ((lh, rh), (lh, rl), (ll, rh)):
                        mm = pe.matmul(out, a, b, start=(start and k == 0), stop=(stop and k == n - 1),
                                       skip_group_check=skip)
                        k += 1
                return mm

            def feature_tile(r, xh, xl, bank=None, out=None):
                h, l = tile_ready(r)
                if out is None:
                    claim([bank], "tile_evac", EVAC[r] + 1)
                    out = work[bank][:, 0:T]
                mm = product(out, [((h[:, c * P:(c + 1) * P], l[:, c * P:(c + 1) * P]), (xh[:, c, :], xl[:, c, :]))
                                   for c in range(DC)])
                mm.then_inc(s("pe_tile"), 1)

            def token_tile(r, xh, xl, bank):
                h, l = tile_ready(r)
                claim([bank], "tile_evac", EVAC[r] + 1)
                for q in range(QT):
                    t = slice(q * P, (q + 1) * P)
                    mm = product(work[bank][:, t], [((xh[:, c, t], xl[:, c, t]),
                                                     (h[:, c * P:(c + 1) * P], l[:, c * P:(c + 1) * P]))
                                                    for c in range(DC)])
                mm.then_inc(s("pe_tile"), 1)

            def wide_tile(r, xh, xl, out, kc=4):
                h, l = tile_ready(r)
                for m in range(2):
                    mm = product(out[:, m * T:(m + 1) * T],
                                 [((h[:, c * T + m * P:c * T + (m + 1) * P], l[:, c * T + m * P:c * T + (m + 1) * P]),
                                   (xh[:, c, :], xl[:, c, :])) for c in range(kc)])
                mm.then_inc(s("pe_tile"), 1)

            def clear(banks):
                pe.wait_ge(s("zero_ready"), 1)
                for out in banks:
                    pe.matmul(out, zero[:, 0:P], zero[:, :], start=True, stop=True)

            def swiglu(stage, out_reader, out_count):
                claim(["acc"], out_reader, out_count)
                clear([acc[:, b * 512:(b + 1) * 512] for b in range(4)])
                base = FIRST_F[stage]
                claim(range(4), "act_ready", base + LOOPED[stage])

                def step(r, what, f, i):
                    h, l = tile_ready(r, i)
                    p = f % 2
                    if what == "d":
                        pe.wait_ge(s("act_ready"), along(base + f + 1, i, 2))
                        for m in range(DC):
                            c = slice(m * P, (m + 1) * P)
                            mm = product(acc_c[:, m, :], [((h[:, c], l[:, c]), (ahi[:, p, :], alo[:, p, :]))],
                                         start=False, skip=True)
                    else:
                        bank = work[2 * p + (what == "u")]
                        mm = product(bank[:, 0:T], [((h[:, c * P:(c + 1) * P], l[:, c * P:(c + 1) * P]),
                                                     (hhi[:, c, :], hlo[:, c, :])) for c in range(DC)])
                    mm.then_inc(s("pe_tile"), 1)

                swiglu_steps(pe, stage, step)

            pe.wait_ge(s("consts_loaded"), 16)
            pe.wait_ge(s("params_loaded"), 16)
            norm_sum(0, 0)
            norm_sum(1, 1)
            for h in range(HEADS):
                claim([h % 4], "bias_rows", h + 1)
                rel = params[0:BUCKETS, PARAM["rel"][0] + h:PARAM["rel"][0] + h + 1]
                pe.matmul(work[h % 4][:, 0:BROW], spread(rel, (P,), (0,)), const("onehot")[0:BUCKETS, :],
                          start=True, stop=True).then_inc(s("bias_mm"), 1)
            pe.wait_ge(s("h_ready"), 2)
            swiglu("ffn1", "x_ready", 1)

            norm_sum(2, 0)
            pe.wait_ge(s("mem_ready"), 2)
            for m in range(4):
                feature_tile(START["memk"] + m, memhi, memlo, 1 + m % 3)
            norm_sum(3, 0)
            for m in range(4):
                token_tile(START["memv"] + m, memhi, memlo, 1 + m % 3)

            pe.wait_ge(s("hf_done"), 6)
            claim([0], "small_ready", 1)
            for q in range(QT):
                for c in range(DC):
                    a = PARAM["w_small"][0] + 32 * c
                    mm = pe.matmul(work[0][:, q * 32:(q + 1) * 32], hf[:, c, q * P:(q + 1) * P],
                                   params[:, a:a + 32], start=(c == 0), stop=(c == DC - 1))
            mm.then_inc(s("small_mm"), 1)
            pe.wait_ge(s("h_ready"), 4)
            for m in range(12):
                feature_tile(START["dn"] + m, hhi, hlo, m % 4)
            for m in range(4):
                feature_tile(START["z"] + m, hhi, hlo, m % 4)
            for m in range(2):
                token_tile(START["v"] + m, hhi, hlo, m)
            for n, stage in enumerate(("q", "kv", "memq")):
                for m in range(4):
                    feature_tile(START[stage] + m, hhi, hlo, (2 + m) % 4)

            pe.wait_ge(s("flat_ready"), 1)
            claim(range(4), "hidden_ready", 2)
            flat = hf[:, :, :].rearrange("p c t -> p (c t)")[:, 0:2 * 16 * 30].rearrange("p (v j c) -> p v j c", v=2, j=16)
            for t in range(8):
                v = t // 4
                w, _ = tile_ready(START["w1"] + t)
                for jj in range(4):
                    j = 4 * (t % 4) + jj
                    for m in range(2):
                        mm = pe.matmul(work[2 * v + m][:, 0:30], w[:, jj * T + m * P:jj * T + (m + 1) * P],
                                       flat[:, v, j, :], start=(j == 0), stop=(j == 15), skip_group_check=True)
                mm.then_inc(s("pe_tile"), 1)

            ada_at = [START["ada"]]

            def ada(n):
                for r in range(ada_at[0], min(ada_at[0] + n, START["gate"])):
                    w, _ = tile_ready(r)
                    a = r - START["ada"]
                    if a == 0:
                        pe.wait_ge(s("c_ready"), 1)
                        claim([1], "mod_ready", 1)
                    for c in range(DC):
                        mm = pe.matmul(work[1][:, a:a + 1], w[:, c * P:(c + 1) * P], c_act[:, c:c + 1],
                                       start=(c == 0), stop=(c == DC - 1))
                    mm.then_inc(s("pe_tile"), 1)
                    ada_at[0] += 1

            def scores(g):
                if g == 0:
                    evacuated(pe, "memq", 3)
                    claim(["acc"], "sm_exp", 1)
                    for q in range(QT):
                        for h in range(4):
                            mm = pe.matmul(acc_c[:, 4 * q + h, :], qmem[:, h, q * P:(q + 1) * P], kmem[:, h, :],
                                           start=True, stop=True)
                elif g == 1:
                    claim(["acc"], "sm_bias", 2)
                    for br in range(2):
                        for h in range(HEADS):
                            d = slice(DH * (h // HPG), DH * (h // HPG) + DH)
                            a = (br * HEADS + h) * P
                            mm = pe.matmul(acc[:, a:a + P], qT[d, h % HPG, 0:P], kvT[d, 2 + br, 0:P],
                                           start=True, stop=True)
                else:
                    claim(["acc"], "sm_bias", g + 1)
                    for h in range(HEADS):
                        d = slice(DH * (h // HPG), DH * (h // HPG) + DH)
                        mm = pe.matmul(acc_c[:, h, :], qT[d, h % HPG, P:T], kvT[d, g, :], start=True, stop=True)
                mm.then_inc(s("sm_scores"), 1)

            def transposes(g):
                for r in range(4):
                    if r % 2 == 0:
                        pe.wait_ge(s("sm_probs"), 2 * g + r // 2 + 1)
                    claim([0], "pt_ready", 4 * g + r + 1)
                    for b in range(4):
                        mm = pe.transpose(work[0][:, b * P:(b + 1) * P],
                                          soft[:, (4 * r + b) * P:(4 * r + b + 1) * P], ident)
                    mm.then_inc(s("pt_mm"), 1)
                    ada(1)

            def values(g):
                pe.wait_ge(s("pt_ready"), 4 * g + 4)
                if g == 0:
                    claim([2, 3], "olo_ready", 2)
                    for h in range(4):
                        for q in range(QT):
                            for k in range(QT):
                                b = ((4 * q + h) * 2 + k) * P
                                mm = pe.matmul(work[2 + h // 2][:, (h % 2) * T + q * P:(h % 2) * T + (q + 1) * P],
                                               vmem[:, k, h * P:(h + 1) * P], pt[:, b:b + P],
                                               start=(k == 0), stop=(k == QT - 1))
                    mm.then_inc(s("o_mm"), 1)
                    return
                for u in range(16):
                    h, k, br, q = (u % HEADS, 0, u // HEADS, 0) if g == 1 else (u // 2, u % 2, g - 2, 1)
                    gr, j = h // HPG, h % HPG
                    out = work[2 + j // 2][DH * gr:DH * gr + DH, (j % 2) * T + q * P:(j % 2) * T + (q + 1) * P]
                    mm = pe.matmul(out, vtok[:, k, br * P + DH * gr:br * P + DH * gr + DH], pt[:, u * P:(u + 1) * P],
                                   start=False, stop=False, skip_group_check=True)
                if g == 3:
                    mm.then_inc(s("o_mm"), 1)

            scores(0)
            pe.wait_ge(s("hidden_ready"), 2)
            claim([0], "cmp_kv", 5)
            for g in range(GROUPS):
                for m in range(2):
                    pe.matmul(work[0][DH * g:DH * g + DH, 0:NCMP], par("w2k")[:, m * DH:(m + 1) * DH],
                              hidden[:, 0, m, g * NCMP:(g + 1) * NCMP], start=(m == 0), stop=(m == 1),
                              skip_group_check=True)
            for g in range(GROUPS):
                for j in range(HPG):
                    for m in range(2):
                        mm = pe.matmul(work[0][32 * j:32 * j + NCMP, 64 + g * DH:64 + (g + 1) * DH],
                                       hidden[:, 1, m, g * NCMP:(g + 1) * NCMP], par("w2v")[:, m * DH:(m + 1) * DH],
                                       start=(m == 0), stop=(m == 1), skip_group_check=True)
            mm.then_inc(s("cmp_mm"), 1)
            ada(7)
            transposes(0)
            values(0)
            pe.wait_ge(s("cmp_kv"), 5)
            claim(["acc"], "cmp_bias", 5)
            for q in range(QT):
                for h in range(HEADS):
                    d = slice(DH * (h // HPG), DH * (h // HPG) + DH)
                    a = (h // HPG) * 512 + (q * HPG + h % HPG) * 16
                    mm = pe.matmul(acc[:, a:a + NCMP], qT[d, h % HPG, q * P:(q + 1) * P], kcmp[d, 0:NCMP],
                                   start=True, stop=True)
            mm.then_inc(s("cmp_scores"), 1)
            pe.wait_ge(s("pt_ready"), 4)
            scores(1)
            claim([2, 3], "olo_ready", 4)
            clear([work[2][:, :], work[3][:, :]])
            ada(2)
            pe.wait_ge(s("cmp_probs"), 1)
            claim([0], "pct_ready", 1)
            for b in range(QT * GROUPS):
                q, g = b // GROUPS, b % GROUPS
                mm = pe.transpose(work[0][:, (g * QT + q) * P:(g * QT + q + 1) * P],
                                  pcmp[:, b, :, :].rearrange("p j c -> p (j c)"), ident)
            mm.then_inc(s("pct_mm"), 1)
            ada(1)
            pe.wait_ge(s("pct_ready"), 1)
            for g in range(GROUPS):
                for j in range(HPG):
                    mm = pe.matmul(work[2 + j // 2][DH * g:DH * g + DH, (j % 2) * T:(j % 2) * T + T],
                                   vcmp[:, g, j, :], pcT[:, g, :],
                                   start=False, stop=False, skip_group_check=True)
            mm.then_inc(s("cmp_values"), 1)
            ada(3)
            transposes(1)
            scores(2)
            values(1)
            ada(4)
            transposes(2)
            scores(3)
            values(2)
            ada(4)
            transposes(3)
            values(3)

            pe.wait_ge(s("dn_squares"), after("dn_squares", 1))
            claim(["acc"], "dn_var", 1)
            for m in range(8):
                mm = pe.matmul(acc_c[:, m, :], ones, hf[:, m, :], start=True, stop=True)
            mm.then_inc(s("dn_sums"), 1)
            ada(8)
            pe.wait_ge(s("dn_decay"), 1)
            claim([0], "dn_gc", 1)
            for c in range(QT):
                pe.matmul(work[0][:, c * 4:c * 4 + 4], upper, sm[:, 16 + 4 * c:20 + 4 * c], start=True, stop=True)
                mm = pe.matmul(work[0][:, 8 + c * 4:12 + c * 4], ones, sm[:, 16 + 4 * c:20 + 4 * c],
                               start=True, stop=True)
            mm.then_inc(s("dn_gc_mm"), 1)
            claim([2, 3], "dn_eg", 1)
            for u in range(8):
                mm = pe.matmul(work[2 + u // 4][:, (u % 4) * P:(u % 4 + 1) * P], spread(sm[:, 16 + u:17 + u], (P,), (0,)),
                               upper, start=True, stop=True)
            mm.then_inc(s("dn_rows_mm"), 1)
            pe.wait_ge(s("dn_unit"), 1)
            claim(["acc"], "dn_kq", 2)
            for u in range(8):
                c, h = u // 4, u % 4
                t = slice(c * P, (c + 1) * P)
                pe.matmul(acc[:, u * P:(u + 1) * P], dnc[:, 4 + h, t], dnc[:, 4 + h, t], start=True, stop=True)
                mm = pe.matmul(acc[:, (8 + u) * P:(9 + u) * P], dnc[:, 4 + h, t], dnc[:, h, t], start=True, stop=True)
            mm.then_inc(s("dn_kq_mm"), 1)
            ada(8)
            claim(["acc"], "dn_tok", 3)
            for u in range(8):
                c, h = u // 4, u % 4
                t = slice(c * P, (c + 1) * P)
                pe.transpose(acc[:, u * P:(u + 1) * P], dnc[:, 4 + h, t], ident)
                mm = pe.transpose(acc[:, (8 + u) * P:(9 + u) * P], dnc[:, 8 + h, t], ident)
            mm.then_inc(s("dn_tok_mm"), 1)
            ada(8)
            for lv in range(LEVELS):
                pe.wait_ge(s("dn_level"), lv + 1)
                claim(["acc"], "dn_update", 2 * lv + 2)
                claim([2, 3], "dn_update", 2 * lv + 2)
                for u in range(8):
                    a = slice(u * P, (u + 1) * P)
                    mm = pe.matmul(acc[:, a], dn_b[:, a], dn_invT[:, a], start=True, stop=True)
                mm.then_inc(s("dn_z_mm"), 1)
                ada(1)
                pe.wait_ge(s("dn_z"), after("dn_z", lv + 1))
                for u in range(8):
                    a = slice(u * P, (u + 1) * P)
                    pe.matmul(acc[:, (8 + u) * P:(9 + u) * P], dn_z[:, a], dn_inv[:, a], start=True, stop=True)
                    mm = pe.matmul(work[2 + u // 4][:, (u % 4) * P:(u % 4 + 1) * P], dn_inv[:, a], dn_z[:, a],
                                   start=True, stop=True)
                mm.then_inc(s("dn_x_mm"), 1)
                ada(3)
            pe.wait_ge(s("dn_update"), 2 * LEVELS)
            claim(["acc"], "dn_vw", 2)
            for h in range(4):
                a, b = slice(h * P, (h + 1) * P), slice((4 + h) * P, (5 + h) * P)
                pe.matmul(acc[:, a], dn_invT[:, a], dn_vb[:, a], start=True, stop=True)
                mm = pe.matmul(acc[:, b], dn_kb[:, b], dn_invT[:, b], start=True, stop=True)
            mm.then_inc(s("dn_vw_mm"), 1)
            ada(4)
            pe.wait_ge(s("dn_vw"), after("dn_vw", 2))
            claim([0], "dn_state", 1)
            for h in range(4):
                a = slice(h * P, (h + 1) * P)
                mm = pe.matmul(work[0][:, a], dn_kd[:, a], dn_vn[:, a], start=True, stop=True)
            mm.then_inc(s("dn_state_mm"), 1)
            ada(4)
            pe.wait_ge(s("dn_state"), after("dn_state", 1))
            claim([2], "dn_v1", 1)
            for h in range(4):
                a, b = slice(h * P, (h + 1) * P), slice((4 + h) * P, (5 + h) * P)
                pe.matmul(work[2][:, a], dn_invT[:, b], dn_vb[:, b], start=True, stop=False)
                mm = pe.matmul(work[2][:, a], dn_w[:, a], dn_s[:, a], start=False, stop=True)
            mm.then_inc(s("dn_v1_mm"), 1)
            ada(1)
            pe.wait_ge(s("dn_v1"), after("dn_v1", 1))
            claim(["acc"], "dn_out", 1)
            for h in range(4):
                a, b = slice(h * P, (h + 1) * P), slice((4 + h) * P, (5 + h) * P)
                pe.matmul(acc_c[:, h, 0:P], dn_vn[:, a], dn_qk[:, a], start=True, stop=True)
                pe.matmul(acc_c[:, h, P:T], dn_s[:, a], dn_qd[:, a], start=True, stop=False)
                mm = pe.matmul(acc_c[:, h, P:T], dn_vn[:, b], dn_qk[:, b], start=False, stop=True)
            mm.then_inc(s("dn_o_mm"), 1)
            ada(96)
            pe.wait_ge(s("dn_osq"), after("dn_osq", 1))
            for h in range(4):
                mm = pe.matmul(acc_c[:, 4 + h, :], ones, hf[:, h, :], start=True, stop=True)
            mm.then_inc(s("dn_osum"), 1)

            for m in range(24):
                feature_tile(START["gate"] + m, hhi, hlo, m % 4)
            pe.wait_ge(s("olo_ready"), 6)
            for n in range(12):
                r = START["branch"] + n
                b = STREAM[r][1][1]
                claim([n % 4], "branch_read", n + 1)
                wide_tile(r, ohi[:, b], olo[:, b], work[n % 4][:, :])
            claim(["acc"], "x_ready", 2)
            pe.wait_ge(s("merged_ready"), 4)
            for m in range(DC):
                feature_tile(START["wout"] + m, hhi, hlo, out=acc_c[:, m, :])
            norm_sum(4, 0)
            norm_sum(5, 0)
            pe.wait_ge(s("h_ready"), 6)
            swiglu("ffn2", "x_ready", 3)
            norm_sum(6, 0)

            for l in range(LAYERS):
                k = 7 + 3 * l
                norm_sum(k, 0)
                pe.wait_ge(s("h_ready"), 8 + 2 * l)
                for n, (stage, count) in enumerate(((f"a{l}", 8), (f"p{l}", 4), (f"G{l}", 16))):
                    for m in range(count):
                        feature_tile(START[stage] + m, hhi, hlo, m % 4)
                pe.wait_ge(s("pooled"), l + 1)
                claim(["acc"], "pool_read", l + 1)
                h, lo = tile_ready(START[f"pool{l}"])
                for m in range(DC):
                    a = slice(m * P, (m + 1) * P)
                    mm = product(acc_c[:, m, :], [((h[:, a], lo[:, a]), (phi[:, m // 2, :], plo[:, m // 2, :]))])
                mm.then_inc(s("pe_tile"), 1)
                pe.wait_ge(s("conv_done2"), l + 1)
                claim([0], "ln_centred", l + 1)
                for m in range(4):
                    mm = pe.matmul(work[0][:, 0:T], ones, yconv[:, m, :], start=(m == 0), stop=(m == 3))
                mm.then_inc(s("ln_mean"), 1)
                norm_sum(k + 1, 1, 4, hf)
                pe.wait_ge(s("y_ready"), l + 1)
                for m in range(4):
                    claim([m], "conv_read", 4 * l + m + 1)
                    wide_tile(START[f"conv{l}"] + m, yhi, ylo, work[m][:, :])
                pe.wait_ge(s("mixed_ready"), 4 * (l + 1))
                claim(["acc"], "x_ready", 4 + 2 * l)
                for m in range(DC):
                    feature_tile(START[f"wout{l}"] + m, hhi, hlo, out=acc_c[:, m, :])
                norm_sum(k + 2, 0)
                pe.wait_ge(s("hf_done"), 12 + 4 * l)
                claim([1], "router_read", l + 1)
                for q in range(QT):
                    for c in range(DC):
                        a = PARAM[f"router{l}"][0] + 36 * c
                        mm = pe.matmul(work[1][:, q * 36:(q + 1) * 36], hf[:, c, q * P:(q + 1) * P],
                                       params[:, a:a + 36], start=(c == 0), stop=(c == DC - 1))
                mm.then_inc(s("router_mm"), 1)
                claim(["acc"], "ht_low", 4 * (l + 1))
                for b in range(QT * DC):
                    mm = pe.transpose(acc[:, b * P:(b + 1) * P], hf[:, b % DC, (b // DC) * P:(b // DC + 1) * P], ident)
                    if b % 4 == 3:
                        mm.then_inc(s("ht_mm"), 1)
                pe.wait_ge(s("mask_ready"), l + 1)
                claim([1], "rank_read", l + 1)
                m0, m1 = rt[:, 384:416], rt[:, 416:448]
                pe.matmul(work[1][:, 0:32], upper, m0, start=True, stop=True)
                pe.matmul(work[1][:, 32:64], ones, m0, start=True, stop=False)
                pe.matmul(work[1][:, 32:64], upper, m1, start=False, stop=True)
                pe.matmul(work[1][:, 64:96], ones, m0, start=True, stop=False)
                pe.matmul(work[1][:, 64:96], ones, m1, start=False, stop=True).then_inc(s("rank_mm"), 1)
                pe.wait_ge(s("slots_ready"), l + 1)
                claim([0], "wslot_read", 2 * (l + 1))
                for p in range(PAIRS):
                    for q in range(QT):
                        for c in (chi, clo):
                            mm = pe.matmul(work[0][:, 2 * p:2 * p + 2], select[:, q, p, :],
                                           c[:, q * EXPERTS + 2 * p:q * EXPERTS + 2 * p + 2],
                                           start=(q == 0 and c is chi), stop=(q == 1 and c is clo))
                mm.then_inc(s("wslot_mm"), 1)
                for r in range(PAIRS // 2):
                    claim([1 + r % 3], "selectT_ready", 8 * l + r + 1)
                    for j in range(2):
                        for q in range(QT):
                            mm = pe.matmul(work[1 + r % 3][:, j * T + q * P:j * T + (q + 1) * P],
                                           select[:, q, 2 * r + j, :], identr[:], start=True, stop=True)
                    mm.then_inc(s("selectT_mm"), 1)
                claim(["acc"], "x_ready", 5 + 2 * l)
                clear([acc[:, b * 512:(b + 1) * 512] for b in range(4)])
                pe.wait_ge(s("flag_ready"), l + 1)
                claim(range(4), "y_low", 2 * PAIRS * (l + 1))
                with pe.If(pe.value_load(overflow[0:1, l:l + 1], min_val=0, max_val=1) > 0):
                    def unit(u, gu, d, i):
                        pe.wait_ge(s(f"spare_weights{l}"), along(u + 1, i, 2))
                        for q in range(QT):
                            pe.matmul(work[1][:, q * P:(q + 1) * P], ones, var[:, q * P:(q + 1) * P],
                                      start=True, stop=True)
                        pe.wait_ge(s(f"spare_loaded{l}"), along(32 * (u + 1), i, 64))
                        for bank in (2, 3):
                            for f in range(2):
                                for c in range(DC):
                                    a = (c % 2) * 512 + (bank - 2) * EH + f * P
                                    w = gate2[:, 4 * (c // 2) + a // T, a % T:a % T + P]
                                    mm = pe.matmul(work[bank][:, f * T:(f + 1) * T], w, hf[:, c, :],
                                                   start=(c == 0), stop=(c == DC - 1))
                        mm.then_inc(s(f"spare_up{l}"), 1)
                        pe.wait_ge(s(f"spare_act{l}"), along(2 * (u + 1), i, 4))
                        for f in range(2):
                            for m in range(DC):
                                mm = pe.matmul(acc_c[:, m, :], spare_d[:, f, m * P:(m + 1) * P], pair_b[:, f, :],
                                               start=False, stop=False, skip_group_check=True)
                        mm.then_inc(s(f"spare_free{l}"), 1)
                    spare_units(pe, unit)
                pe.wait_ge(s("slots_clear"), l + 1)
                base = PAIRS * l
                pe.wait_ge(s("ht_low"), 4 * (l + 1))
                tok_hi = hhi[:, :, :].rearrange("p c t -> p (c t)")
                tok_lo = hlo[:, :, :].rearrange("p c t -> p (c t)")

                def event(what, p, k, i):
                    if what == "gu":
                        if k == 0:
                            pe.wait_ge(s("g_low"), along(2 * (base + p) + 2, i, 2))
                            if p > 0:
                                pe.wait_ge(s("mprod"), along(base + p, i, 1))
                        r = moe_tile(l, "gu", p, k)
                        h, lw = tile_ready(r, i, 12)
                        for c in range(2):
                            a = (2 * (k % 4) + c) * T + (k // 4) * P
                            x = (xghi[:, a:a + P], xglo[:, a:a + P])
                            w = (h[:, c * 512:(c + 1) * 512], lw[:, c * 512:(c + 1) * 512])
                            mm = product(work[0][:, :], [(x, w)], start=(k == 0 and c == 0),
                                         stop=(k == 7 and c == 1), skip=True)
                        mm.then_inc(s("pe_tile"), 1)
                    elif what == "d":
                        if k == 0:
                            pe.wait_ge(s("mt_low"), along(base + p + 1, i, 1))
                        r = moe_tile(l, "d", p, k)
                        h, lw = tile_ready(r, i, 12)
                        a = (k % 2) * T + (k // 2) * P
                        act_f = ahi[:, :, :].rearrange("p f t -> p (f t)")[:, a:a + P]
                        act_l = alo[:, :, :].rearrange("p f t -> p (f t)")[:, a:a + P]
                        for half in range(2):
                            c = slice(half * 512, (half + 1) * 512)
                            mm = product(work[2 + half][:, :], [((act_f, act_l), (h[:, c], lw[:, c]))],
                                         start=(k == 0), stop=(k == 3), skip=True)
                        mm.then_inc(s("pe_tile"), 1)
                    elif what == "G":
                        if k == 1 or p == 1:
                            pe.wait_ge(s("g_low"), along(2 * (base + p) + k, i, 2))
                        elif p > 1:
                            pe.wait_ge(s("mt_low"), along(base + p - 1, i, 1))
                        for c in range(4):
                            for q in range(QT):
                                sel = (select[:, q, p, :] if i is None else
                                       select[:, q, bass.ds(p + i, 1), :].rearrange("p o t -> p (o t)"))
                                a = q * D + (4 * k + c) * P
                                for j, tok in enumerate((tok_hi, tok_lo)):
                                    mm = pe.matmul(work[1][:, c * P:(c + 1) * P], tok[:, a:a + P], sel,
                                                   start=(q == 0 and j == 0), stop=(q == 1 and j == 1))
                        mm.then_inc(s("g_mm"), 1)
                    elif what == "T":
                        if p < PAIRS - 1:
                            pe.wait_ge(s("g_low"), along(2 * (base + p + 1) + 2, i, 2))
                        else:
                            pe.wait_ge(s("mt_low"), base + p)
                        pe.wait_ge(s("mprod"), along(base + p + 1, i, 1))
                        for f in range(2):
                            mm = pe.transpose(work[1][:, f * P:(f + 1) * P], pair_b[:, 0, f * P:(f + 1) * P], ident)
                        mm.then_inc(s("mt_mm"), 1)
                    elif what == "S":
                        pe.wait_ge(s("y_low"), along(2 * (base + p) + 2, i, 2))
                        sel = (selectT[:, p, :] if i is None else
                               selectT[:, bass.ds(p + i, 1), :].rearrange("p o t -> p (o t)"))
                        for m in range(DC):
                            for y in (yshi, yslo):
                                mm = pe.matmul(acc_c[:, m, :], y[:, m * P:(m + 1) * P], sel, start=False,
                                               stop=False, skip_group_check=True)
                        if p == PAIRS - 1:
                            mm.then_inc(s("moe_done"), 1)
                moe_events(pe, event)
            norm_sum(7 + 3 * LAYERS, 0)

        @block.scalar
        def _(act):
            done = [0, 0]

            def hi(n, i=None, turn=6):
                if n >= len(SPLITS) or n in held:
                    return
                tile_loaded(act, SPLITS[n], i, turn)
                if n >= AHEAD:
                    act.wait_ge(s("pe_tile"), along(SPLITS[n - AHEAD] + 1, i, turn))
                act.activation(whi[n % AHEAD][:], raw[SPLITS[n] % RAW][:], ACT.Copy).then_inc(s("hi_done"), 1)

            def evac(r, out, bank, func=ACT.Copy):
                act.wait_ge(s("pe_tile"), r + 1)
                src = work[bank][:, 0:T]
                if len(out.shape) == 3:
                    src = src.rearrange("p (q f) -> p q f", q=QT)
                assert EVAC[r] == done[0]
                act.activation(out, src, func).then_inc(s("tile_evac"), 1)
                done[0] += 1

            def squares(k, src, ready=None, count=0, out=None):
                if ready:
                    act.wait_ge(s(ready), count)
                dst = hf[:, :, :].rearrange("p c t -> p (c t)") if out is None else out
                act.activation(dst, src, ACT.Square).then_inc(s("norm_sq"), 1)

            def roots(k):
                act.wait_ge(s("norm_var"), k + 1)
                act.activation(std[:], var[:], ACT.Sqrt).then_inc(s("norm_std"), 1)

            def high_h(p, dst=None, unread=0):
                for j in range(2):
                    act.wait_ge(s("hf_done"), 2 * (p + unread) + j + 1)
                    act.activation((dst or hhi)[:, 4 * j:4 * j + 4, :], hf[:, 4 * j:4 * j + 4, :], ACT.Copy
                                   ).then_inc(s("h_high"), 1)

            def swiglu(stage):
                base = FIRST_F[stage]

                def step(r, what, f, i):
                    hi(NUMBER[r] + AHEAD, i)
                    if what == "u":
                        act.wait_ge(s("pe_tile"), along(r + 1, i, 6))
                        act.activation(pair_a[:, f % 2, :], work[2 * (f % 2)][:, 0:T], ACT.Silu
                                       ).then_inc(s("silu_done"), 1)
                swiglu_steps(act, stage, step)

            xflat = xT[:, :, :].rearrange("p c t -> p (c t)")
            act.wait_ge(s("x_loaded"), 16)
            squares(0, xflat)
            for n in range(AHEAD):
                hi(n)
            roots(0)
            high_h(0)
            act.wait_ge(s("mem_loaded"), 16)
            act.wait_ge(s("h_ready"), 2)
            squares(1, soft[:, :])
            roots(1)
            high_h(1, memhi)
            act.wait_ge(s("params_loaded"), 16)
            act.activation(c_act[:], par("c"), ACT.Silu).then_inc(s("c_ready"), 1)
            swiglu("ffn1")
            squares(2, acc[:, :], "pe_tile", START["memk"])
            roots(2)
            for m in range(4):
                r = START["memk"] + m
                hi(NUMBER[r] + AHEAD)
                evac(r, kmem[:, m, :], 1 + m % 3)
            squares(3, xflat, "x_ready", 1)
            roots(3)
            for m in range(4):
                r = START["memv"] + m
                hi(NUMBER[r] + AHEAD)
                evac(r, vmem[:, :, m * P:(m + 1) * P], 1 + m % 3)
                if m == 1:
                    high_h(2)
            act.wait_ge(s("small_mm"), 1)
            act.activation(small[:, :, 0:32], work[0][:, 0:64].rearrange("p (q f) -> p q f", q=QT), ACT.Copy
                           ).then_inc(s("small_ready"), 1)
            act.wait_ge(s("pads_ready"), 1)
            for m in range(12):
                r = START["dn"] + m
                hi(NUMBER[r] + AHEAD)
                if m >= 3:
                    act.wait_ge(s("conv_done"), m - 2)
                evac(r, convin[:, m % 3, 3:3 + T], m % 4)
            for m in range(4):
                r = START["z"] + m
                hi(NUMBER[r] + AHEAD)
                evac(r, zT[:, m, :], m % 4)
            for m in range(2):
                r = START["v"] + m
                hi(NUMBER[r] + AHEAD)
                evac(r, vtok[:, :, m * P:(m + 1) * P], m)
            for stage, dst in (("q", qT), ("kv", kvT), ("memq", qmem)):
                for m in range(4):
                    r = START[stage] + m
                    hi(NUMBER[r] + AHEAD)
                    evac(r, dst[:, m, :], (2 + m) % 4)
            for v in range(2):
                act.wait_ge(s("pe_tile"), START["w1"] + 4 * (v + 1))
                for m in range(2):
                    a = act.activation(hidden[:, v, m, :], work[2 * v + m][:, 0:30], ACT.Silu)
                a.then_inc(s("hidden_ready"), 1)
            act.wait_ge(s("conv_done"), 12)
            act.activation(dnc[:, :, :].rearrange("p c t -> p (c t)"), dnc[:, :, :].rearrange("p c t -> p (c t)"),
                           ACT.Silu)
            act.activation(zT[:, :, :].rearrange("p c t -> p (c t)"), zT[:, :, :].rearrange("p c t -> p (c t)"),
                           ACT.Silu).then_inc(s("z_silu"), 1)
            act.wait_ge(s("small_ready"), 1)
            act.activation(sm[:, 128:176].rearrange("p (q f) -> p q f", q=QT), small[:, :, 0:24], ACT.Sigmoid
                           ).then_inc(s("nsa_gates"), 1)
            act.activation(sm[:, 184:192].rearrange("p (q f) -> p q f", q=QT), small[:, :, 28:32], ACT.Sigmoid
                           ).then_inc(s("dn_beta"), 1)
            act.wait_ge(s("dn_absz"), 1)
            act.activation(sm[:, 32:40], sm[:, 24:32], ACT.Exp, scale=-1.0).then_inc(s("act_chain"), 1)
            act.wait_ge(s("act_chain"), 1)
            act.activation(sm[:, 40:48], sm[:, 32:40], ACT.Ln, bias=1.0).then_inc(s("act_chain"), 1)
            act.activation(sm[:, 48:52], par("a_log"), ACT.Exp).then_inc(s("dn_logs"), 1)

            def exps(g):
                act.wait_ge(s("sm_max"), g + 1)
                n = 16 if g == 1 else 8
                w = DC * T // n
                for u in range(n):
                    src = acc if g == 0 else soft
                    a = act.activation(soft[:, u * w:(u + 1) * w], src[:, u * w:(u + 1) * w], ACT.Exp,
                                       bias=sm[:, 64 + u:65 + u], scale=128 ** -0.5 if g == 0 else 1.0,
                                       accum_out=sm[:, 80 + u:81 + u])
                a.then_inc(s("sm_exp"), 1)

            def pt_evac(g):
                for r in range(4):
                    act.wait_ge(s("pt_mm"), 4 * g + r + 1)
                    act.activation(pt[:, r * 512:(r + 1) * 512], work[0][:, :], ACT.Copy).then_inc(s("pt_ready"), 1)

            def o_high(b, n):
                act.wait_ge(s("o_mm"), n)
                for j in range(2):
                    a = act.activation(ohi[:, b, 2 * j:2 * j + 2, :].rearrange("p c t -> p (c t)"),
                                       work[2 + j][:, :], ACT.Copy)
                    a.then_inc(s("o_high"), 1)

            act.wait_ge(s("tb_loaded"), 16)
            exps(0)
            act.wait_ge(s("cmp_mm"), 1)
            act.wait_ge(s("pads_ready"), 1)
            act.activation(kcmp[:, 0:NCMP], work[0][:, 0:NCMP], ACT.Copy).then_inc(s("cmp_kv"), 1)
            for j in range(HPG):
                act.activation(vcmp[32 * j:32 * j + NCMP, :, j, :],
                               work[0][32 * j:32 * j + NCMP, 64:64 + 2 * DH].rearrange("p (g d) -> p g d", d=DH),
                               ACT.Copy).then_inc(s("cmp_kv"), 1)
            pt_evac(0)
            o_high(2, 1)
            act.wait_ge(s("cmp_centred"), 1)
            act.activation(scmp[:, :, :].rearrange("p a b -> p (a b)"), scmp[:, :, :].rearrange("p a b -> p (a b)"),
                           ACT.Exp).then_inc(s("cmp_exp"), 1)
            act.wait_ge(s("pct_mm"), 1)
            act.activation(pt[:, 0:512], work[0][:, :], ACT.Copy).then_inc(s("pct_ready"), 1)
            exps(1)
            act.wait_ge(s("cmp_values"), 1)
            pt_evac(1)
            exps(2)
            pt_evac(2)
            exps(3)
            pt_evac(3)
            o_high(0, 2)

            act.wait_ge(s("olo_ready"), 4)
            flat_hf = hf[:, :, :].rearrange("p c t -> p (c t)")
            act.activation(flat_hf, dnc[:, 0:8, :].rearrange("p c t -> p (c t)"), ACT.Square
                           ).then_inc(s("dn_squares"), 1)
            act.wait_ge(s("dn_var"), 1)
            act.activation(flat_hf, flat_hf, ACT.Sqrt).then_inc(s("dn_root"), 1)
            act.wait_ge(s("dn_gc"), 1)
            act.activation(sm[:, 192:200], sm[:, 0:8], ACT.Exp).then_inc(s("dn_exp"), 1)
            act.wait_ge(s("dn_rest"), 1)
            act.activation(sm[:, 200:208], sm[:, 208:216], ACT.Exp).then_inc(s("dn_exp"), 1)
            act.wait_ge(s("dn_diff"), 2)
            act.activation(dn_el[:, :], dn_el[:, :], ACT.Exp, scale=-1.0).then_inc(s("dn_decays"), 1)
            act.activation(dn_eu[:, :], dn_eu[:, :], ACT.Exp).then_inc(s("dn_decays"), 1)
            act.activation(dn_qd[:, :], work[3][:, :], ACT.Exp).then_inc(s("dn_eg"), 1)
            act.wait_ge(s("dn_tok_mm"), after("dn_tok_mm", 1))
            act.wait_ge(s("dn_scales"), 1)
            for u in range(8):
                a = act.activation(dn_vb[:, u * P:(u + 1) * P], acc[:, (8 + u) * P:(9 + u) * P], ACT.Copy,
                                   scale=sm[:, 184 + u:185 + u])
            a.then_inc(s("dn_vtok"), 1)
            for lv in range(LEVELS):
                act.wait_ge(s("dn_z_mm"), lv + 1)
                act.activation(dn_z[:, :], acc[:, 0:8 * P], ACT.Copy).then_inc(s("dn_z"), 1)
            act.wait_ge(s("dn_vw_mm"), after("dn_vw_mm", 1))
            act.activation(dn_vn[:, 0:4 * P], acc[:, 0:4 * P], ACT.Copy).then_inc(s("dn_vw"), 1)
            act.activation(dn_w[:, :], acc[:, 4 * P:8 * P], ACT.Copy, scale=-1.0).then_inc(s("dn_vw"), 1)
            act.wait_ge(s("dn_state_mm"), after("dn_state_mm", 1))
            act.activation(dn_s[:, :], work[0][:, :], ACT.Copy).then_inc(s("dn_state"), 1)
            act.wait_ge(s("dn_v1_mm"), after("dn_v1_mm", 1))
            act.activation(dn_vn[:, 4 * P:8 * P], work[2][:, :], ACT.Copy).then_inc(s("dn_v1"), 1)
            act.wait_ge(s("dn_o_mm"), after("dn_o_mm", 1))
            act.activation(flat_hf[:, 0:4 * T], acc[:, 0:4 * T], ACT.Square).then_inc(s("dn_osq"), 1)
            act.wait_ge(s("dn_ovar"), 1)
            act.activation(flat_hf[:, 4 * T:8 * T], flat_hf[:, 4 * T:8 * T], ACT.Sqrt).then_inc(s("dn_oroot"), 1)

            first = sorted(held)
            held.clear()
            for n in first:
                hi(n)
            held.update(first)
            for m in range(24):
                r = START["gate"] + m
                hi(NUMBER[r] + AHEAD)
                if m == 0:
                    act.wait_ge(s("dn_o_scaled"), 1)
                evac(r, gates[:, m, :], m % 4, ACT.Sigmoid)
            for n in range(12):
                hi(NUMBER[START["branch"] + n] + AHEAD)
                if n % 3 == 2:
                    act.wait_ge(s("merged"), n // 3 + 1)
                    m = 2 * (n // 3)
                    act.activation(hhi[:, m:m + 2, :], hf[:, m:m + 2, :], ACT.Copy).then_inc(s("merged_high"), 1)
            for m in range(DC):
                hi(NUMBER[START["wout"] + m] + AHEAD)
            squares(4, acc[:, :], "pe_tile", START["wout"] + DC)
            roots(4)
            squares(5, xflat, "x_ready", 2)
            roots(5)
            high_h(3)
            swiglu("ffn2")
            squares(6, acc[:, :], "pe_tile", START["a0"])
            roots(6)
            for l in range(LAYERS):
                k = 7 + 3 * l
                squares(k, xflat, "x_ready", 3 + 2 * l)
                roots(k)
                high_h(4 + l, unread=l)
                for m in range(8):
                    r = START[f"a{l}"] + m
                    hi(NUMBER[r] + AHEAD)
                    if m >= 4:
                        act.wait_ge(s("glu_done"), 4 * l + m // 2 - 1)
                    evac(r, (pair_a, pair_b)[m % 2][:, (m // 2) % 2, :], m % 4, (ACT.Copy, ACT.Sigmoid)[m % 2])
                for m in range(4):
                    r = START[f"p{l}"] + m
                    hi(NUMBER[r] + AHEAD)
                    evac(r, ppad[:, m, 16:16 + T], m % 4)
                for m in range(16):
                    r = START[f"G{l}"] + m
                    hi(NUMBER[r] + AHEAD)
                    evac(r, gate2[:, m, :], m % 4, ACT.Sigmoid)
                hi(NUMBER[START[f"pool{l}"]] + AHEAD)
                act.wait_ge(s("ln_centred"), l + 1)
                squares(k + 1, yconv[:, :, :].rearrange("p c t -> p (c t)"), out=flat_hf[:, 0:4 * T])
                roots(k + 1)
                for m in range(4):
                    if m == 0:
                        act.wait_ge(s("ln_scaled"), l + 1)
                    a = act.activation(yconv[:, m, :], yconv[:, m, :], ACT.Silu, bias=col(f"ln_b{l}", m),
                                       scale=col(f"ln_g{l}", m))
                a.then_inc(s("y_silu"), 1)
                act.wait_ge(s("y_silu"), l + 1)
                act.activation(yhi[:, :, :], yconv[:, :, :], ACT.Copy).then_inc(s("y_high"), 1)
                for m in range(4):
                    hi(NUMBER[START[f"conv{l}"] + m] + AHEAD)
                    act.wait_ge(s("mixed"), 4 * l + m + 1)
                    act.activation(hhi[:, 2 * m:2 * m + 2, :], hf[:, 2 * m:2 * m + 2, :], ACT.Copy
                                   ).then_inc(s("mixed_high"), 1)
                for m in range(DC):
                    hi(NUMBER[START[f"wout{l}"] + m] + AHEAD)
                squares(k + 2, xflat, "x_ready", 4 + 2 * l)
                roots(k + 2)
                act.wait_ge(s("router_centred"), 2 * l + 1)
                act.activation(rt[:, 80:88], rt[:, 80:88], ACT.Exp).then_inc(s("router_exp"), 1)
                for b in range(4):
                    act.wait_ge(s("ht_mm"), 4 * l + b + 1)
                    act.activation(hhi[:, 2 * b:2 * b + 2, :].rearrange("p c t -> p (c t)"),
                                   acc[:, b * 512:(b + 1) * 512], ACT.Copy).then_inc(s("ht_high"), 1)
                    if b == 1:
                        act.wait_ge(s("router_centred"), 2 * l + 2)
                        act.activation(rt[:, 148:150], rt[:, 146:148], ACT.Exp).then_inc(s("router_exp"), 1)
                act.wait_ge(s("wslot_mm"), l + 1)
                wcols = work[0][:, 0:EXPERTS].rearrange("p (n j) -> p n j", j=2)
                for j in range(2):
                    act.activation(rt[64 * j:64 * j + 64, 576:576 + PAIRS], wcols[64 * j:64 * j + 64, :, j], ACT.Copy
                                   ).then_inc(s("wslot_read"), 1)
                for r in range(PAIRS // 2):
                    act.wait_ge(s("selectT_mm"), 8 * l + r + 1)
                    act.activation(selectT[:, 2 * r:2 * r + 2, :].rearrange("p c t -> p (c t)"),
                                   work[1 + r % 3][:, :], ACT.Copy).then_inc(s("selectT_ready"), 1)
                act.wait_ge(s("flag_ready"), l + 1)
                with act.If(act.value_load(overflow[0:1, l:l + 1], min_val=0, max_val=1) > 0):
                    def unit(u, gu, d, i):
                        act.wait_ge(s(f"spare_up{l}"), along(u + 1, i, 2))
                        act.activation(pair_a[:, :, :].rearrange("p f t -> p (f t)"), work[2][:, :], ACT.Silu
                                       ).then_inc(s(f"spare_silu{l}"), 1)
                    spare_units(act, unit)
                    act.wait_ge(s(f"spare_free{l}"), EXPERTS)
                base = PAIRS * l

                def event(what, p, k, i):
                    if what in ("gu", "d"):
                        hi(NUMBER[moe_tile(l, what, p, k)] + AHEAD, i, 12)
                    elif what == "A":
                        act.wait_ge(s("pe_tile"), along(moe_tile(l, "gu", p, 7) + 1, i, 12))
                        act.activation(pair_a[:, 0, :], work[0][:, 0:EH], ACT.Silu).then_inc(s("msilu"), 1)
                    elif what == "G":
                        act.wait_ge(s("g_mm"), along(2 * (base + p) + k + 1, i, 2))
                        act.activation(own_slots(xghi, 4 * k, 4), work[1][:, :].rearrange("p (c e s) -> p c e s", c=4, e=2),
                                       ACT.Copy).then_inc(s("g_high"), 1)
                    elif what == "Y":
                        act.wait_ge(s("pe_tile"), along(moe_tile(l, "d", p, 3) + 1, i, 12))
                        w = rt[:, 576 + p:577 + p] if i is None else rt[:, bass.ds(576 + p + i, 1)]
                        for half in range(2):
                            act.activation(yshi[:, half * 512:(half + 1) * 512], work[2 + half][:, :], ACT.Copy,
                                           scale=w).then_inc(s("y_high_moe"), 1)
                moe_events(act, event)
            k = 7 + 3 * LAYERS
            squares(k, xflat, "x_ready", 3 + 2 * LAYERS)
            roots(k)

        @block.vector
        def _(dve):
            n_own = [0]

            def own(ins):
                ins.then_inc(s("dve_own"), 1)
                n_own[0] += 1
                dve.wait_ge(s("dve_own"), n_own[0])

            def lo(n, i=None, turn=6):
                if n >= len(SPLITS) or n in held:
                    return
                dve.wait_ge(s("hi_done"), along(n + 1, i, turn))
                dve.tensor_tensor(wlo[n % AHEAD][:], raw[SPLITS[n] % RAW][:], whi[n % AHEAD][:].bitcast(F32),
                                  ALU.subtract).then_inc(s("lo_done"), 1)

            def variance(k, n, times=1.0, src=None):
                dve.wait_ge(s("norm_sum"), k + 1)
                dve.tensor_scalar(var[:], src if src is not None else work[0][:, 0:T], times ** 2 / n,
                                  times ** 2 * EPS, ALU.mult, ALU.add).then_inc(s("norm_var"), 1)

            def root_done(k):
                dve.wait_ge(s("norm_std"), k + 1)
                own(dve.reciprocal(rstd[:], std[:]))

            def rest_h(p, dst=None, src_hi=None):
                for j in range(2):
                    dve.wait_ge(s("h_high"), 2 * p + j + 1)
                    c = slice(4 * j, 4 * j + 4)
                    ins = dve.tensor_tensor((dst or hlo)[:, c, :], hf[:, c, :],
                                            (src_hi or hhi)[:, c, :].bitcast(F32), ALU.subtract)
                    ins.then_inc(s("mem_ready" if dst is not None else "h_ready"), 1)

            def normalise(src, gain):
                for m in range(DC):
                    ins = dve.scalar_tensor_tensor(hf[:, m, :], src(m), gain(m), rstd[:], ALU.mult, ALU.mult)
                    if m % 4 == 3:
                        ins.then_inc(s("hf_done"), 1)

            def modulated(src, scale, shift):
                for m in range(DC):
                    ins = dve.scalar_tensor_tensor(hf[:, m, :], src(m), scale(m), rstd[:], ALU.mult, ALU.mult)
                own(ins)
                for m in range(DC):
                    ins = dve.tensor_scalar(hf[:, m, :], hf[:, m, :], shift(m), None, ALU.add)
                    if m % 4 == 3:
                        ins.then_inc(s("hf_done"), 1)

            def add_branch(gain):
                for m in range(DC):
                    ins = dve.scalar_tensor_tensor(hf[:, m, :], acc_c[:, m, :], gain(m), rstd[:], ALU.mult, ALU.mult)
                own(ins)
                dve.tensor_tensor(xT[:, :, :], xT[:, :, :], hf[:, :, :], ALU.add).then_inc(s("x_ready"), 1)

            def swiglu(stage):
                base = FIRST_F[stage]
                per = 2
                start = n_own[0]

                def step(r, what, f, i):
                    lo(NUMBER[r] + AHEAD, i)
                    if what != "u":
                        return
                    p = f % 2
                    mine = start + per * f

                    def chain(ins, k):
                        ins.then_inc(s("dve_own"), 1)
                        dve.wait_ge(s("dve_own"), along(mine + k, i, 2 * per))
                    dve.wait_ge(s("silu_done"), along(base + f + 1, i, 2))
                    chain(dve.tensor_tensor(pair_b[:, p, :], work[2 * p + 1][:, 0:T], pair_a[:, p, :], ALU.mult), 1)
                    chain(dve.tensor_copy(ahi[:, p, :], pair_b[:, p, :]), per)
                    dve.tensor_tensor(alo[:, p, :], pair_b[:, p, :], ahi[:, p, :].bitcast(F32), ALU.subtract
                                      ).then_inc(s("act_ready"), 1)
                swiglu_steps(dve, stage, step)
                n_own[0] = start + per * LOOPED[stage]

            def x_chunk(m):
                return xT[:, m, :]

            dve.memset(zero[:], 0.0).then_inc(s("zero_ready"), 1)
            dve.wait_ge(s("params_loaded"), 16)
            dve.wait_ge(s("x_loaded"), 16)
            for n in range(AHEAD):
                lo(n)
            variance(0, D)
            root_done(0)
            normalise(x_chunk, lambda m: col("ffn1_pre", m))
            rest_h(0)
            variance(1, D, src=work[1][:, 0:T])
            root_done(1)
            normalise(lambda m: soft[:, m * T:(m + 1) * T], lambda m: col("mem_norm", m))
            rest_h(1, memlo, memhi)
            dve.wait_ge(s("consts_loaded"), 16)
            for h in range(HEADS):
                dve.wait_ge(s("bias_mm"), h + 1)
                if h == HEADS // 2:
                    dve.wait_ge(s("rows_stored"), 16)
                a = (h % 4) * BROW
                dve.tensor_tensor(soft[:, a:a + BROW], work[h % 4][:, 0:BROW], const("maskrow"), ALU.add
                                  ).then_inc(s("bias_rows"), 1)
            swiglu("ffn1")
            variance(2, D, 2.0)
            root_done(2)
            add_branch(lambda m: col("ffn1_post", m))
            for m in range(4):
                lo(NUMBER[START["memk"] + m] + AHEAD)
            variance(3, D)
            root_done(3)
            normalise(x_chunk, lambda m: col("mix_pre", m))
            for m in range(4):
                lo(NUMBER[START["memv"] + m] + AHEAD)
                if m == 1:
                    rest_h(2)
            dve.wait_ge(s("tile_evac"), EVAC[START["memv"] + 3] + 1)
            dve.memset(convin[:, :, 0:3], 0.0)
            dve.memset(scmp[:], NEG)
            dve.memset(vcmp[:], 0.0)
            dve.memset(pcmp[:], 0.0).then_inc(s("pads_ready"), 1)
            for m in range(12):
                lo(NUMBER[START["dn"] + m] + AHEAD)
                evacuated(dve, "dn", m)
                src = convin[:, m % 3, :]
                own(dve.tensor_scalar(dnc[:, m, :], src[:, 3:3 + T], col("dn_conv", 4 * m + 3), None, ALU.mult))
                for i in range(3):
                    ins = dve.scalar_tensor_tensor(dnc[:, m, :], src[:, i:i + T], col("dn_conv", 4 * m + i),
                                                   dnc[:, m, :], ALU.mult, ALU.add)
                    if i < 2:
                        own(ins)
                ins.then_inc(s("conv_done"), 1)
            for stage, count in (("z", 4), ("v", 2), ("q", 4), ("kv", 4), ("memq", 4)):
                for m in range(count):
                    lo(NUMBER[START[stage] + m] + AHEAD)
            evacuated(dve, "kv", 1)
            flat = hf[:, :, :].rearrange("p c t -> p (c t)")[:, 0:2 * 16 * 30].rearrange(
                "p (v j g c) -> p v j g c", v=2, j=16, g=GROUPS)
            for v in range(2):
                for g in range(GROUPS):
                    for jp in range(2):
                        base = kvT[DH * g:DH * g + DH, v, jp:jp + 1]
                        src = spread(base, (16, NCMP), (2, CMP_STRIDE))
                        ins = dve.tensor_copy(flat[DH * jp:DH * jp + DH, v, :, g, :], src)
            own(ins)
            for v in range(2):
                pos = spread(par(("posk", "posv")[v])[:, 0:1], (16, 2 * NCMP), (1, 0))
                out = flat[:, v, :, :, :].rearrange("p j g c -> p j (g c)")
                ins = dve.tensor_tensor(out, out, pos, ALU.add)
            ins.then_inc(s("flat_ready"), 1)
            dve.wait_ge(s("small_ready"), 1)
            own(dve.tensor_tensor(sm[:, 52:60].rearrange("p (q f) -> p q f", q=QT), small[:, :, 24:28],
                                  spread(par("dt_bias"), (QT, 4), (0, 1)), ALU.add))
            own(dve.tensor_scalar(sm[:, 216:224], sm[:, 52:60], -1.0, None, ALU.mult))
            dve.tensor_tensor(sm[:, 24:32], sm[:, 52:60], sm[:, 216:224], ALU.max).then_inc(s("dn_absz"), 1)
            dve.wait_ge(s("dn_logs"), 1)
            own(dve.scalar_tensor_tensor(sm[:, 216:224], sm[:, 52:60], 0.0, sm[:, 40:48], ALU.max, ALU.add))
            dve.scalar_tensor_tensor(sm[:, 16:24].rearrange("p (q f) -> p q f", q=QT),
                                     sm[:, 216:224].rearrange("p (q f) -> p q f", q=QT), -1.0,
                                     spread(sm[:, 48:49], (QT, 4), (0, 1)), ALU.mult, ALU.mult
                                     ).then_inc(s("dn_decay"), 1)

            def maxima(g):
                dve.wait_ge(s("sm_scores"), g + 1)
                n = 16 if g == 1 else 8
                if g == 0:
                    own(dve.tensor_reduce(sm[:, 96:104], acc_c, X_AXIS, ALU.max))
                    dve.tensor_scalar(sm[:, 64:72], sm[:, 96:104], -(128 ** -0.5), None, ALU.mult
                                      ).then_inc(s("sm_max"), 1)
                    return
                if g == 1:
                    dve.wait_ge(s("tb_loaded"), 16)
                dve.wait_ge(s("pt_mm"), 4 * g)
                if g == 1:
                    for br in range(2):
                        a = slice(br * HEADS * P, (br + 1) * HEADS * P)
                        ins = dve.scalar_tensor_tensor(soft[:, a].rearrange("p (h k) -> p h k", k=P),
                                                       acc[:, a].rearrange("p (h k) -> p h k", k=P), DH ** -0.5,
                                                       tb[:, :, P:T], ALU.mult, ALU.add)
                        ins.then_inc(s("sm_bias"), 1)
                else:
                    dve.scalar_tensor_tensor(soft[:, :], acc[:, :], DH ** -0.5,
                                             tb[:, :, :].rearrange("p h t -> p (h t)"), ALU.mult, ALU.add
                                             ).then_inc(s("sm_bias"), 1)
                dve.wait_ge(s("sm_bias"), g + 1)
                dve.tensor_reduce(sm[:, 64:64 + n], soft[:, :].rearrange("p (u k) -> p u k", u=n), X_AXIS, ALU.max,
                                  negate=True).then_inc(s("sm_max"), 1)

            def probs(g, gate):
                dve.wait_ge(s("sm_exp"), g + 1)
                n = 16 if g == 1 else 8
                own(dve.reciprocal(sm[:, 96:96 + n], sm[:, 80:80 + n]))
                if gate is not None:
                    own(dve.tensor_tensor(sm[:, 96:96 + n], sm[:, 96:96 + n], gate, ALU.mult))
                for j in range(2):
                    a = soft[:, j * 1024:(j + 1) * 1024].rearrange("p (u k) -> p u k", u=n // 2)
                    r = spread(sm[:, 96 + j * n // 2:97 + j * n // 2], (n // 2, DC * T // n), (1, 0))
                    dve.tensor_tensor(a, a, r, ALU.mult).then_inc(s("sm_probs"), 1)

            def o_low(b, k):
                for j in range(2):
                    dve.wait_ge(s("o_high"), k + j + 1)
                    dve.tensor_tensor(olo[:, b, 2 * j:2 * j + 2, :].rearrange("p c t -> p (c t)"), work[2 + j][:, :],
                                      ohi[:, b, 2 * j:2 * j + 2, :].rearrange("p c t -> p (c t)").bitcast(F32),
                                      ALU.subtract).then_inc(s("olo_ready"), 1)

            maxima(0)
            probs(0, None)
            o_low(2, 0)
            dve.wait_ge(s("tb_loaded"), 16)
            dve.wait_ge(s("cmp_scores"), 1)
            for q in range(QT):
                for g in range(GROUPS):
                    n, at = (NCMP0, P + 31) if q == 0 else (NCMP, 31)
                    u = q * HEADS + g * HPG
                    cs = acc[:, g * 512 + q * 64:g * 512 + (q + 1) * 64].rearrange("p (j c) -> p j c", c=16)
                    dve.scalar_tensor_tensor(scmp[:, u:u + HPG, 0:n], cs[:, :, 0:n], DH ** -0.5,
                                             spread(tb[:, g * HPG, at:at + 1], (HPG, n), (T, CMP_STRIDE)),
                                             ALU.mult, ALU.add).then_inc(s("cmp_bias"), 1)
            dve.wait_ge(s("cmp_bias"), 4)
            dve.tensor_reduce(sm[:, 112:128], scmp[:], X_AXIS, ALU.max).then_inc(s("cmp_bias"), 1)
            dve.wait_ge(s("cmp_bias"), 5)
            dve.tensor_tensor(scmp[:], scmp[:], spread(sm[:, 112:113], (16, 16), (1, 0)), ALU.subtract
                              ).then_inc(s("cmp_centred"), 1)
            dve.wait_ge(s("cmp_exp"), 1)
            own(dve.tensor_reduce(sm[:, 224:240], scmp[:], X_AXIS, ALU.add))
            own(dve.reciprocal(sm[:, 112:128], sm[:, 224:240]))
            dve.wait_ge(s("nsa_gates"), 1)
            gv = sm[:, 128:176].rearrange("p (q f) -> p q f", q=QT)
            r16 = sm[:, 112:128].rearrange("p (q h) -> p q h", q=QT)
            own(dve.tensor_tensor(r16, r16, gv[:, :, 0:HEADS], ALU.mult))
            own(dve.tensor_tensor(r16, r16, spread(const("has_block")[:, 0:1], (QT, HEADS), (1, 0)), ALU.mult))
            dve.tensor_tensor(pcmp[:, :, :, 0:16].rearrange("p a j c -> p (a j) c"), scmp[:],
                              spread(sm[:, 112:113], (16, 16), (1, 0)), ALU.mult).then_inc(s("cmp_probs"), 1)
            maxima(1)
            probs(1, gv[:, 0, 8:24])
            maxima(2)
            probs(2, gv[:, 1, 8:16])
            maxima(3)
            probs(3, gv[:, 1, 16:24])
            o_low(0, 2)

            dve.wait_ge(s("dn_sums"), after("dn_sums", 1))
            flat_hf = hf[:, :, :].rearrange("p c t -> p (c t)")
            dve.tensor_scalar(flat_hf, acc[:, :], EPS, None, ALU.add).then_inc(s("dn_var"), 1)
            dve.wait_ge(s("dn_root"), after("dn_root", 1))
            own(dve.reciprocal(flat_hf, flat_hf))
            dqk = dnc[:, 0:8, :].rearrange("p c t -> p (c t)")
            dve.tensor_tensor(dqk, dqk, flat_hf, ALU.mult).then_inc(s("dn_unit"), 1)
            dve.wait_ge(s("dn_gc_mm"), after("dn_gc_mm", 1))
            dve.tensor_copy(sm[:, 0:16], work[0][:, 0:16]).then_inc(s("dn_gc"), 1)
            dve.wait_ge(s("dn_gc"), 1)
            dve.tensor_tensor(sm[:, 208:216], sm[:, 8:16], sm[:, 0:8], ALU.subtract).then_inc(s("dn_rest"), 1)
            dve.wait_ge(s("dn_rows_mm"), after("dn_rows_mm", 1))
            for dst, op in ((dn_el, ALU.max), (dn_eu, ALU.min)):
                for u in range(8):
                    ins = dve.tensor_scalar(dst[:, u * P:(u + 1) * P], work[2 + u // 4][:, (u % 4) * P:(u % 4 + 1) * P],
                                            sm[:, u:u + 1], 0.0, ALU.subtract, op)
                ins.then_inc(s("dn_diff"), 1)
            idn = spread(ident[:, 0:1], (8, P), (0, 1))
            dve.tensor_copy(dn_inv[:, :].rearrange("p (u k) -> p u k", k=P), idn)
            dve.tensor_copy(dn_invT[:, :].rearrange("p (u k) -> p u k", k=P), idn).then_inc(s("dn_ident"), 1)
            dve.wait_ge(s("dn_exp"), after("dn_exp", 2))
            dve.wait_ge(s("dn_beta"), 1)
            dve.tensor_tensor(sm[:, 216:224], sm[:, 184:192], sm[:, 192:200], ALU.mult).then_inc(s("dn_scales"), 1)
            dve.wait_ge(s("dn_decays"), after("dn_decays", 2))
            dve.wait_ge(s("dn_kq_mm"), after("dn_kq_mm", 1))
            for u in range(8):
                a = slice(u * P, (u + 1) * P)
                ins = dve.scalar_tensor_tensor(dn_a[:, a], acc[:, a], sm[:, 184 + u:185 + u], dn_el[:, a],
                                               ALU.mult, ALU.mult)
            ins.then_inc(s("dn_kq"), 1)
            dve.scalar_tensor_tensor(dn_qk[:, :], acc[:, 8 * P:16 * P], P ** -0.5, dn_eu[:, :], ALU.mult, ALU.mult
                                     ).then_inc(s("dn_kq"), 1)
            dve.wait_ge(s("dn_kq"), 2)
            qk3 = dn_qk[:, :].rearrange("p (u k) -> p u k", k=P)
            own(dve.tensor_tensor(qk3, qk3, spread(upper[:, 0:1], (8, P), (0, 1)), ALU.mult))
            dve.wait_ge(s("dn_eg"), after("dn_eg", 1))
            own(dve.scalar_tensor_tensor(dn_qd[:, :].rearrange("p (h t) -> p h t", t=P),
                                         dn_qd[:, :].rearrange("p (h t) -> p h t", t=P), P ** -0.5,
                                         dnc[:, 0:4, P:T], ALU.mult, ALU.mult))
            dve.wait_ge(s("dn_tok_mm"), after("dn_tok_mm", 1))
            for u in range(8):
                ins = dve.tensor_scalar(dn_kb[:, u * P:(u + 1) * P], acc[:, u * P:(u + 1) * P],
                                        sm[:, 216 + u:217 + u], None, ALU.mult)
            ins.then_inc(s("dn_tok"), 1)
            for u in range(4):
                ins = dve.tensor_scalar(dn_kd[:, u * P:(u + 1) * P], acc[:, u * P:(u + 1) * P],
                                        sm[:, 200 + u:201 + u], None, ALU.mult)
            ins.then_inc(s("dn_tok"), 1)
            dve.wait_ge(s("dn_vtok"), after("dn_vtok", 1))
            dve.nop().then_inc(s("dn_tok"), 1)
            for lv in range(LEVELS):
                mask = spread(const("levels")[:, lv * P:lv * P + 1], (8, P), (0, 1))
                dve.wait_ge(s("dn_kq"), 2)
                if lv == 0:
                    dve.wait_ge(s("dn_ident"), 1)
                dve.tensor_tensor(dn_b[:, :].rearrange("p (u k) -> p u k", k=P),
                                  dn_a[:, :].rearrange("p (u k) -> p u k", k=P), mask, ALU.mult
                                  ).then_inc(s("dn_level"), 1)
                dve.wait_ge(s("dn_x_mm"), lv + 1)
                dve.tensor_tensor(dn_inv[:, :], dn_inv[:, :], acc[:, 8 * P:16 * P], ALU.subtract
                                  ).then_inc(s("dn_update"), 1)
                for j in range(2):
                    a = slice(j * 512, (j + 1) * 512)
                    ins = dve.tensor_tensor(dn_invT[:, a], dn_invT[:, a], work[2 + j][:, :], ALU.subtract)
                ins.then_inc(s("dn_update"), 1)
                dve.wait_ge(s("dn_update"), 2 * lv + 2)
            dve.wait_ge(s("dn_osum"), after("dn_osum", 1))
            dve.tensor_scalar(flat_hf[:, 4 * T:8 * T], acc[:, 4 * T:8 * T], 1.0 / P, EPS, ALU.mult, ALU.add
                              ).then_inc(s("dn_ovar"), 1)
            dve.wait_ge(s("dn_oroot"), after("dn_oroot", 1))
            own(dve.reciprocal(flat_hf[:, 4 * T:8 * T], flat_hf[:, 4 * T:8 * T]))
            own(dve.scalar_tensor_tensor(flat_hf[:, 0:4 * T], acc[:, 0:4 * T], col("dn_norm", 0),
                                         flat_hf[:, 4 * T:8 * T], ALU.mult, ALU.mult))
            dve.wait_ge(s("z_silu"), 1)
            own(dve.tensor_tensor(flat_hf[:, 0:4 * T], flat_hf[:, 0:4 * T],
                                  zT[:, :, :].rearrange("p c t -> p (c t)"), ALU.mult))
            own(dve.tensor_copy(ohi[:, 1, :, :].rearrange("p c t -> p (c t)"), flat_hf[:, 0:4 * T]))
            dve.tensor_tensor(olo[:, 1, :, :].rearrange("p c t -> p (c t)"), flat_hf[:, 0:4 * T],
                              ohi[:, 1, :, :].rearrange("p c t -> p (c t)").bitcast(F32), ALU.subtract
                              ).then_inc(s("olo_ready"), 1)
            dve.wait_ge(s("olo_ready"), 5)
            dve.nop().then_inc(s("olo_ready"), 1)
            dve.nop().then_inc(s("dn_out"), 1)
            dve.nop().then_inc(s("dn_o_scaled"), 1)

            dve.wait_ge(s("pe_tile"), START["gate"])
            for l in range(LAYERS):
                ins = dve.tensor_tensor(mod[:, l * 48:(l + 1) * 48], work[1][:, l * 48:(l + 1) * 48],
                                        par(f"b_ada{l}"), ALU.add)
            ins.then_inc(s("mod_ready"), 1)
            dve.wait_ge(s("mod_ready"), 1)
            for l in range(LAYERS):
                for j, name in enumerate(("norm", "ffn_norm")):
                    a = l * 48 + (1, 4)[j] * DC
                    ins = dve.scalar_tensor_tensor(gscale[:, (2 * l + j) * DC:(2 * l + j + 1) * DC], mod[:, a:a + DC],
                                                   1.0, par(f"{name}{l}"), ALU.add, ALU.mult)
            own(ins)

            def mod_col(l, part, m):
                a = l * 48 + part * DC + m
                return mod[:, a:a + 1]

            def gs_col(l, j, m):
                a = (2 * l + j) * DC + m
                return gscale[:, a:a + 1]

            first = sorted(held)
            held.clear()
            for n in first:
                lo(n)
            held.update(first)
            for m in range(24):
                lo(NUMBER[START["gate"] + m] + AHEAD)
            for n in range(12):
                r = START["branch"] + n
                m, b = STREAM[r][1]
                lo(NUMBER[r] + AHEAD)
                dve.wait_ge(s("pe_tile"), r + 1)
                evacuated(dve, "gate", 23)
                g = gates[:, b * DC + 2 * m:b * DC + 2 * m + 2, :].rearrange("p c t -> p (c t)")
                out = hf[:, 2 * m:2 * m + 2, :].rearrange("p c t -> p (c t)")
                if b == 0:
                    dve.tensor_tensor(out, work[n % 4][:, :], g, ALU.mult).then_inc(s("branch_read"), 1)
                    dve.wait_ge(s("branch_read"), n + 1)
                    continue
                dve.tensor_tensor(g, work[n % 4][:, :], g, ALU.mult).then_inc(s("branch_read"), 1)
                dve.wait_ge(s("branch_read"), n + 1)
                ins = dve.tensor_tensor(out, out, g, ALU.add)
                if b == 1:
                    own(ins)
                    continue
                ins.then_inc(s("merged"), 1)
                dve.wait_ge(s("merged_high"), m + 1)
                dve.tensor_tensor(hlo[:, 2 * m:2 * m + 2, :], hf[:, 2 * m:2 * m + 2, :],
                                  hhi[:, 2 * m:2 * m + 2, :].bitcast(F32), ALU.subtract).then_inc(s("merged_ready"), 1)
            for m in range(DC):
                lo(NUMBER[START["wout"] + m] + AHEAD)
            variance(4, D)
            root_done(4)
            add_branch(lambda m: col("mix_post", m))
            variance(5, D)
            root_done(5)
            normalise(x_chunk, lambda m: col("ffn2_pre", m))
            rest_h(3)
            swiglu("ffn2")
            variance(6, D, 2.0)
            root_done(6)
            add_branch(lambda m: col("ffn2_post", m))

            dve.tensor_copy(identr[:], ident)
            dve.memset(vpad[:, :, 0:30], 0.0)
            own(dve.memset(ppad[:, :, 0:16], 0.0))
            for l in range(LAYERS):
                k = 7 + 3 * l
                variance(k, D)
                root_done(k)
                modulated(x_chunk, lambda m: gs_col(l, 0, m), lambda m: mod_col(l, 0, m))
                rest_h(4 + l)
                taps = []

                def tap_ops(c):
                    def tap(i):
                        def run():
                            w = col(f"conv_w{l}", c * CONV_K + i)
                            if i == 0:
                                own(dve.tensor_scalar(yconv[:, c, :], vpad[:, c, 0:T], w, col(f"conv_b{l}", c),
                                                      ALU.mult, ALU.add))
                            else:
                                own(dve.scalar_tensor_tensor(yconv[:, c, :], vpad[:, c, i:i + T], w, yconv[:, c, :],
                                                             ALU.mult, ALU.add))
                        return run
                    return [tap(i) for i in range(CONV_K)]

                def some_taps(n):
                    for _ in range(min(n, len(taps))):
                        taps.pop(0)()

                for m in range(8):
                    lo(NUMBER[START[f"a{l}"] + m] + AHEAD)
                    if m % 2:
                        c = m // 2
                        evacuated(dve, f"a{l}", m)
                        dve.tensor_tensor(vpad[:, c, 30:30 + T], pair_a[:, c % 2, :], pair_b[:, c % 2, :], ALU.mult
                                          ).then_inc(s("glu_done"), 1)
                        dve.wait_ge(s("glu_done"), 4 * l + c + 1)
                        taps += tap_ops(c)
                    some_taps(4)
                for m in range(4):
                    lo(NUMBER[START[f"p{l}"] + m] + AHEAD)
                    some_taps(5)
                evacuated(dve, f"p{l}", 3)
                for g, w in enumerate(WINDOWS):
                    src, reach = ppad[:, g, :], 1
                    bufs = [flat_hf[:, 0:16 + T], flat_hf[:, 512:528 + T]]
                    while reach < w:
                        a = 2 * reach - 1
                        dst = bufs.pop(0)
                        bufs.append(dst)
                        own(dve.tensor_tensor(dst[:, a:16 + T], src[:, a:16 + T], src[:, a - reach:16 + T - reach],
                                              ALU.add))
                        src, reach = dst, 2 * reach
                    mean = flat_hf[:, 1024:1024 + T]
                    own(dve.tensor_scalar(mean, src[:, 16:16 + T], 1.0 / w, None, ALU.mult))
                    own(dve.tensor_tensor(mean[:, 0:16], src[:, 16:32], const("inv_count")[:, 16 * g:16 * g + 16], ALU.mult))
                    own(dve.tensor_tensor(mean, mean, ppad[:, g, 16:16 + T], ALU.subtract))
                    own(dve.tensor_copy(phi[:, g, :], mean))
                    ins = dve.tensor_tensor(plo[:, g, :], mean, phi[:, g, :].bitcast(F32), ALU.subtract)
                    if g < 3:
                        own(ins)
                ins.then_inc(s("pooled"), 1)
                for m in range(16):
                    lo(NUMBER[START[f"G{l}"] + m] + AHEAD)
                    some_taps(6)
                some_taps(len(taps))
                dve.nop().then_inc(s("conv_done2"), 1)
                lo(NUMBER[START[f"pool{l}"]] + AHEAD)
                dve.wait_ge(s("ln_mean"), l + 1)
                dve.scalar_tensor_tensor(yconv[:], spread(work[0][:, 0:1], (4, T), (0, 1)), -1.0 / 512, yconv[:],
                                         ALU.mult, ALU.add).then_inc(s("ln_centred"), 1)
                variance(k + 1, 512, src=work[1][:, 0:T])
                root_done(k + 1)
                dve.tensor_tensor(yconv[:], yconv[:], spread(rstd[:, 0:1], (4, T), (0, 1)), ALU.mult
                                  ).then_inc(s("ln_scaled"), 1)
                dve.wait_ge(s("pe_tile"), START[f"pool{l}"] + 1)
                evacuated(dve, f"G{l}", 15)
                for m in range(DC):
                    ins = dve.scalar_tensor_tensor(hf[:, m, :], acc_c[:, m, :], col(f"pool_scale{l}", m),
                                                   gate2[:, DC + m, :], ALU.mult, ALU.mult)
                ins.then_inc(s("pool_read"), 1)
                dve.wait_ge(s("y_high"), l + 1)
                dve.tensor_tensor(ylo[:], yconv[:], yhi[:].bitcast(F32), ALU.subtract).then_inc(s("y_ready"), 1)
                for m in range(4):
                    lo(NUMBER[START[f"conv{l}"] + m] + AHEAD)
                    dve.wait_ge(s("pe_tile"), START[f"conv{l}"] + m + 1)
                    for j in range(2):
                        c = 2 * m + j
                        ins = dve.scalar_tensor_tensor(gate2[:, c, :], work[m][:, j * T:(j + 1) * T],
                                                       col(f"b_out{l}", c), gate2[:, c, :], ALU.add, ALU.mult)
                    ins.then_inc(s("conv_read"), 1)
                    dve.wait_ge(s("conv_read"), 4 * l + m + 1)
                    c = slice(2 * m, 2 * m + 2)
                    dve.tensor_tensor(hf[:, c, :], hf[:, c, :], gate2[:, c, :], ALU.add).then_inc(s("mixed"), 1)
                    dve.wait_ge(s("mixed_high"), 4 * l + m + 1)
                    dve.tensor_tensor(hlo[:, c, :], hf[:, c, :], hhi[:, c, :].bitcast(F32), ALU.subtract
                                      ).then_inc(s("mixed_ready"), 1)
                for m in range(DC):
                    lo(NUMBER[START[f"wout{l}"] + m] + AHEAD)
                dve.wait_ge(s("pe_tile"), START[f"wout{l}"] + DC)
                for m in range(DC):
                    ins = dve.scalar_tensor_tensor(xT[:, m, :], acc_c[:, m, :], mod_col(l, 2, m), xT[:, m, :],
                                                   ALU.mult, ALU.add)
                ins.then_inc(s("x_ready"), 1)
                variance(k + 2, D)
                root_done(k + 2)
                modulated(x_chunk, lambda m: gs_col(l, 1, m), lambda m: mod_col(l, 3, m))

                def v3(a, n, w=QT):
                    return rt[:, a:a + w * n].rearrange("p (q f) -> p q f", q=w)
                rl = v3(0, 36)
                dve.wait_ge(s("router_mm"), l + 1)
                dve.tensor_tensor(rl, work[1][:, 0:72].rearrange("p (q f) -> p q f", q=QT),
                                  spread(par(f"router_b{l}"), (QT, 36), (0, 1)), ALU.add).then_inc(s("router_read"), 1)
                dve.wait_ge(s("router_read"), l + 1)

                def first_max(out, scores, top, iota, n, eq, at):
                    own(dve.tensor_tensor(v3(eq, n), scores, spread(top, (QT, n), (1, 0)), ALU.is_equal))
                    own(dve.tensor_tensor(v3(eq, n), v3(eq, n), spread(iota[:, 0:1], (QT, n), (0, 1)), ALU.mult))
                    own(dve.tensor_reduce(rt[:, at:at + QT], v3(eq, n), X_AXIS, ALU.min))
                    own(dve.tensor_tensor(v3(out, n), spread(iota[:, 0:1], (QT, n), (0, 1)),
                                          spread(rt[:, at:at + 1], (QT, n), (1, 0)), ALU.is_equal))

                own(dve.tensor_reduce(rt[:, 72:74], rl[:, :, 0:4], X_AXIS, ALU.max))
                dve.tensor_tensor(v3(80, 4), rl[:, :, 0:4], spread(rt[:, 72:73], (QT, 4), (1, 0)), ALU.subtract
                                  ).then_inc(s("router_centred"), 1)
                first_max(88, rl[:, :, 0:4], rt[:, 72:73], const("iota4"), 4, 96, 74)
                for q in range(QT):
                    el = rt[:, q * 36 + 4:q * 36 + 36].rearrange("p (g e) -> p g e", e=EPG)
                    ins = dve.tensor_tensor(rt[:, 320 + 32 * q:352 + 32 * q].rearrange("p (g e) -> p g e", e=EPG), el,
                                            spread(rt[:, 88 + 4 * q:89 + 4 * q], (EGROUPS, EPG), (1, 0)), ALU.mult)
                own(ins)
                for q in range(QT):
                    ins = dve.tensor_reduce(rt[:, 104 + 8 * q:112 + 8 * q],
                                            spread(rt[:, 320 + 32 * q:321 + 32 * q], (EPG, EGROUPS), (1, EPG)),
                                            X_AXIS, ALU.add)
                own(ins)
                ig = v3(104, 8)
                own(dve.tensor_reduce(rt[:, 142:144], ig, X_AXIS, ALU.max))
                first_max(120, ig, rt[:, 142:143], const("iota8"), 8, 160, 76)
                own(dve.scalar_tensor_tensor(rt[:, 176:192], rt[:, 120:136], NEG, rt[:, 104:120], ALU.mult, ALU.add))
                own(dve.tensor_reduce(rt[:, 144:146], v3(176, 8), X_AXIS, ALU.max))
                dve.tensor_tensor(rt[:, 146:148], rt[:, 144:146], rt[:, 142:144], ALU.subtract
                                  ).then_inc(s("router_centred"), 1)
                first_max(192, v3(176, 8), rt[:, 144:145], const("iota8"), 8, 160, 78)
                own(dve.tensor_tensor(rt[:, 208:224], rt[:, 120:136], rt[:, 192:208], ALU.add))

                def per_expert(out, of_group, of_place):
                    for q in range(QT):
                        ins = dve.tensor_tensor(
                            rt[:, out + 32 * q:out + 32 + 32 * q].rearrange("p (g e) -> p g e", e=EPG),
                            spread(rt[:, of_group + 4 * q:of_group + 1 + 4 * q], (EGROUPS, EPG), (1, 0)),
                            spread(rt[:, of_place + 8 * q:of_place + 1 + 8 * q], (EGROUPS, EPG), (0, 1)), ALU.mult)
                    return ins
                per_expert(384, 88, 208).then_inc(s("mask_ready"), 1)
                dve.wait_ge(s("router_exp"), 2 * l + 2)
                own(dve.tensor_reduce(rt[:, 150:152], v3(80, 4), X_AXIS, ALU.add))
                own(dve.scalar_tensor_tensor(rt[:, 152:154], rt[:, 148:150], 1.0, rt[:, 150:152], ALU.add, ALU.mult))
                own(dve.reciprocal(rt[:, 154:156], rt[:, 152:154]))
                own(dve.tensor_tensor(v3(192, 8), v3(192, 8), spread(rt[:, 148:149], (QT, 8), (1, 0)), ALU.mult))
                own(dve.tensor_tensor(rt[:, 120:136], rt[:, 120:136], rt[:, 192:208], ALU.add))
                own(dve.tensor_tensor(v3(120, 8), v3(120, 8), spread(rt[:, 154:155], (QT, 8), (1, 0)), ALU.mult))
                own(per_expert(256, 88, 120))
                dve.wait_ge(s("rank_mm"), l + 1)
                own(dve.tensor_tensor(rt[:, 448:512], work[1][:, 0:64], rt[:, 384:448], ALU.mult))
                dve.tensor_reduce(rt[:, 592:593], work[1][:, 64:96], X_AXIS, ALU.max).then_inc(s("rank_read"), 1)
                own(dve.tensor_scalar(rt[:, 448:512], rt[:, 448:512], -1.0, None, ALU.add))
                for q in range(QT):
                    dve.tensor_tensor(select[:, q, :, :].rearrange("p n (j c) -> p (n j) c", j=2),
                                      spread(const("slots")[:, 0:1], (EXPERTS, SLOTS), (0, 1)),
                                      spread(rt[:, 448 + 32 * q:449 + 32 * q], (EXPERTS, SLOTS), (1, 0)), ALU.is_equal)
                own(dve.tensor_copy(chi[:], rt[:, 256:320]))
                dve.tensor_tensor(clo[:], rt[:, 256:320], chi[:].bitcast(F32), ALU.subtract
                                  ).then_inc(s("slots_ready"), 1)
                for b in range(4):
                    dve.wait_ge(s("ht_high"), 4 * l + b + 1)
                    dve.tensor_tensor(hlo[:, 2 * b:2 * b + 2, :].rearrange("p c t -> p (c t)"),
                                      acc[:, b * 512:(b + 1) * 512],
                                      hhi[:, 2 * b:2 * b + 2, :].rearrange("p c t -> p (c t)").bitcast(F32),
                                      ALU.subtract).then_inc(s("ht_low"), 1)
                own(dve.scalar_tensor_tensor(rt[:, 512:576], rt[:, 448:512], float(CAPACITY), rt[:, 256:320],
                                             ALU.is_ge, ALU.mult))
                dve.wait_ge(s("rank_read"), l + 1)
                own(dve.tensor_scalar(rt[:, 593:594], rt[:, 592:593], float(CAPACITY), None, ALU.is_gt))
                dve.tensor_copy(overflow[0:1, l:l + 1], rt[0:1, 593:594]).then_inc(s("flag_ready"), 1)
                for t in (xghi, xglo):
                    dve.memset(t[:, :].rearrange("p (c s) -> p c s", s=T)[:, :, SLOTS:T - SLOTS].bitcast(F32), 0.0)
                for t in (ahi, alo):
                    ins = dve.memset(t[:, :, SLOTS:T - SLOTS].bitcast(F32), 0.0)
                ins.then_inc(s("slots_clear"), 1)
                dve.wait_ge(s("slots_clear"), l + 1)
                dve.wait_ge(s("flag_ready"), l + 1)
                with dve.If(dve.value_load(overflow[0:1, l:l + 1], min_val=0, max_val=1) > 0):
                    def unit(u, gu, d, i):
                        if u > 0:
                            dve.wait_ge(s(f"spare_free{l}"), along(u, i, 2))
                        for q in range(QT):
                            c = rt[:, 512 + 32 * q + u:513 + 32 * q + u] if i is None else \
                                rt[:, bass.ds(512 + 32 * q + u + 2 * i, 1)]
                            ins = dve.tensor_scalar(var[:, q * P:(q + 1) * P], ident, c, None, ALU.mult)
                        ins.then_inc(s(f"spare_weights{l}"), 1)
                        dve.wait_ge(s(f"spare_silu{l}"), along(u + 1, i, 2))
                        flat = pair_b[:, :, :].rearrange("p f t -> p (f t)")
                        dve.tensor_tensor(flat, work[3][:, :], pair_a[:, :, :].rearrange("p f t -> p (f t)"), ALU.mult
                                          ).then_inc(s(f"spare_act{l}"), 1)
                        dve.wait_ge(s(f"spare_act{l}"), along(2 * u + 1, i, 4))
                        dve.tensor_tensor(pair_b[:], pair_b[:], spread(work[1][:, 0:1], (2, T), (0, 1)), ALU.mult
                                          ).then_inc(s(f"spare_act{l}"), 1)
                    spare_units(dve, unit)
                    dve.wait_ge(s(f"spare_free{l}"), EXPERTS)
                base = PAIRS * l

                def event(what, p, k, i):
                    if what in ("gu", "d"):
                        lo(NUMBER[moe_tile(l, what, p, k)] + AHEAD, i, 12)
                    elif what == "A":
                        dve.wait_ge(s("msilu"), along(base + p + 1, i, 1))
                        dve.tensor_tensor(pair_b[:, 0, :], work[0][:, EH:2 * EH], pair_a[:, 0, :], ALU.mult
                                          ).then_inc(s("mprod"), 1)
                    elif what == "G":
                        dve.wait_ge(s("g_high"), along(2 * (base + p) + k + 1, i, 2))
                        dve.tensor_tensor(own_slots(xglo, 4 * k, 4),
                                          work[1][:, :].rearrange("p (c e s) -> p c e s", c=4, e=2),
                                          own_slots(xghi, 4 * k, 4).bitcast(F32), ALU.subtract).then_inc(s("g_low"), 1)
                    elif what == "Y":
                        w = rt[:, 576 + p:577 + p] if i is None else rt[:, bass.ds(576 + p + i, 1)]
                        for half in range(2):
                            c = slice(half * 512, (half + 1) * 512)
                            dve.wait_ge(s("y_high_moe"), along(2 * (base + p) + half + 1, i, 2))
                            dve.scalar_tensor_tensor(yslo[:, c], work[2 + half][:, :], w, yshi[:, c].bitcast(F32),
                                                     ALU.mult, ALU.subtract).then_inc(s("y_low"), 1)
                    elif what == "T":
                        dve.wait_ge(s("mt_mm"), along(base + p + 1, i, 1))
                        src = work[1][:, 0:T].rearrange("p (f e s) -> p f e s", f=2, e=2)
                        fhi = ahi[:, :, :].rearrange("p f t -> p (f t)")
                        flo = alo[:, :, :].rearrange("p f t -> p (f t)")
                        dve.tensor_copy(own_slots(fhi, 0, 2), src).then_inc(s("mt_high"), 1)
                        dve.wait_ge(s("mt_high"), along(base + p + 1, i, 1))
                        dve.tensor_tensor(own_slots(flo, 0, 2), src, own_slots(fhi, 0, 2).bitcast(F32), ALU.subtract
                                          ).then_inc(s("mt_low"), 1)
                moe_events(dve, event)
                dve.wait_ge(s("moe_done"), l + 1)
                for m in range(DC):
                    ins = dve.scalar_tensor_tensor(xT[:, m, :], acc_c[:, m, :], mod_col(l, 5, m), xT[:, m, :],
                                                   ALU.mult, ALU.add)
                ins.then_inc(s("x_ready"), 1)
            k = 7 + 3 * LAYERS
            variance(k, D)
            root_done(k)
            for m in range(DC):
                ins = dve.scalar_tensor_tensor(hf[:, m, :], xT[:, m, :], col("final", m), rstd[:], ALU.mult, ALU.mult)
            ins.then_inc(s("final_ready"), 1)


def features(v):
    return np.ascontiguousarray(np.reshape(v, (-1, P)).T)


def rel_bucket(dist):
    d = np.maximum(dist, 1).astype(np.float32)
    exact = BUCKETS // 2
    log = exact + (np.log(d / np.float32(exact)) / np.float32(np.log(MAX_DIST / exact))
                   * np.float32(BUCKETS - exact)).astype(np.int32)
    return np.where(dist < exact, dist, np.minimum(log, BUCKETS - 1))


def host_consts():
    out = np.zeros((P, NCONST), np.float32)

    def put(name, a):
        a = np.asarray(a, np.float32)
        out[:a.shape[0], CONST[name][0]:CONST[name][1]] = a
    i, j = np.arange(P)[:, None], np.arange(P)[None, :]
    put("ident", i == j)
    put("ones", np.ones((P, P)))
    put("upper", i <= j)
    put("levels", np.concatenate([(i // (2 << n) == j // (2 << n)) & (i >> n & 1 == 1) & (j >> n & 1 == 0)
                                  for n in range(LEVELS)], axis=1))
    dist = (T - 1) - np.arange(BROW)
    put("onehot", (rel_bucket(np.maximum(dist, 0))[None, :] == np.arange(BUCKETS)[:, None]) & (dist >= 0)[None, :])
    put("maskrow", np.broadcast_to(np.where(dist < 0, NEG, 0.0), (P, BROW)))
    put("has_block", (np.arange(P)[:, None] + P * np.arange(QT)[None, :]) >= CMP_BLOCK - 1)
    put("slots", np.broadcast_to(np.where(np.arange(SLOTS) < CAPACITY, np.arange(SLOTS), -9), (P, SLOTS)))
    put("iota4", np.broadcast_to(np.arange(4) - 4, (P, 4)))
    put("iota8", np.broadcast_to(np.arange(8) - 8, (P, 8)))
    put("inv_count", np.broadcast_to(np.concatenate([1.0 / np.minimum(np.arange(1, 17), w) for w in WINDOWS]), (P, 64)))
    return out


def host_params(a):
    out = np.zeros((P, NPARAM), np.float32)

    def put(name, v):
        lo, hi = PARAM[name]
        v = np.asarray(v).reshape(v.shape[0], -1)
        out[:v.shape[0], lo:hi] = v

    def wide(v):
        return np.broadcast_to(v, (P, v.shape[-1]))
    for name, key in (("ffn1_pre", "ffn1_pre_norm"), ("ffn1_post", "ffn1_post_norm"), ("mix_pre", "mix_pre_norm"),
                      ("mix_post", "mix_post_norm"), ("ffn2_pre", "ffn2_pre_norm"), ("ffn2_post", "ffn2_post_norm"),
                      ("mem_norm", "mem_norm"), ("final", "final_norm_g_2"), ("c", "c_2"), ("dn_norm", "dn_out_norm")):
        put(name, features(a[key]))
    put("dn_conv", a["dn_conv_w"][0].reshape(4, 12, P).transpose(2, 1, 0))
    put("a_log", wide(a["dn_a_log"][0]))
    put("dt_bias", wide(a["dn_dt_bias"][0]))
    w = a["w_in"][0]
    cols = np.concatenate([w[:, 1280:1304], w[:, 2840:2844], w[:, 2844:2848]], axis=1)
    put("w_small", cols.reshape(DC, P, 32).transpose(1, 0, 2))
    put("w2k", a["cmp_k_w2"][0].reshape(2, P, DH).transpose(1, 0, 2))
    put("w2v", a["cmp_v_w2"][0].reshape(2, P, DH).transpose(1, 0, 2))
    for name, key in (("posk", "cmp_pos_k"), ("posv", "cmp_pos_v")):
        put(name, a[key][0].reshape(16, 2 * DH).T)
    put("rel", a["rel_bias"])
    for l in range(LAYERS):
        put(f"norm{l}", features(a["mixer_norm_g_2"][l]))
        put(f"b_ada{l}", features(a["b_ada_2"][l]))
        put(f"conv_w{l}", a["conv_w_2"][l].reshape(CONV_K, 4, P).transpose(2, 1, 0))
        for name, key in (("conv_b", "conv_b_2"), ("ln_g", "conv_ln_g_2"), ("ln_b", "conv_ln_b_2"),
                          ("b_out", "b_conv_out_2"), ("pool_scale", "pool_scale_2"), ("ffn_norm", "ffn_norm_g_2")):
            put(f"{name}{l}", features(a[key][l]))
        r = np.concatenate([a["w_router_group_2"][l], a["w_router_expert_2"][l]], axis=1)
        put(f"router{l}", r.reshape(DC, P, 36).transpose(1, 0, 2))
        put(f"router_b{l}", wide(np.concatenate([a["b_router_group_2"][l], a["b_router_expert_2"][l]])))
    return out


def host_stream(a):
    out = np.empty((len(STREAM), P, TILE), np.float32)

    def cols(w, at, n=P):
        return w[:, at:at + n].reshape(-1, P, n).transpose(1, 0, 2).reshape(P, -1)
    w_in = a["w_in"][0]
    head = np.arange(DH)
    pair = [np.concatenate([j * DH + head, (j + HPG) * DH + head]) for j in range(HPG)]
    kv = HEADS * DH
    dn_at = kv + 6 * P + 24
    z_at = dn_at + 1536 + 8
    nsa_rows = np.concatenate(pair)
    branch = [a["w_branch_nsa"][0][nsa_rows], a["w_branch_dn"][0], a["w_branch_mem"][0]]
    w1 = [a[n][0].reshape(16, P, CMP_HIDDEN) for n in ("cmp_k_w1", "cmp_v_w1")]
    for r, (stage, m, _) in enumerate(STREAM):
        l = int(stage[-1]) if stage[-1] in "01" and stage not in ("ffn1", "w1") else 0
        name = stage.rstrip("01") if stage not in ("ffn1", "w1") else stage
        if name == "moe":
            what, p, k = m
            e = 2 * p + (k // 4 if what == "gu" else k // 2)
            g, u, d = (a[f"w_expert_{n}_2"][l, e] for n in ("gate", "up", "down"))
            if what == "d":
                out[r] = d[(k % 2) * P:(k % 2 + 1) * P]
            else:
                rows = slice((k % 4) * T, (k % 4 + 1) * T)
                out[r] = cols(np.concatenate([g[rows], u[rows]], axis=1), 0, 2 * EH)
        elif name in ("ffn1", "ffn2"):
            what, c = m
            g, u, d = (a[f"{name}_w_{n}"][0] for n in ("gate", "up", "down"))
            tile = {"g": g, "u": u}[what] if what != "d" else d
            out[r] = cols(tile, c * P) if what != "d" else tile[c * P:(c + 1) * P]
        elif name == "memk":
            out[r] = cols(a["w_mem_kv"][0], m * P)
        elif name == "memv":
            out[r] = cols(a["w_mem_kv"][0], 512 + m * P)
        elif name == "dn":
            out[r] = cols(w_in, dn_at + m * P)
        elif name == "z":
            out[r] = cols(w_in, z_at + m * P)
        elif name == "v":
            out[r] = cols(w_in, kv + (3, 5)[m] * P)
        elif name == "q":
            out[r] = cols(w_in[:, pair[m]], 0)
        elif name == "kv":
            out[r] = cols(w_in, kv + (0, 1, 2, 4)[m] * P)
        elif name == "memq":
            out[r] = cols(w_in, z_at + 512 + m * P)
        elif name == "w1":
            out[r] = w1[m // 4][4 * (m % 4):4 * (m % 4) + 4].transpose(1, 0, 2).reshape(P, -1)
        elif name == "ada":
            out[r] = cols(a["w_ada_2"][m // 48], (m % 48) * P)
        elif name == "gate":
            out[r] = cols(a["w_branch_gate"][0], m * P)
        elif name == "branch":
            out[r] = cols(branch[m[1]], m[0] * T, T)
        elif stage == "wout":
            out[r] = cols(a["w_out"][0], m * P)
        elif name == "wout":
            out[r] = cols(a["w_out_2"][l], m * P)
        elif name == "a":
            out[r] = cols(a["w_in_2"][l], (m // 2) * P + 512 * (m % 2))
        elif name == "p":
            out[r] = cols(a["w_in_2"][l], 1024 + m * P)
        elif name == "G":
            out[r] = cols(a["w_in_2"][l], 1536 + m * P)
        elif name == "pool":
            out[r] = a["pool_w_2"][l].transpose(1, 0, 2).reshape(P, -1)
        elif name == "conv":
            out[r] = cols(a["w_conv_out_2"][l], m * T, T)
        else:
            raise ValueError(stage)
    return out


def kernel(**inputs):
    import concourse.bacc as bacc
    from concourse.bass_utils import run_bass_kernel_spmd

    a = {k: np.asarray(v) for k, v in inputs.items()}

    def token_last(v):
        return np.ascontiguousarray(v[0].reshape(T, DC, P).transpose(2, 1, 0))
    arrays = {"wstream_d": host_stream(a), "consts_d": host_consts(), "params_d": host_params(a),
              "x_d": token_last(a["x"]), "mem_d": token_last(a["mem"])}
    nc = bacc.Bacc("TRN2", target_bir_lowering=False, num_devices=1)
    args = [nc.dram_tensor(n, v.shape, F32, kind="ExternalInput").ap() for n, v in arrays.items()]
    rows = nc.dram_tensor("bias_rows_d", (HEADS, P, BROW), F32, kind="Internal").ap()
    out = nc.dram_tensor("out_d", (P, DC, T), F32, kind="ExternalOutput").ap()
    program(nc, *args, rows, out)
    r = run_bass_kernel_spmd(nc, [arrays], core_ids=[0])
    got = r.results[0]["out_d"]
    return np.ascontiguousarray(got.transpose(2, 1, 0)).reshape(1, T, D)
```
